# Optimizing a Trainium2 kernel written in Bass

```python
import functools
import jax
import jax.numpy as jnp
from jax import lax
import numpy as np
import jax, jax.numpy as jnp

D_MODEL = 2048
BATCH = 1
SEQ = 256
DEPTH = 1

CTX_LEN = 256
GRID_W = 64
CHUNK = 128
EPS = 1e-6
ADA_CHUNKS = 6

R_HEADS = 8
R_DK = 64
R_DV = 128
R_QK = R_HEADS * R_DK
R_WIDTH = R_HEADS * R_DV
ROPE_BASE = 10000.0

M_HEADS = 4
M_DK = 128
M_DV = 256
M_QK = M_HEADS * M_DK
M_WIDTH = M_HEADS * M_DV
M_CONV = 3
M_N_GATES = 2 * 2 * M_HEADS

P_HEADS = 8
P_NKEYS = 128
P_EXPERTS = P_NKEYS * P_NKEYS
P_DQ = 256
P_TOPK = 16
P_BLOCK = 128

IN_SPLITS = (R_QK, R_QK, R_WIDTH, R_WIDTH, M_QK, M_QK, M_WIDTH, M_WIDTH, M_N_GATES, D_MODEL, D_MODEL)
IN_COLS = 2 * R_QK + 2 * R_WIDTH + 2 * M_QK + 2 * M_WIDTH + M_N_GATES + 2 * D_MODEL


def _split_in(p):
    out, off = [], 0
    for size in IN_SPLITS:
        out.append(p[..., off:off + size])
        off += size
    return out

def _rmsnorm(x, g):
    xf = x.astype(jnp.float32)
    y = xf * lax.rsqrt(jnp.mean(xf * xf, axis=-1, keepdims=True) + EPS)
    return (y * g.astype(jnp.float32)).astype(x.dtype)

def _modulate(x, g, shift, scale):
    return _rmsnorm(x, g) * (1.0 + scale) + shift

def _head_norm(y):
    yc = y - jnp.mean(y, axis=-1, keepdims=True)
    return yc * lax.rsqrt(jnp.mean(yc * yc, axis=-1, keepdims=True) + EPS)

def _rotary_2d(t, row, col):
    half = t.shape[-1] // 2
    n_ax = half // 2
    freq = ROPE_BASE ** (-jnp.arange(n_ax, dtype=jnp.float32) / n_ax)
    ang = jnp.concatenate([row[:, None] * freq, col[:, None] * freq], axis=-1)
    cos = jnp.cos(ang)[None, :, None, :]
    sin = jnp.sin(ang)[None, :, None, :]
    t1, t2 = t[..., :half], t[..., half:]
    return jnp.concatenate([t1 * cos - t2 * sin, t2 * cos + t1 * sin], axis=-1)

def _to_chunks(t):
    bsz, length = t.shape[:2]
    t = t.reshape((bsz, length // CHUNK, CHUNK) + t.shape[2:])
    return jnp.swapaxes(jnp.moveaxis(t, 1, 0), 2, 3)

def _from_chunks(t):
    t = jnp.moveaxis(jnp.swapaxes(t, 2, 3), 0, 1)
    return t.reshape((t.shape[0], t.shape[1] * t.shape[2]) + t.shape[3:])

def _flip(ts):
    return tuple(jnp.flip(t, axis=1) for t in ts)

def _bidirectional(scan_f, scan_b, lat_f, lat_b, ctx_f, ctx_b, init, need_ctx):
    st_f, yc_f = scan_f(ctx_f, init, need_ctx)
    st_b, yc_b = scan_b(_flip(ctx_b), init, need_ctx)
    _, yl_f = scan_f(lat_f, st_f, True)
    _, yl_b = scan_b(_flip(lat_b), st_b, True)
    y_lat = yl_f + jnp.flip(yl_b, axis=1)
    y_ctx = yc_f + jnp.flip(yc_b, axis=1) if need_ctx else None
    return y_lat, y_ctx

def _retention_scan(seqs, s0, with_out, log_gamma):
    q, k, v = (_to_chunks(t) for t in seqs)
    pos = jnp.arange(CHUNK, dtype=jnp.float32)
    lg = log_gamma[:, None]
    rel = pos[:, None] - pos[None, :]
    intra = jnp.where(rel >= 0, jnp.exp(lg[:, :, None] * jnp.maximum(rel, 0.0)), 0.0)
    q_dec = jnp.exp(lg * (pos + 1.0))[None, :, :, None]
    k_dec = jnp.exp(lg * (CHUNK - 1.0 - pos))[None, :, :, None]
    c_dec = jnp.exp(lg * CHUNK)[None, :, :, None]

    def step(s, inp):
        qc, kc, vc = inp
        s_new = c_dec * s + jnp.einsum('bhcd,bhce->bhde', kc * k_dec, vc)
        if not with_out:
            return s_new, None
        att = jnp.einsum('bhcd,bhsd->bhcs', qc, kc) * intra
        y = jnp.einsum('bhcs,bhse->bhce', att, vc) + jnp.einsum('bhcd,bhde->bhce', qc * q_dec, s)
        return s_new, y

    s_fin, ys = lax.scan(step, s0, (q, k, v))
    return s_fin, (_from_chunks(ys) if with_out else None)

def _mlstm_scan(seqs, state0, with_out):
    q, k, v, ig, lf = (_to_chunks(t) for t in seqs)
    tri = jnp.tril(jnp.ones((CHUNK, CHUNK), dtype=bool))

    def step(carry, inp):
        c_prev, n_prev, m_prev = carry
        qc, kc, vc, ic, fc = inp
        b = jnp.cumsum(fc, axis=-1)
        b_end = b[..., -1]
        w_log = b_end[..., None] - b + ic
        a_end = b_end + m_prev
        m_new = jnp.maximum(a_end, jnp.max(w_log, axis=-1))
        p = jnp.exp(a_end - m_new)
        kw = kc * jnp.exp(w_log - m_new[..., None])[..., None]
        c_new = p[..., None, None] * c_prev + jnp.einsum('bhcd,bhce->bhde', kw, vc)
        n_new = p[..., None] * n_prev + jnp.sum(kw, axis=2)
        new = (c_new, n_new, m_new)
        if not with_out:
            return new, None
        a = b + m_prev[..., None]
        d_log = jnp.where(tri, b[..., :, None] - b[..., None, :] + ic[..., None, :], -jnp.inf)
        m_t = jnp.maximum(a, jnp.max(d_log, axis=-1))
        att = jnp.einsum('bhcd,bhsd->bhcs', qc, kc) * jnp.exp(d_log - m_t[..., None])
        inter = jnp.exp(a - m_t)[..., None]
        num = jnp.einsum('bhcs,bhse->bhce', att, vc) + inter * jnp.einsum('bhcd,bhde->bhce', qc, c_prev)
        den = jnp.sum(att, axis=-1, keepdims=True) + inter * jnp.einsum('bhcd,bhd->bhc', qc, n_prev)[..., None]
        h = num / jnp.maximum(jnp.abs(den), jnp.exp(-m_t)[..., None])
        return new, h

    st, hs = lax.scan(step, state0, (q, k, v, ig, lf))
    return st, (_from_chunks(hs) if with_out else None)

def _retention_inputs(q, k, v, row, col):
    bsz, length = q.shape[:2]
    qh = q.reshape(bsz, length, R_HEADS, R_DK).astype(jnp.float32)
    kh = k.reshape(bsz, length, R_HEADS, R_DK).astype(jnp.float32)
    if row is not None:
        qh = _rotary_2d(qh, row, col)
        kh = _rotary_2d(kh, row, col)
    vh = v.reshape(bsz, length, R_HEADS, R_DV).astype(jnp.float32)
    return (qh, kh * (R_DK ** -0.5), vh)

def _dwconv_centred(x, w):
    ksz, ch = w.shape
    return lax.conv_general_dilated(x, w[:, None, :].astype(x.dtype), window_strides=(1,),
                                    padding=[(ksz // 2, ksz - 1 - ksz // 2)],
                                    dimension_numbers=('NWC', 'WIO', 'NWC'), feature_group_count=ch)

def _mlstm_inputs(q, k, v, gates, conv_w, gate_bias):
    bsz, length = q.shape[:2]
    qk = jax.nn.silu(_dwconv_centred(jnp.concatenate([q, k], axis=-1), conv_w))
    qh = qk[..., :M_QK].reshape(bsz, length, M_HEADS, M_DK).astype(jnp.float32)
    kh = qk[..., M_QK:].reshape(bsz, length, M_HEADS, M_DK).astype(jnp.float32) * (M_DK ** -0.5)
    vh = v.reshape(bsz, length, M_HEADS, M_DV).astype(jnp.float32)
    g = gates.astype(jnp.float32).reshape(bsz, length, 2, 2, M_HEADS) + gate_bias.astype(jnp.float32)
    fwd = (qh, kh, vh, g[:, :, 0, 0], jax.nn.log_sigmoid(g[:, :, 0, 1]))
    bwd = (qh, kh, vh, g[:, :, 1, 0], jax.nn.log_sigmoid(g[:, :, 1, 1]))
    return fwd, bwd

def _retention_out(y, gate):
    bsz, length = y.shape[:2]
    return _head_norm(y).reshape(bsz, length, R_WIDTH).astype(gate.dtype) * jax.nn.silu(gate)

def _mlstm_out(h, o):
    bsz, length = h.shape[:2]
    return _head_norm(h).reshape(bsz, length, M_WIDTH).astype(o.dtype) * jax.nn.sigmoid(o)

def _merge(yr, ym, g_r, g_m, w_ret_out, w_mlstm_out, w_out):
    merged = jax.nn.sigmoid(g_r) * (yr @ w_ret_out) + jax.nn.sigmoid(g_m) * (ym @ w_mlstm_out)
    return merged @ w_out

def _peer(h, w_query, sub_keys, expert_down, expert_up):
    bsz, length, dm = h.shape
    tokens = h.reshape(-1, P_BLOCK, dm)

    def block(tb):
        qh = (tb @ w_query).reshape(P_BLOCK, P_HEADS, 2, P_DQ // 2)
        s = jnp.einsum('thpd,hpkd->thpk', qh, sub_keys).astype(jnp.float32)
        sv, si = lax.top_k(s, P_TOPK)
        cand_s = (sv[:, :, 0, :, None] + sv[:, :, 1, None, :]).reshape(P_BLOCK, P_HEADS, P_TOPK * P_TOPK)
        cand_i = (si[:, :, 0, :, None] * P_NKEYS + si[:, :, 1, None, :]).reshape(P_BLOCK, P_HEADS, P_TOPK * P_TOPK)
        best_s, best_j = lax.top_k(cand_s, P_TOPK)
        eid = jnp.take_along_axis(cand_i, best_j, axis=-1)
        g = jax.nn.softmax(best_s, axis=-1)
        act = jax.nn.gelu(jnp.einsum('thkd,td->thk', expert_down[eid], tb).astype(jnp.float32), approximate=False)
        return jnp.einsum('thk,thkd->td', (g * act).astype(tb.dtype), expert_up[eid])

    return lax.map(block, tokens).reshape(bsz, length, dm)

def _layer(x, ctx, c, c_ctx, row, col, w_ada, b_ada, norm1_g, w_in, ret_decay, m_conv, m_gate_bias,
           w_ret_out, w_mlstm_out, w_out, norm2_g, peer_query, peer_keys, peer_down, peer_up, update_ctx):
    f32 = jnp.float32
    bsz = x.shape[0]
    sh1, sc1, gt1, sh2, sc2, gt2 = jnp.split((jax.nn.silu(c) @ w_ada + b_ada)[:, None, :], ADA_CHUNKS, axis=-1)
    csh1, csc1, cgt1, csh2, csc2, cgt2 = jnp.split(jax.nn.silu(c_ctx) @ w_ada + b_ada, ADA_CHUNKS, axis=-1)
    rq, rk, rv, rg, mq, mk, mv, mo, mg, gr, gm = _split_in(_modulate(x, norm1_g, sh1, sc1) @ w_in)
    crq, crk, crv, crg, cmq, cmk, cmv, cmo, cmg, cgr, cgm = _split_in(_modulate(ctx, norm1_g, csh1, csc1) @ w_in)

    log_gamma = jax.nn.log_sigmoid(ret_decay.astype(f32))
    r_lat = _retention_inputs(rq, rk, rv, row, col)
    r_ctx = _retention_inputs(crq, crk, crv, None, None)
    s0 = jnp.zeros((bsz, R_HEADS, R_DK, R_DV), f32)
    yr, yr_c = _bidirectional(functools.partial(_retention_scan, log_gamma=log_gamma[0]),
                              functools.partial(_retention_scan, log_gamma=log_gamma[1]),
                              r_lat, r_lat, r_ctx, r_ctx, s0, update_ctx)

    m_lat_f, m_lat_b = _mlstm_inputs(mq, mk, mv, mg, m_conv, m_gate_bias)
    m_ctx_f, m_ctx_b = _mlstm_inputs(cmq, cmk, cmv, cmg, m_conv, m_gate_bias)
    m0 = (jnp.zeros((bsz, M_HEADS, M_DK, M_DV), f32), jnp.zeros((bsz, M_HEADS, M_DK), f32),
          jnp.zeros((bsz, M_HEADS), f32))
    ym, ym_c = _bidirectional(_mlstm_scan, _mlstm_scan, m_lat_f, m_lat_b, m_ctx_f, m_ctx_b, m0, update_ctx)

    x = x + gt1 * _merge(_retention_out(yr, rg), _mlstm_out(ym, mo), gr, gm, w_ret_out, w_mlstm_out, w_out)
    x = x + gt2 * _peer(_modulate(x, norm2_g, sh2, sc2), peer_query, peer_keys, peer_down, peer_up)
    if update_ctx:
        ctx = ctx + cgt1 * _merge(_retention_out(yr_c, crg), _mlstm_out(ym_c, cmo), cgr, cgm,
                                  w_ret_out, w_mlstm_out, w_out)
        ctx = ctx + cgt2 * _peer(_modulate(ctx, norm2_g, csh2, csc2), peer_query, peer_keys, peer_down, peer_up)
    return x, ctx

def first_inputs(seed: int = 0) -> dict:
    key = jax.random.key(seed)
    ks = jax.random.split(key, 24)
    f32 = jnp.float32

    def nrm(k, shape, scale):
        return jax.random.normal(k, shape, f32) * scale

    x = nrm(ks[0], (BATCH, SEQ, D_MODEL), 1.0)
    c = nrm(ks[1], (BATCH, D_MODEL), 1.0)
    ctx = nrm(ks[2], (BATCH, CTX_LEN, D_MODEL), 1.0)
    c_ctx = nrm(ks[3], (D_MODEL,), 1.0)
    w_ada = nrm(ks[4], (DEPTH, D_MODEL, ADA_CHUNKS * D_MODEL), D_MODEL ** -0.5)
    b_ada = nrm(ks[5], (DEPTH, ADA_CHUNKS * D_MODEL), 0.02)
    norm1_g = 1.0 + nrm(ks[6], (DEPTH, D_MODEL), 0.02)
    w_in = nrm(ks[7], (DEPTH, D_MODEL, IN_COLS), D_MODEL ** -0.5)
    decay_logit = jnp.log(2.0 ** (5.0 + jnp.arange(R_HEADS, dtype=f32)) - 1.0)
    ret_decay = decay_logit[None, None, :] + nrm(ks[8], (DEPTH, 2, R_HEADS), 0.05)
    m_conv = nrm(ks[9], (DEPTH, M_CONV, 2 * M_QK), M_CONV ** -0.5)
    gate_base = jnp.stack([jnp.zeros((M_HEADS,), f32), jnp.linspace(3.0, 6.0, M_HEADS, dtype=f32)])
    m_gate_bias = gate_base[None, None] + nrm(ks[10], (DEPTH, 2, 2, M_HEADS), 0.1)
    w_ret_out = nrm(ks[11], (DEPTH, R_WIDTH, D_MODEL), R_WIDTH ** -0.5)
    w_mlstm_out = nrm(ks[12], (DEPTH, M_WIDTH, D_MODEL), M_WIDTH ** -0.5)
    w_out = nrm(ks[13], (DEPTH, D_MODEL, D_MODEL), D_MODEL ** -0.5)
    norm2_g = 1.0 + nrm(ks[14], (DEPTH, D_MODEL), 0.02)
    peer_query = nrm(ks[15], (DEPTH, D_MODEL, P_HEADS * P_DQ), D_MODEL ** -0.5)
    peer_keys = nrm(ks[16], (DEPTH, P_HEADS, 2, P_NKEYS, P_DQ // 2), (P_DQ // 2) ** -0.5)
    peer_down = nrm(ks[17], (DEPTH, P_EXPERTS, D_MODEL), D_MODEL ** -0.5)
    peer_up = nrm(ks[18], (DEPTH, P_EXPERTS, D_MODEL), P_HEADS ** -0.5)
    final_g = 1.0 + nrm(ks[19], (D_MODEL,), 0.02)
    return {'x': x, 'c': c, 'ctx': ctx, 'c_ctx': c_ctx, 'w_ada': w_ada, 'b_ada': b_ada,
            'norm1_g': norm1_g, 'w_in': w_in, 'ret_decay': ret_decay, 'm_conv': m_conv,
            'm_gate_bias': m_gate_bias, 'w_ret_out': w_ret_out, 'w_mlstm_out': w_mlstm_out,
            'w_out': w_out, 'norm2_g': norm2_g, 'peer_query': peer_query, 'peer_keys': peer_keys,
            'peer_down': peer_down, 'peer_up': peer_up, 'final_g': final_g}

def first_block(x, c, ctx, c_ctx, w_ada, b_ada, norm1_g, w_in, ret_decay, m_conv, m_gate_bias,
              w_ret_out, w_mlstm_out, w_out, norm2_g, peer_query, peer_keys, peer_down, peer_up, final_g):
    length = x.shape[1]
    ROWS = length // GRID_W
    row = jnp.repeat(jnp.arange(ROWS, dtype=jnp.float32), GRID_W)
    col = jnp.tile(jnp.arange(GRID_W, dtype=jnp.float32), ROWS)
    for layer in range(DEPTH):
        x, ctx = _layer(x, ctx, c, c_ctx, row, col, w_ada[layer], b_ada[layer], norm1_g[layer], w_in[layer],
                        ret_decay[layer], m_conv[layer], m_gate_bias[layer], w_ret_out[layer],
                        w_mlstm_out[layer], w_out[layer], norm2_g[layer], peer_query[layer],
                        peer_keys[layer], peer_down[layer], peer_up[layer], update_ctx=layer < DEPTH - 1)
    return _rmsnorm(x, final_g)


N_MEM = 256
NEG = -1e30
POOL_WINDOWS = (2, 4, 8, 16)
POOL_GROUPS = 4
POOL_GW = D_MODEL // 8
POOL_W = POOL_GROUPS * POOL_GW
SWA_CONFIGS = ((128, 1), (512, 4), (2048, 16))
SWA_GROUPS = 3
SWA_HPG = 4
SWA_HEADS = SWA_GROUPS * SWA_HPG
HEAD_DIM = 128
SWA_QKV = SWA_HEADS * HEAD_DIM
SWA_OUT = SWA_HPG * HEAD_DIM
BLK = 128
GLA_HEADS = 4
GLA_DK = D_MODEL // 16
GLA_DV = D_MODEL // 8
GLA_K = GLA_HEADS * GLA_DK
GLA_V = GLA_HEADS * GLA_DV
GLA_RANK = 16
GLA_TAU = 16.0
GLA_CHUNK = 64
MEM_HEADS = 4
MEM_W = MEM_HEADS * HEAD_DIM
N_BRANCH = 4
IN_SPLITS_2 = (POOL_W, POOL_W,
             SWA_QKV, SWA_QKV, SWA_QKV, SWA_OUT,
             GLA_K, GLA_K, GLA_V, GLA_V, GLA_RANK,
             MEM_W, MEM_W,
             N_BRANCH * D_MODEL)
D_IN = sum(IN_SPLITS_2)


def rms_norm(x, g):
    xf = x.astype(jnp.float32)
    y = xf * lax.rsqrt(jnp.mean(xf * xf, axis=-1, keepdims=True) + EPS)
    return (y * g.astype(jnp.float32)).astype(x.dtype)

def pool_mixer(u, gate, w_pool, scale):
    B, S, _ = u.shape
    ug = u.reshape(B, S, POOL_GROUPS, POOL_GW).astype(jnp.float32)
    cs = jnp.cumsum(ug, axis=1)
    cs0 = jnp.pad(cs, ((0, 0), (1, 0), (0, 0), (0, 0)))
    pos = jnp.arange(S)
    outs = []
    for g, w in enumerate(POOL_WINDOWS):
        hi = cs[:, :, g]
        lo = jnp.pad(cs0[:, :S - w + 1, g], ((0, 0), (w - 1, 0), (0, 0)))
        cnt = jnp.minimum(pos + 1, w).astype(jnp.float32)[None, :, None]
        outs.append((hi - lo) / cnt - ug[:, :, g])
    pooled = jnp.stack(outs, axis=2).astype(u.dtype)
    mixed = jnp.einsum('bsgc,gcd->bsgd', pooled, w_pool).reshape(B, S, POOL_W) * scale
    return mixed * jax.nn.silu(gate)

def dilated_window_attn(q, k, v, window, dilation, slopes):
    B, S, H, Dh = q.shape
    nk = window // dilation
    L = -(-S // (dilation * BLK)) * BLK
    pad = L * dilation - S
    nb = L // BLK

    def to_blocks(t):
        t = jnp.pad(t, ((0, 0), (0, pad), (0, 0), (0, 0)))
        t = t.reshape(B, L, dilation, H, Dh).transpose(0, 2, 1, 3, 4)
        return t.reshape(B, dilation, nb, BLK, H, Dh)

    def band(t):
        prev = jnp.pad(t[:, :, :-1], ((0, 0), (0, 0), (1, 0), (0, 0), (0, 0), (0, 0)))
        return jnp.concatenate([prev, t], axis=3)

    qb = to_blocks(q)
    kk = band(to_blocks(k))
    vv = band(to_blocks(v))
    s = jnp.einsum('brnqhd,brnkhd->brnhqk', qb, kk).astype(jnp.float32) * (Dh ** -0.5)
    qi = jnp.arange(BLK)[:, None]
    kj = jnp.arange(2 * BLK)[None, :] - BLK
    delta = qi - kj
    first = (jnp.arange(nb) == 0)[:, None, None]
    valid = (delta >= 0) & (delta <= nk) & ~(first & (kj < 0))
    bias = -slopes[:, None, None] * (delta * dilation).astype(jnp.float32)
    s = jnp.where(valid[None, None, :, None], s + bias[None, None, None], NEG)
    m = jnp.max(s, axis=-1, keepdims=True)
    e = jnp.exp(s - m)
    den = jnp.sum(e, axis=-1, keepdims=True)
    o = jnp.einsum('brnhqk,brnkhd->brnqhd', (e / den).astype(v.dtype), vv)
    lse = (m + jnp.log(den))[..., 0]
    o = o.reshape(B, dilation, L, H, Dh).transpose(0, 2, 1, 3, 4).reshape(B, L * dilation, H, Dh)[:, :S]
    lse = lse.transpose(0, 1, 2, 4, 3).reshape(B, dilation, L, H).transpose(0, 2, 1, 3)
    lse = lse.reshape(B, L * dilation, H)[:, :S]
    return o, lse

def swa_mixer(q, k, v, gate):
    B, S, _ = q.shape
    slopes = jnp.exp2(-8.0 * (jnp.arange(SWA_HEADS, dtype=jnp.float32) + 1.0) / SWA_HEADS)
    qg = q.reshape(B, S, SWA_GROUPS, SWA_HPG, HEAD_DIM)
    kg = k.reshape(B, S, SWA_GROUPS, SWA_HPG, HEAD_DIM)
    vg = v.reshape(B, S, SWA_GROUPS, SWA_HPG, HEAD_DIM)
    outs, lses = [], []
    for g, (w, d) in enumerate(SWA_CONFIGS):
        o_g, l_g = dilated_window_attn(qg[:, :, g], kg[:, :, g], vg[:, :, g], w, d,
                                       slopes[g * SWA_HPG:(g + 1) * SWA_HPG])
        outs.append(o_g)
        lses.append(l_g)
    o = jnp.stack(outs, axis=2)
    wts = jax.nn.softmax(jnp.stack(lses, axis=2), axis=2)
    o = jnp.sum(wts[..., None].astype(o.dtype) * o, axis=2).reshape(B, S, SWA_OUT)
    return o * jax.nn.silu(gate)

def gla_mixer(q, k, v, lr, gate, w_alpha, b_alpha, g_gla):
    B, S, _ = q.shape
    C = GLA_CHUNK
    nc = S // C
    f32 = jnp.float32
    z = (lr @ w_alpha + b_alpha).astype(f32)
    log_a = jax.nn.log_sigmoid(z) / GLA_TAU
    qc = q.astype(f32).reshape(B, nc, C, GLA_HEADS, GLA_DK) * (GLA_DK ** -0.5)
    kc = k.astype(f32).reshape(B, nc, C, GLA_HEADS, GLA_DK)
    vc = v.astype(f32).reshape(B, nc, C, GLA_HEADS, GLA_DV)
    bc = jnp.cumsum(log_a.reshape(B, nc, C, GLA_HEADS, GLA_DK), axis=2)
    b_last = bc[:, :, -1]
    q_t = qc * jnp.exp(bc)
    k_t = kc * jnp.exp(-bc)
    causal = jnp.tril(jnp.ones((C, C), dtype=bool))
    a = jnp.where(causal, jnp.einsum('bcihk,bcjhk->bchij', q_t, k_t), 0.0)
    o_intra = jnp.einsum('bchij,bcjhv->bcihv', a, vc)
    kv = jnp.einsum('bcjhk,bcjhv->bchkv', kc * jnp.exp(b_last[:, :, None] - bc), vc)
    decay = jnp.exp(b_last)

    def step(state, inp):
        dec, kv_c = inp
        return dec[..., None] * state + kv_c, state

    _, s_prev = lax.scan(step, jnp.zeros((B, GLA_HEADS, GLA_DK, GLA_DV), f32),
                         (decay.transpose(1, 0, 2, 3), kv.transpose(1, 0, 2, 3, 4)))
    s_prev = s_prev.transpose(1, 0, 2, 3, 4)
    o = o_intra + jnp.einsum('bcihk,bchkv->bcihv', q_t, s_prev)
    o = o.reshape(B, S, GLA_HEADS, GLA_DV)
    o = o * lax.rsqrt(jnp.mean(o * o, axis=-1, keepdims=True) + EPS)
    o = o.reshape(B, S, GLA_V) * g_gla.astype(f32)
    return o.astype(q.dtype) * jax.nn.silu(gate)

def mem_attn(q, gate, mem, g_mem, w_mem_kv):
    B, S, _ = q.shape
    kv = rms_norm(mem, g_mem) @ w_mem_kv
    km, vm = jnp.split(kv, 2, axis=-1)
    km = km.reshape(B, N_MEM, MEM_HEADS, HEAD_DIM)
    vm = vm.reshape(B, N_MEM, MEM_HEADS, HEAD_DIM)
    qh = q.reshape(B, S, MEM_HEADS, HEAD_DIM)
    s = jnp.einsum('bshd,bmhd->bhsm', qh, km).astype(jnp.float32) * (HEAD_DIM ** -0.5)
    p = jax.nn.softmax(s, axis=-1)
    o = jnp.einsum('bhsm,bmhd->bshd', p.astype(vm.dtype), vm).reshape(B, S, MEM_W)
    return o * jax.nn.silu(gate)

def second_inputs(seed: int = 0) -> dict:
    key = jax.random.key(seed)
    ks = jax.random.split(key, 20)
    f32 = jnp.float32
    nrm = lambda k, shape, scale: (jax.random.normal(k, shape, f32) * scale)
    return {
        'x': nrm(ks[0], (BATCH, SEQ, D_MODEL), 1.0),
        'mem': nrm(ks[1], (BATCH, N_MEM, D_MODEL), 1.0),
        'g_pre': 1.0 + nrm(ks[2], (DEPTH, D_MODEL), 0.05),
        'g_post': 1.0 + nrm(ks[3], (DEPTH, D_MODEL), 0.05),
        'g_mem': 1.0 + nrm(ks[4], (DEPTH, D_MODEL), 0.05),
        'w_in': nrm(ks[5], (DEPTH, D_MODEL, D_IN), D_MODEL ** -0.5),
        'b_merge': nrm(ks[6], (DEPTH, N_BRANCH, D_MODEL), 0.1),
        'w_pool': nrm(ks[7], (DEPTH, POOL_GROUPS, POOL_GW, POOL_GW), POOL_GW ** -0.5),
        'pool_scale': 1.0 + nrm(ks[8], (DEPTH, POOL_W), 0.05),
        'w_alpha': nrm(ks[9], (DEPTH, GLA_RANK, GLA_K), GLA_RANK ** -0.5),
        'b_alpha': nrm(ks[10], (DEPTH, GLA_K), 0.1),
        'g_gla': 1.0 + nrm(ks[11], (DEPTH, GLA_V), 0.05),
        'w_mem_kv': nrm(ks[12], (DEPTH, D_MODEL, 2 * MEM_W), D_MODEL ** -0.5),
        'w_br_pool': nrm(ks[13], (DEPTH, POOL_W, D_MODEL), POOL_W ** -0.5),
        'w_br_swa': nrm(ks[14], (DEPTH, SWA_OUT, D_MODEL), SWA_OUT ** -0.5),
        'w_br_gla': nrm(ks[15], (DEPTH, GLA_V, D_MODEL), GLA_V ** -0.5),
        'w_br_mem': nrm(ks[16], (DEPTH, MEM_W, D_MODEL), MEM_W ** -0.5),
        'w_out': nrm(ks[17], (DEPTH, D_MODEL, D_MODEL), D_MODEL ** -0.5),
    }

def second_block(x, mem, g_pre, g_post, g_mem, w_in, b_merge, w_pool, pool_scale, w_alpha, b_alpha,
              g_gla, w_mem_kv, w_br_pool, w_br_swa, w_br_gla, w_br_mem, w_out):
    B, S, _ = x.shape
    split_at = np.cumsum(IN_SPLITS_2)[:-1]
    for l in range(DEPTH):
        h = rms_norm(x, g_pre[l])
        proj = h @ w_in[l]
        (a_val, a_gate, sq, sk, sv, s_gate, cq, ck, cv, c_gate, c_lr,
         mq, m_gate, g_logits) = jnp.split(proj, split_at, axis=-1)
        y_a = pool_mixer(a_val, a_gate, w_pool[l], pool_scale[l])
        y_b = swa_mixer(sq, sk, sv, s_gate)
        y_c = gla_mixer(cq, ck, cv, c_lr, c_gate, w_alpha[l], b_alpha[l], g_gla[l])
        y_m = mem_attn(mq, m_gate, mem, g_mem[l], w_mem_kv[l])
        gates = jax.nn.sigmoid(g_logits.reshape(B, S, N_BRANCH, D_MODEL) + b_merge[l])
        merged = (gates[:, :, 0] * (y_a @ w_br_pool[l]) + gates[:, :, 1] * (y_b @ w_br_swa[l])
                  + gates[:, :, 2] * (y_c @ w_br_gla[l]) + gates[:, :, 3] * (y_m @ w_br_mem[l]))
        x = x + rms_norm(merged @ w_out[l], g_post[l])
    return x


def setup_inputs(seed=0):
    out = dict(first_inputs(seed))
    for name, value in second_inputs(seed + 1).items():
        if name != "x":
            out[name + "_2"] = value
    return out


def reference(
    x, c, ctx, c_ctx, w_ada, b_ada, norm1_g, w_in, ret_decay, m_conv, m_gate_bias, w_ret_out,
    w_mlstm_out, w_out, norm2_g, peer_query, peer_keys, peer_down, peer_up, final_g, mem_2,
    g_pre_2, g_post_2, g_mem_2, w_in_2, b_merge_2, w_pool_2, pool_scale_2, w_alpha_2, b_alpha_2,
    g_gla_2, w_mem_kv_2, w_br_pool_2, w_br_swa_2, w_br_gla_2, w_br_mem_2, w_out_2,
):
    x = first_block(
        x, c, ctx, c_ctx, w_ada, b_ada, norm1_g, w_in, ret_decay, m_conv, m_gate_bias,
        w_ret_out, w_mlstm_out, w_out, norm2_g, peer_query, peer_keys, peer_down, peer_up,
        final_g,
    )
    return second_block(
        x, mem_2, g_pre_2, g_post_2, g_mem_2, w_in_2, b_merge_2, w_pool_2, pool_scale_2,
        w_alpha_2, b_alpha_2, g_gla_2, w_mem_kv_2, w_br_pool_2, w_br_swa_2, w_br_gla_2,
        w_br_mem_2, w_out_2,
    )


_drawn_inputs = setup_inputs


def setup_inputs(seed=0):
    import zlib

    import numpy as np

    out = dict(_drawn_inputs(seed))
    spreads = {}
    factors = {}
    for name, (base, spread) in spreads.items():
        noise = np.random.default_rng([zlib.crc32(name.encode()), seed]).standard_normal(out[name].shape)
        drawn = base * np.exp(spread * noise) if base else spread * noise
        out[name] = jnp.asarray(drawn.astype(out[name].dtype))
    for name, factor in factors.items():
        out[name] = (out[name] * factor).astype(out[name].dtype)
    return out
```

```python
from contextlib import ExitStack

import numpy as np

import concourse.bass as bass
from concourse import mybir

F32 = mybir.dt.float32
F32R = mybir.dt.float32r
U32 = mybir.dt.uint32
ALU = mybir.AluOpType
ACT = mybir.ActivationFunctionType
AX = mybir.AxisListType.X
ds = bass.ds

P = 128
T = 256
TB = T // P
D = 2048
KB = D // P
CG = 512
EPS = 1e-6
SLOTS = 4
TILE_K = 4

R_HEADS, R_DK, R_DV = 8, 64, 128
M_HEADS, M_DK, M_DV = 4, 128, 256
RQ, RK, RV, RG, MQ, MK, MV, MO, MG = 0, 512, 1024, 2048, 3072, 3584, 4096, 5120, 6144
GR, GM = 6160, 8208
N_GATES = 16
PEER_H, PEER_K, PEER_TOP = 8, 128, 16
HP = 2 * PEER_H
PICKS = PEER_H * PEER_TOP
A_VAL, A_GATE, SQ, SK, SV, S_GATE = 0, 1024, 2048, 3584, 5120, 6656
CQ, CK, CV, C_GATE, C_LR, MEMQ, MEM_GATE, G_LOGIT = 7168, 7680, 8192, 9216, 10240, 10256, 10768, 11280
P2_COLS = 11280
SWA_CFG = ((128, 1), (512, 4), (2048, 16))
POOL_WINDOWS = (2, 4, 8, 16)
N_BRANCH = 4
MEM_W = 512
BIG = 1e33


class Steps:

    def __init__(self, eng, sem):
        self.eng, self.sem, self.n, self.moved = eng, sem, 0, 0

    def __call__(self, ins):
        ins.then_inc(self.sem, 1)
        self.n += 1
        self.eng.wait_ge(self.sem, self.n + self.moved)

    def enter(self, i, per):
        self.first, self.per, self.moved = self.n, per, i * per

    def leave(self, count):
        assert self.n - self.first == self.per, (self.n - self.first, self.per)
        self.n, self.moved = self.first + self.per * count, 0


def phase_semaphores(nc, ctx):
    held = []
    ctx.callback(nc.all_engine_barrier)
    ctx.callback(lambda: nc.clear_and_free_semaphores(held))

    def sem(name):
        held.append(nc.alloc_semaphore(name=name))
        return held[-1]

    return sem


def shape_constants():
    f = np.float32
    t = np.arange(T)
    p = np.arange(P)

    def split(a):
        return np.ascontiguousarray(a.reshape(TB, P, -1).transpose(1, 0, 2), dtype=f)

    n_ax = R_DK // 4
    freq = 10000.0 ** (-np.arange(n_ax, dtype=np.float64) / n_ax)
    freq = freq.astype(f)
    ang = np.concatenate([(t // 64).astype(f)[:, None] * freq, (t % 64).astype(f)[:, None] * freq], axis=1)
    rope = np.stack([np.cos(ang), np.sin(ang)], axis=1).reshape(T, -1)
    s_, t_ = t[:, None], t[None, :]
    rel = np.concatenate([np.maximum(t_ - s_, 0), np.maximum(s_ - t_, 0), t_ == s_], axis=1)
    pos = np.stack([T - 1 - t, t, t + 1, T - t], axis=1)
    causal = np.concatenate([t_ >= s_, t_ <= s_], axis=1)
    ltri = np.stack([p[:, None] <= p[None, :], p[:, None] >= p[None, :], np.ones((P, P))], axis=1)
    pool = []
    for w in POOL_WINDOWS:
        inside = (s_ <= t_) & (s_ > t_ - w)
        pool.append(inside / np.minimum(t_ + 1, w).astype(f) - (s_ == t_))
    pool = np.concatenate(pool, axis=1)
    dist = []
    for w, d in SWA_CFG:
        gap = t[:, None] - t[None, :]
        ok = (gap >= 0) & (gap % d == 0) & (gap <= w)
        dist.append(np.where(ok, gap, BIG))
    dist = np.concatenate(dist, axis=1)
    same = (p[:, None] // 64 == p[None, :] // 64) & (p[None, :] >= p[:, None])
    top = np.finfo(f).max
    chunk = np.stack([np.where(same, top, 0.0), np.where(same, -top, 0.0)], axis=1)
    seg = np.tile((np.arange(4 * T) % 64 != 0).astype(f), (P, 1))
    pick = np.zeros((8, 8, P))
    for r in range(8):
        pick[r, r] = 1.0
    iota16 = np.tile(np.arange(16), (P, 1))
    return {
        "k_ident": np.eye(P, dtype=f), "k_rope": split(rope), "k_rel": split(rel), "k_pos": split(pos),
        "k_causal": split(causal), "k_ltri": np.ascontiguousarray(ltri, f), "k_pool": split(pool),
        "k_dist": split(dist), "k_chunk": np.ascontiguousarray(chunk, f), "k_seg": seg,
        "k_pick": np.ascontiguousarray(pick, f), "k_iota16": iota16.astype(f),
    }


def rows_of(ap):
    return ap.rearrange("(r c) -> r c", c=P)


def tokens_of(ap):
    return ap.rearrange("(b p) d -> p b d", p=P)


def k_tile(w, s, cols):
    return w[s * TILE_K * P:(s + 1) * TILE_K * P, cols].rearrange("(k p) n -> p k n", p=P)


class WeightRing:

    def __init__(self, nc, ctx):
        self.tile = ctx.enter_context(nc.sbuf_tensor("weight_ring", [P, SLOTS, TILE_K, CG], F32))
        self.landed = [ctx.enter_context(nc.semaphore(f"weight_landed{s}")) for s in range(SLOTS)]
        self.used = ctx.enter_context(nc.semaphore("weight_used"))
        self.granted = ctx.enter_context(nc.semaphore("weight_slot_granted"))
        self.turn = 0

    def load(self, sp, s, src, turn):
        if not (isinstance(turn, int) and turn == 0):
            sp.wait_ge(self.used, (turn - 1) * SLOTS + (s + 1))
            sp.sem_inc(self.granted, 1)
        sp.dma_start(self.tile[:, s], src).then_inc(self.landed[s], 16)

    def load_turn(self, sp, sources, turn):
        for s in range(SLOTS):
            self.load(sp, s, sources[s], turn)

    def arrived(self, pe, s, turn):
        pe.wait_ge(self.landed[s], (turn + 1) * 16)


def turn_of(w, cols):
    return [k_tile(w, s, cols) for s in range(SLOTS)]


def gemm_token_major(pe, ring, pieces, lhs, outs, before, tb_done):
    n = len(pieces) * TILE_K
    last_tb = len(outs) - 1
    for tb, out in enumerate(outs):
        before(tb)
        for i, (slot, turn) in enumerate(pieces):
            if tb == 0:
                ring.arrived(pe, slot, turn)
            for kk in range(TILE_K):
                k = i * TILE_K + kk
                mm = pe.matmul(out, lhs(k, tb), ring.tile[:, slot, kk, :], start=(k == 0), stop=(k == n - 1))
            if tb == last_tb:
                mm.then_inc(ring.used, 1)
        if tb != last_tb:
            mm.then_inc(tb_done, 1)


def phase_modulation(nc, e):
    ring, ps = e.ring, e.ps
    with ExitStack() as ctx:
        sb = lambda name, shape: ctx.enter_context(nc.sbuf_tensor(name, shape, F32))
        sem = phase_semaphores(nc, ctx)
        rows_a = sb("rows_a", [P, P])
        rows_b = sb("rows_b", [92, P])
        raw = sb("ctx_tokens", [P, TB, D])
        xn = sb("normed_tokens", [P, TB, D])
        ss = sb("square_sums", [P, 4])
        rstd = sb("rstd", [P, 4])
        scale1 = sb("scale1", [P, KB, 2])
        rows_in, x_in, ctx_in = sem("rows_in"), sem("x_in"), sem("ctx_in")
        silu_done, rows_turned, cols_ready = sem("silu_done"), sem("rows_turned"), sem("cols_ready")
        squares, var_ready, root_ready, xn_ready = sem("squares"), sem("var_ready"), sem("root_ready"), sem("xn_ready")
        scale1_ready, x_turned, h_out = sem("scale1_ready"), sem("x_turned"), sem("h_out")
        cond_bank_free, cond_turned = sem("cond_bank_free"), sem("cond_turned")
        cond_rows = e.lat[0:2, 0, 0:2 * D]
        ADA1 = 2 * D // CG
        normed = [xn[:, 0], xn[:, 1], raw[:, 0], raw[:, 1]]
        block = ctx.enter_context(nc.Block())

        @block.sync
        def _(sp):
            ring.load_turn(sp, turn_of(e.io["w_ada"][0], slice(0, CG)), 0)
            with sp.Fori(1, ADA1) as g:
                ring.load_turn(sp, turn_of(e.io["w_ada"][0], ds(g * CG, CG)), g)
            ring.load_turn(sp, turn_of(e.io["w_in"][0], slice(RK, RK + CG)), ADA1)

        @block.scalar
        def _(act):
            io = e.io
            for dst, vec in ((rows_b[0:16], io["c"][0]), (rows_b[16:32], io["c_ctx"]), (rows_b[56:72], io["g_pre_2"][0]),
                             (rows_b[72:88], io["g_mem_2"][0]), (rows_b[88:92], io["b_alpha_2"][0]),
                             (rows_a[0:96], io["b_ada"][0]), (rows_a[96:112], io["norm1_g"][0]),
                             (rows_a[112:128], io["norm2_g"][0])):
                act.dma_start(dst, rows_of(vec)).then_inc(rows_in, 16)
            act.dma_start(rows_b[32:56], io["m_conv"][0].rearrange("j (r c) -> (j r) c", c=P)).then_inc(rows_in, 16)
            act.dma_start(e.ident[:], io["k_ident"]).then_inc(rows_in, 16)
            act.dma_start(e.x[:], tokens_of(io["x"][0])).then_inc(x_in, 16)
            act.dma_start(raw[:], tokens_of(io["ctx"][0])).then_inc(ctx_in, 16)
            act.wait_ge(rows_in, 160)
            act.activation(rows_b[0:32], rows_b[0:32], ACT.Silu).then_inc(silu_done, 1)
            act.wait_ge(x_in, 16)
            act.wait_ge(ctx_in, 16)
            for j, t in enumerate((e.x[:, 0], e.x[:, 1], raw[:, 0], raw[:, 1])):
                if j:
                    act.wait_ge(squares, j)
                act.activation(ps[:, 2:6].rearrange("p b n -> p (b n)"), t, ACT.Square, accum_out=ss[:, j:j + 1]).then_inc(squares, 1)
            act.wait_ge(var_ready, 1)
            act.activation(rstd[:], rstd[:], ACT.Sqrt).then_inc(root_ready, 1)
            act.wait_ge(scale1_ready, 1)
            for k in range(KB):
                act.wait_ge(x_turned, k + 1)
                bank = ps[:, 4 + k % 2]
                for j, dst in enumerate((e.hT, e.chT)):
                    act.activation(dst[:, k], bank[:, j * T:(j + 1) * T], ACT.Identity, scale=scale1[:, k, j:j + 1],
                                   bias=e.ada[:, k, j:j + 1]).then_inc(h_out, 1)

        @block.vector
        def _(dve):
            step = e.dve_step
            dve.sem_inc(cond_bank_free, 2)
            dve.wait_ge(rows_turned, 1)
            step(dve.tensor_copy(e.cols_b[:], ps[:, 6, 0:92]))
            dve.tensor_copy(e.cT[:], ps[:, 6, 0:32].rearrange("p (v k) -> p k v", v=2)).then_inc(cols_ready, 1)
            dve.wait_ge(rows_turned, 2)
            step(dve.tensor_copy(e.cols_a[:], ps[:, 7, 0:P]))
            dve.wait_ge(squares, 4)
            dve.tensor_scalar(rstd[:], ss[:], 1.0 / D, EPS, ALU.mult, ALU.add).then_inc(var_ready, 1)
            dve.wait_ge(root_ready, 1)
            step(dve.reciprocal(rstd[:], rstd[:]))
            for j, t in enumerate((e.x[:, 0], e.x[:, 1], raw[:, 0], raw[:, 1])):
                dve.tensor_scalar(normed[j], t, rstd[:, j:j + 1], None, ALU.mult).then_inc(xn_ready, 1)
            with dve.Fori(0, ADA1 // 2) as i:
                for j in range(2):
                    dve.wait_ge(ring.used, (i * 2 + (j + 1)) * SLOTS)
                    dve.tensor_scalar(cond_rows[:, ds((i * 2 + j) * CG, CG)], ps[0:2, j], 1.0, None, ALU.mult).then_inc(cond_bank_free, 1)
            dve.wait_ge(cond_turned, 1)
            step(dve.tensor_tensor(e.ada[:], ps[:, 6, 0:4 * KB].rearrange("p (n v) -> p n v", v=2),
                                   e.cols_a[:, 0:2 * KB].unsqueeze(2).to_broadcast([P, 2 * KB, 2]), ALU.add))
            dve.scalar_tensor_tensor(scale1[:], e.ada[:, KB:2 * KB], 1.0,
                                     e.cols_a[:, 96:112].unsqueeze(2).to_broadcast([P, KB, 2]),
                                     ALU.add, ALU.mult).then_inc(scale1_ready, 1)

        @block.tensor
        def _(pe):
            pe.wait_ge(rows_in, 160)
            pe.wait_ge(silu_done, 1)
            pe.transpose(ps[:, 6, 0:92], rows_b[:], e.ident[0:92, 0:92]).then_inc(rows_turned, 1)
            pe.transpose(ps[:, 7, 0:P], rows_a[:], e.ident[:]).then_inc(rows_turned, 1)
            pe.wait_ge(cols_ready, 1)
            with pe.Fori(0, ADA1 // 2) as i:
                for j in range(2):
                    pe.wait_ge(cond_bank_free, i * 2 + (j + 1))
                    for s in range(SLOTS):
                        ring.arrived(pe, s, i * 2 + j)
                        for kk in range(TILE_K):
                            k = s * TILE_K + kk
                            mm = pe.matmul(ps[0:2, j], e.cT[:, k], ring.tile[:, s, kk], start=(k == 0), stop=(k == KB - 1))
                        mm.then_inc(ring.used, 1)
            pe.wait_ge(cond_bank_free, ADA1 + 2)
            for n in range(2 * KB):
                tr = pe.transpose(ps[:, 6, 2 * n:2 * n + 2], cond_rows[:, n * P:(n + 1) * P], e.ident[0:2, 0:2])
            tr.then_inc(cond_turned, 1)
            pe.wait_ge(xn_ready, 4)
            for k in range(KB):
                if k >= 2:
                    pe.wait_ge(h_out, 2 * (k - 1))
                for j in range(4):
                    tr = pe.transpose(ps[:, 4 + k % 2, j * P:(j + 1) * P], normed[j][:, k * P:(k + 1) * P], e.ident[:])
                tr.then_inc(x_turned, 1)
    ring.turn += ADA1


def phase_projection(nc, e):
    ring, ps, io = e.ring, e.ps, e.io
    with ExitStack() as ctx:
        sem = phase_semaphores(nc, ctx)
        tb_done, bank_free, gates_in, gates_done = sem("tb_done"), sem("bank_free"), sem("gates_in"), sem("gates_done")
        w_gate = ctx.enter_context(nc.sbuf_tensor("w_gate", [P, KB, N_GATES], F32))
        w_in, base = io["w_in"][0], ring.turn
        runs = ((1, 3, 4, 2), (7, 3, 4, 2), (4, 3, 2, 1), (10, 1, 2, 1), (11, 1, 2, 0), (0, 1, 2, 0))
        n_turns = sum(n for _, n, _, _ in runs)
        ADA1, ADA2 = 2 * D // CG, 4 * D // CG
        assert sum(n * m for _, n, _, m in runs) == ADA2
        cond_tile = ctx.enter_context(nc.sbuf_tensor("cond_ring", [P, SLOTS, TILE_K, CG], F32))
        cond_acc = ctx.enter_context(nc.sbuf_tensor("cond_acc", [P, 2, CG], F32))
        cond_bias = ctx.enter_context(nc.sbuf_tensor("cond_bias", [1, CG], F32))
        cond_row = ctx.enter_context(nc.sbuf_tensor("cond_row", [1, CG], F32))
        ones = ctx.enter_context(nc.sbuf_tensor("ones", [P, 1], F32))
        cond_landed = [sem(f"cond_landed{s}") for s in range(SLOTS)]
        cond_bias_in, cond_used, cond_summed = sem("cond_bias_in"), sem("cond_used"), sem("cond_summed")
        cond_done, cond_row_ready, cond_stored, ones_ready, go = sem("cond_done"), sem("cond_row_ready"), sem("cond_stored"), sem("ones_ready"), sem("store_go")
        block = ctx.enter_context(nc.Block())

        @block.sync
        def _(sp):
            turn = base
            for first, n, _, _ in runs:
                skip = 1 if turn == base else 0
                with sp.Fori(skip, n) as i:
                    ring.load_turn(sp, turn_of(w_in, ds((i + first) * CG, CG)), i + turn)
                turn += n
            ring.load_turn(sp, turn_of(w_in, slice(GR, GR + CG)), turn)

        @block.scalar
        def _(act):
            act.dma_start(e.gate_bias[:], io["m_gate_bias"][0].rearrange("a b c -> (a b c)").partition_broadcast(P)).then_inc(e.gate_bias_in, 16)

            def load(g, first):
                for s in range(SLOTS):
                    if not first:
                        act.wait_ge(cond_used, (g - 1) * SLOTS + (s + 1))
                    act.dma_start(cond_tile[:, s], k_tile(io["w_ada"][0], s, ds((g + ADA1) * CG, CG))).then_inc(cond_landed[s], 16)

            load(0, True)
            with act.Fori(1, ADA2) as g:
                load(g, False)

        @block.gpsimd
        def _(pool):
            pool.memset(ones[:], 1.0).then_inc(ones_ready, 1)
            pool.dma_start(w_gate[:], w_in[:, MG:MG + N_GATES].rearrange("(k p) n -> p k n", p=P)).then_inc(gates_in, 16)
            with pool.Fori(0, ADA2) as g:
                pool.wait_ge(cond_row_ready, g + 1)
                pool.sem_inc(go, 1)
                pool.dma_start(cond_bias[:], io["b_ada"][0:1, ds((g + ADA1) * CG, CG)]).then_inc(cond_bias_in, 16)
                pool.wait_ge(cond_row_ready, g + 2)
                pool.sem_inc(go, 1)
                pool.dma_start(e.mod_rows[0:1, ds(g * CG, CG)], cond_row[:]).then_inc(cond_stored, 16)
                pool.wait_ge(cond_stored, g * 16 + 16)
                pool.sem_inc(go, 1)

        @block.tensor
        def _(pe):
            lhs = lambda k, j: (e.hT if j < TB else e.chT)[:, k, (j % TB) * P:(j % TB + 1) * P]
            turn, used, summed = base, 0, 0
            pe.wait_ge(ones_ready, 1)
            for first, n, ntb, m in runs:
                with pe.Fori(0, n) as i:
                    gemm_token_major(pe, ring, [(s, i + turn) for s in range(SLOTS)], lhs,
                                     [ps[:, 2 + j] for j in range(ntb)],
                                     lambda j: pe.wait_ge(bank_free, i * ntb + (used + j + 1 + 4 - ntb)), tb_done)
                    for j in range(m):
                        g = i * m + (summed + j)
                        pe.wait_ge(cond_summed, g + 1)
                        pe.wait_ge(cond_row_ready, g + 1)
                        pe.matmul(ps[0:1, 0], ones[:], cond_acc[:, j], start=True, stop=True).then_inc(cond_done, 1)
                turn, used, summed = turn + n, used + n * ntb, summed + n * m
            pe.wait_ge(gates_in, 16)
            for j in range(4):
                for k in range(KB):
                    mm = pe.matmul(ps[:, 6, j * N_GATES:(j + 1) * N_GATES], lhs(k, j), w_gate[:, k],
                                   start=(j == 0 and k == 0), stop=(k == KB - 1), skip_group_check=True)
            mm.then_inc(gates_done, 1)

        @block.vector
        def _(dve):
            step = e.dve_step
            dve.sem_inc(bank_free, 4)
            dve.sem_inc(cond_row_ready, 1)
            turn, done, summed = base, 0, 0
            for first, n, ntb, m in runs:
                with dve.Fori(0, n) as i:
                    step.enter(i, m * SLOTS * (TILE_K - 1))
                    for j in range(m):
                        g = i * m + (summed + j)
                        for s in range(SLOTS):
                            dve.wait_ge(cond_landed[s], (g + 1) * 16)
                            for kk in range(TILE_K):
                                k, acc = s * TILE_K + kk, cond_acc[:, j]
                                if k == 0:
                                    x = dve.tensor_scalar(acc, cond_tile[:, s, kk], e.cT[:, k, 0:1], None, ALU.mult)
                                else:
                                    x = dve.scalar_tensor_tensor(acc, cond_tile[:, s, kk], e.cT[:, k, 0:1], acc, ALU.mult, ALU.add)
                                if kk < TILE_K - 1:
                                    step(x)
                            x.then_inc(cond_used, 1)
                            dve.wait_ge(cond_used, g * SLOTS + (s + 1))
                        dve.sem_inc(cond_summed, 1)
                    for j in range(ntb):
                        if j < ntb - 1:
                            dve.wait_ge(tb_done, i * (ntb - 1) + (done + j + 1))
                        else:
                            dve.wait_ge(ring.used, (i + (turn + 1)) * SLOTS)
                        if j < TB:
                            dst = e.lat[:, j, ds((i + first) * CG, CG)]
                        else:
                            dst = e.cxt[:, j - TB, ds((i + (0 if first == 1 else 3)) * CG, CG)]
                        dve.tensor_scalar(dst, ps[:, 2 + j], 1.0, None, ALU.mult).then_inc(bank_free, 1)
                    for j in range(m):
                        g = i * m + (summed + j)
                        dve.wait_ge(cond_done, g + 1)
                        dve.wait_ge(cond_bias_in, (g + 1) * 16)
                        dve.tensor_tensor(cond_row[:], ps[0:1, 0], cond_bias[:], ALU.add).then_inc(cond_row_ready, 1)
                step.leave(n)
                turn, done, summed = turn + n, done + n * (ntb - 1), summed + n * m
            dve.wait_ge(gates_done, 1)
            dve.wait_ge(e.gate_bias_in, 16)
            dve.tensor_tensor(e.gates[:], ps[:, 6, 0:4 * N_GATES].rearrange("p (j g) -> p j g", j=4),
                              e.gate_bias[:].unsqueeze(1).to_broadcast([P, 4, N_GATES]), ALU.add).then_inc(e.gates_ready, 1)
    ring.turn += n_turns


def log_sigmoid_on_vector(dve, step, e, z, u, w, out):
    e.ls_uses += 1
    dve.scalar_tensor_tensor(u, z, -1.0, z, ALU.mult, ALU.min).then_inc(e.ls_neg_abs, 1)
    dve.wait_ge(e.ls_exp, e.ls_uses)
    dve.tensor_scalar(w, u, 1.0, None, ALU.add).then_inc(e.ls_one_plus, 1)
    dve.wait_ge(e.ls_ln, e.ls_uses)
    step(dve.scalar_tensor_tensor(u, w, -1.0, u, ALU.add, ALU.subtract))
    step(dve.reciprocal(w, w))
    step(dve.tensor_tensor(u, u, w, ALU.mult))
    step(dve.tensor_tensor(out, out, u, ALU.subtract))
    step(dve.scalar_tensor_tensor(out, z, 0.0, out, ALU.min, ALU.subtract))


def log_sigmoid_on_scalar(act, e, use, u, w, out):
    act.wait_ge(e.ls_neg_abs, use)
    act.activation(u, u, ACT.Exp).then_inc(e.ls_exp, 1)
    act.wait_ge(e.ls_one_plus, use)
    act.activation(out, w, ACT.Ln).then_inc(e.ls_ln, 1)


def head_norm_on_vector(dve, step, e, y, sq, stat, width):
    e.hn_uses += 1
    n = y.shape[1]
    wide = [P, n, width]
    step(dve.tensor_reduce(stat, y, AX, ALU.add))
    step(dve.tensor_scalar(stat, stat, 1.0 / width, None, ALU.mult))
    dve.tensor_tensor(y, y, stat.unsqueeze(2).to_broadcast(wide), ALU.subtract).then_inc(e.hn_centred, 1)
    dve.wait_ge(e.hn_squared, e.hn_uses)
    step(dve.tensor_reduce(stat, sq, AX, ALU.add))
    dve.tensor_scalar(stat, stat, 1.0 / width, EPS, ALU.mult, ALU.add).then_inc(e.hn_var, 1)
    dve.wait_ge(e.hn_root, e.hn_uses)
    step(dve.reciprocal(stat, stat))
    step(dve.tensor_tensor(y, y, stat.unsqueeze(2).to_broadcast(wide), ALU.mult))


def head_norm_on_scalar(act, e, use, y, sq, stat):
    act.wait_ge(e.hn_centred, use)
    act.activation(sq, y, ACT.Square).then_inc(e.hn_squared, 1)
    act.wait_ge(e.hn_var, use)
    act.activation(stat, stat, ACT.Sqrt).then_inc(e.hn_root, 1)


def phase_retention(nc, e):
    ps, io, H = e.ps, e.io, R_HEADS
    with ExitStack() as ctx:
        sb = lambda name, shape: ctx.enter_context(nc.sbuf_tensor(name, shape, F32))
        sem = phase_semaphores(nc, ctx)
        rope, rel, pos = sb("rope", [P, TB, 64]), sb("rel", [P, TB, 3 * T]), sb("pos", [P, TB, 4])
        z, u, w, lg = (sb(f"ls_ret_{n}", [P, 2 * H]) for n in "zuwl")
        dec = sb("decays", [P, TB, 4, H])
        rot = sb("rotated_qk", [P, TB, 2 * H, 2, 32])
        tmp = sb("rotary_tmp", [P, TB, 2 * H, 32])
        kdec = sb("k_decayed", [P, TB, H, 2, R_DK])
        qdec = sb("q_decayed", [P, TB, H, 2, R_DK])
        turned = sb("turned_qk", [P, 8, 2, T])
        state = sb("ret_state", [P, H, R_DV])
        dti = sb("decay_matrix", [P, 2, TB, T])
        att = sb("ret_att", [P, 2, TB, T])
        y = rot[:].rearrange("p b g a n -> p (b g a n)").rearrange("p (h e) -> p h e", e=R_DV)
        sq = kdec[:].rearrange("p b h a n -> p (b h a n)").rearrange("p (h e) -> p h e", e=R_DV)
        stat = sb("ret_stat", [P, TB * H])
        tables, expo_ready, dec_ready = sem("tables"), sem("expo_ready"), sem("dec_ready")
        rot1_ready, qdec_ready, kdec_ready, rot0_ready = sem("rot1_ready"), sem("qdec_ready"), sem("kdec_ready"), sem("rot0_ready")
        state_done, state_out = sem("state_done"), sem("state_out")
        turn_done, turn_out = sem("turn_done"), sem("turn_out")
        dlog_ready, dexp_ready, decay_ready = sem("dlog_ready"), sem("dexp_ready"), sem("decay_ready")
        att_done, att_ready, y_done, y_out, gate_ready = sem("att_done"), sem("att_ready"), sem("y_done"), sem("y_out"), sem("gate_ready")
        q_cols = lambda tb: rot[:, tb, 0:H].rearrange("p h a n -> p h (a n)")
        use = e.ls_uses + 1
        hn_use = e.hn_uses + 1
        lat_gate = e.lat[:, :, RG:RG + H * R_DV]
        FILLS = 8

        def rotary(eng, step, tb, ready):
            v = e.lat[:, tb, RQ:RQ + 2 * H * R_DK].rearrange("p (h a n) -> p h a n", a=2, n=32)
            cos, sin = (rope[:, tb, c:c + 32].unsqueeze(1).to_broadcast([P, 2 * H, 32]) for c in (0, 32))
            t1, t2, o = v[:, :, 0], v[:, :, 1], rot[:, tb]
            step(eng.tensor_tensor(o[:, :, 0], t1, cos, ALU.mult))
            step(eng.tensor_tensor(tmp[:, tb], t2, sin, ALU.mult))
            step(eng.tensor_tensor(o[:, :, 0], o[:, :, 0], tmp[:, tb], ALU.subtract))
            step(eng.tensor_tensor(o[:, :, 1], t2, cos, ALU.mult))
            step(eng.tensor_tensor(tmp[:, tb], t1, sin, ALU.mult))
            eng.tensor_tensor(o[:, :, 1], o[:, :, 1], tmp[:, tb], ALU.add).then_inc(ready, 1)

        block = ctx.enter_context(nc.Block())

        @block.scalar
        def _(act):
            act.dma_start(z[:], io["ret_decay"][0].rearrange("a h -> (a h)").partition_broadcast(P)).then_inc(tables, 16)
            act.dma_start(rope[:], io["k_rope"]).then_inc(tables, 16)
            act.dma_start(pos[:], io["k_pos"]).then_inc(tables, 16)
            act.dma_start(rel[:], io["k_rel"]).then_inc(tables, 16)
            log_sigmoid_on_scalar(act, e, use, u[:], w[:], lg[:])
            act.wait_ge(expo_ready, 1)
            act.activation(dec[:], dec[:], ACT.Exp).then_inc(dec_ready, 1)
            act.wait_ge(state_done, 1)
            act.activation(state[:], ps[:, 0:2].rearrange("p b (h e) -> p (b h) e", e=R_DV), ACT.Copy).then_inc(state_out, 1)
            for f in range(FILLS):
                act.wait_ge(turn_done, f + 1)
                act.activation(turned[:, f].rearrange("p a t -> p (a t)"), ps[:, 2 + f % 2], ACT.Copy,
                               scale=R_DK ** -0.5 if f in (2, 3) else 1.0).then_inc(turn_out, 1)
            for h in range(H):
                act.wait_ge(dlog_ready, h + 1)
                act.activation(dti[:, h % 2], dti[:, h % 2], ACT.Exp).then_inc(dexp_ready, 1)
            for tb in range(TB):
                act.wait_ge(y_done, H)
                act.activation(y[:, tb * H:(tb + 1) * H], ps[:, 2 * tb:2 * tb + 2].rearrange("p b (h e) -> p (b h) e", e=R_DV),
                               ACT.Copy).then_inc(y_out, 1)
            head_norm_on_scalar(act, e, hn_use, y, sq, stat[:])
            act.activation(lat_gate, lat_gate, ACT.Silu).then_inc(gate_ready, 1)

        @block.vector
        def _(dve):
            step = e.dve_step
            dve.wait_ge(tables, 64)
            log_sigmoid_on_vector(dve, step, e, z[:], u[:], w[:], lg[:])
            for tb in range(TB):
                for kind in range(4):
                    d = kind % 2
                    x = dve.tensor_scalar(dec[:, tb, kind], lg[:, d * H:(d + 1) * H], pos[:, tb, kind:kind + 1], None, ALU.mult)
                    if (tb, kind) != (TB - 1, 3):
                        step(x)
            x.then_inc(expo_ready, 1)
            rotary(dve, step, 0, rot0_ready)
            dve.wait_ge(dec_ready, 1)
            for tb in range(TB):
                for d in range(2):
                    dve.scalar_tensor_tensor(kdec[:, tb, :, d], e.cxt[:, tb, 0:H * R_DK].rearrange("p (h n) -> p h n", h=H),
                                             R_DK ** -0.5, dec[:, tb, d].unsqueeze(2).to_broadcast([P, H, R_DK]),
                                             ALU.mult, ALU.mult).then_inc(kdec_ready, 1)
            for h in range(H + 1):
                if h < H:
                    if h >= 2:
                        dve.wait_ge(att_ready, h - 1)
                    step(dve.tensor_scalar(dti[:, h % 2], rel[:, :, 0:T], lg[:, h:h + 1], None, ALU.mult))
                    dve.scalar_tensor_tensor(dti[:, h % 2], rel[:, :, T:2 * T], lg[:, H + h:H + h + 1], dti[:, h % 2],
                                             ALU.mult, ALU.add).then_inc(dlog_ready, 1)
                if h >= 1:
                    g = h - 1
                    dve.wait_ge(decay_ready, g + 1)
                    dve.wait_ge(att_done, g + 1)
                    if g >= 2:
                        dve.wait_ge(y_done, g - 1)
                    dve.tensor_tensor(att[:, g % 2], ps[:, 4 + g % 2].rearrange("p (s t) -> p s t", s=TB), dti[:, g % 2],
                                      ALU.mult).then_inc(att_ready, 1)
            dve.wait_ge(y_out, TB)
            head_norm_on_vector(dve, step, e, y, sq, stat[:], R_DV)
            dve.wait_ge(gate_ready, 1)
            step(dve.tensor_tensor(lat_gate, lat_gate, y.rearrange("p (b h) e -> p b (h e)", b=TB), ALU.mult))

        @block.gpsimd
        def _(pool):
            step = e.pool_step
            pool.wait_ge(tables, 64)
            rotary(pool, step, 1, rot1_ready)
            pool.wait_ge(rot1_ready, 1)
            pool.wait_ge(dec_ready, 1)
            pool.wait_ge(rot0_ready, 1)
            for tb in range(TB):
                for d in range(2):
                    pool.tensor_tensor(qdec[:, tb, :, d], q_cols(tb),
                                       dec[:, tb, 2 + d].unsqueeze(2).to_broadcast([P, H, R_DK]), ALU.mult).then_inc(qdec_ready, 1)
            for h in range(H):
                pool.wait_ge(dexp_ready, h + 1)
                pool.tensor_tensor(dti[:, h % 2], dti[:, h % 2], rel[:, :, 2 * T:3 * T], ALU.add).then_inc(decay_ready, 1)

        @block.tensor
        def _(pe):
            pe.wait_ge(kdec_ready, 4)
            for h in range(H):
                for tb in range(TB):
                    mm = pe.matmul(ps[:, h // 4, (h % 4) * P:(h % 4 + 1) * P],
                                   kdec[:, tb, h].rearrange("p a n -> p (a n)"),
                                   e.cxt[:, tb, 512 + h * R_DV:512 + (h + 1) * R_DV], start=(tb == 0), stop=(tb == TB - 1))
            mm.then_inc(state_done, 1)
            pe.wait_ge(rot0_ready, 1)
            pe.wait_ge(rot1_ready, 1)
            for f in range(FILLS):
                if f == 4:
                    pe.wait_ge(qdec_ready, 4)
                if f >= 2:
                    pe.wait_ge(turn_out, f - 1)
                for a in range(2):
                    for tb in range(TB):
                        if f < 4:
                            j = 2 * f + a
                            src = rot[:, tb, 2 * j:2 * j + 2].rearrange("p h a n -> p (h a n)")
                        else:
                            src = qdec[:, tb, 2 * (f - 4) + a].rearrange("p a n -> p (a n)")
                        tr = pe.transpose(ps[:, 2 + f % 2, a * T + tb * P:a * T + (tb + 1) * P], src, e.ident[:])
                tr.then_inc(turn_done, 1)
            pe.wait_ge(turn_out, FILLS)
            pe.wait_ge(state_out, 1)

            def scores(h):
                lo, pair = (h % 2) * R_DK, h // 2
                if h >= 2:
                    pe.wait_ge(att_ready, h - 1)
                for s in range(TB):
                    mm = pe.matmul(ps[:, 4 + h % 2, s * T:(s + 1) * T], turned[lo:lo + R_DK, 2 + pair // 2, pair % 2, s * P:(s + 1) * P],
                                   turned[lo:lo + R_DK, pair // 2, pair % 2, :], start=True, stop=True)
                mm.then_inc(att_done, 1)

            scores(0)
            for h in range(H):
                if h + 1 < H:
                    scores(h + 1)
                pe.wait_ge(att_ready, h + 1)
                for tb in range(TB):
                    out = ps[:, 2 * tb + h // 4, (h % 4) * P:(h % 4 + 1) * P]
                    for s in range(TB):
                        pe.matmul(out, att[:, h % 2, s, tb * P:(tb + 1) * P], e.lat[:, s, RV + h * R_DV:RV + (h + 1) * R_DV],
                                  start=(s == 0), stop=False)
                    mm = pe.matmul(out, turned[:, 4 + h // 2, h % 2, tb * P:(tb + 1) * P], state[:, h], start=False, stop=True)
                mm.then_inc(y_done, 1)


def phase_mlstm(nc, e):
    ps, io, H = e.ps, e.io, M_HEADS
    J, R = 2 * TB, 2 * M_HEADS
    with ExitStack() as ctx:
        sb = lambda name, shape: ctx.enter_context(nc.sbuf_tensor(name, shape, F32))
        sem = phase_semaphores(nc, ctx)
        causal = sb("causal", [P, TB, 2 * T])
        ltri = sb("ltri", [P, 3, P])
        pick = sb("pick", [8, 8, P])
        qT, kT = sb("mq_T", [P, H, T]), sb("mk_T", [P, H, 2 * T])
        z, u, w, lf = (sb(f"ls_gate_{n}", [P, J, R]) for n in "zuwl")
        G, us = sb("gate_sums", [P, J, R]), sb("u_cols", [P, J, R])
        urow = sb("u_rows", [R, J * P])
        mctx = sb("ctx_max", [R, 1])
        M = sb("running_max", [R, 2, T])
        em = sb("exp_minus_m", [P, TB, R])
        ew = sb("weights_exp", [P, 2, J, T])
        att = sb("m_att", [P, 2, J, T])
        den = sb("den", [P, TB, 2])
        hs = sb("m_y", [P, TB, H, M_DV])
        sq = sb("m_squares", [P, TB * H, M_DV])
        stat = sb("m_stat", [P, TB * H])
        tables, conv_in, conv_out, conv_ready, silu_out = sem("m_tables"), sem("conv_in"), sem("conv_out"), sem("conv_ready"), sem("silu_out")
        lf_ready, sums_done, u_ready, u_turned = sem("lf_ready"), sem("sums_done"), sem("u_ready"), sem("u_turned")
        max_ready, max_turned, m_ready, em_ready = sem("max_ready"), sem("max_turned"), sem("m_ready"), sem("em_ready")
        mrow_done, gap_ready, exp_ready, weight_ready = sem("mrow_done"), sem("gap_ready"), sem("exp_ready"), sem("weight_ready")
        qk_done, m_att_ready, num_done, h_ready, o_ready = sem("qk_done"), sem("m_att_ready"), sem("num_done"), sem("h_ready"), sem("o_ready")
        use = e.ls_uses + 1
        hn_use = e.hn_uses + 1
        lat_o = e.lat[:, :, MO:MO + H * M_DV]
        seq = ((2, 3, 0, 1), (3, 2, 1, 0))
        convs = [(e.lat, MQ + h * P, h, qT[:, h]) for h in range(H)]
        convs += [(e.lat, MK + h * P, H + h, kT[:, h, 0:T]) for h in range(H)]
        convs += [(e.cxt, 1536 + h * P, H + h, kT[:, h, T:2 * T]) for h in range(H)]
        block = ctx.enter_context(nc.Block())

        @block.scalar
        def _(act):
            act.dma_start(ltri[:], io["k_ltri"]).then_inc(tables, 16)
            act.dma_start(causal[:], io["k_causal"]).then_inc(tables, 16)
            act.dma_start(pick[:], io["k_pick"]).then_inc(tables, 16)
            log_sigmoid_on_scalar(act, e, use, u[:], w[:], lf[:])
            for n, (_, _, _, dst) in enumerate(convs):
                act.wait_ge(conv_ready, n + 1)
                act.activation(dst, dst, ACT.Silu).then_inc(silu_out, 1)
            act.wait_ge(m_ready, 1)
            act.activation(em[:], em[:], ACT.Exp).then_inc(em_ready, 1)
            for n in range(R):
                act.wait_ge(gap_ready, n + 1)
                act.activation(ew[:, n % 2], ew[:, n % 2], ACT.Exp, scale=-1.0).then_inc(exp_ready, 1)
            head_norm_on_scalar(act, e, hn_use, hs[:].rearrange("p b h e -> p (b h) e"), sq[:], stat[:])
            act.activation(lat_o, lat_o, ACT.Sigmoid).then_inc(o_ready, 1)

        @block.vector
        def _(dve):
            step = e.dve_step
            gates = e.gates[:].rearrange("p j (d k h) -> p j d k h", d=2, k=2)
            by_dir = lambda t: t[:].rearrange("p j (d h) -> p j d h", d=2)
            step(dve.tensor_copy(by_dir(z), gates[:, :, :, 1]))
            log_sigmoid_on_vector(dve, step, e, z[:], u[:], w[:], lf[:])
            dve.sem_inc(lf_ready, 1)
            for n, (_, _, r, dst) in enumerate(convs):
                dve.wait_ge(conv_in, n + 1)
                x = ps[:, n % 2, 0:T]
                tap = [e.cols_b[:, 32 + 8 * j + r:33 + 8 * j + r] for j in range(3)]
                step(dve.tensor_scalar(dst, x, tap[1], None, ALU.mult))
                step(dve.scalar_tensor_tensor(dst[:, 1:T], x[:, 0:T - 1], tap[0], dst[:, 1:T], ALU.mult, ALU.add))
                dve.scalar_tensor_tensor(dst[:, 0:T - 1], x[:, 1:T], tap[2], dst[:, 0:T - 1], ALU.mult,
                                         ALU.add).then_inc(conv_ready, 1)
            dve.wait_ge(sums_done, 1)
            step(dve.tensor_copy(G[:], ps[:, 2, 0:J * R].rearrange("p (j r) -> p j r", j=J)))
            dve.tensor_tensor(by_dir(us), gates[:, :, :, 0], by_dir(G), ALU.subtract).then_inc(u_ready, 1)
            dve.wait_ge(u_turned, 1)
            step(dve.tensor_copy(urow[:], ps[0:R, 3]))
            step(dve.tensor_reduce(mctx[:], urow[:, T:2 * T], AX, ALU.max))
            step(dve.tensor_scalar(mctx[:], mctx[:], 0.0, None, ALU.max))
            step(dve.tensor_tensor_scan(M[:, 0], urow[:, 0:T], urow[:, 0:T], mctx[:], ALU.max, ALU.max))
            dve.tensor_tensor_scan(M[:, 1, ::-1], urow[:, 0:T][:, ::-1], urow[:, 0:T][:, ::-1], mctx[:], ALU.max,
                                   ALU.max).then_inc(max_ready, 1)
            dve.wait_ge(max_turned, 1)
            for d in range(2):
                for tb in range(TB):
                    at = (d * TB + tb) * R + d * H
                    step(dve.tensor_tensor(em[:, tb, d * H:(d + 1) * H], G[:, tb, d * H:(d + 1) * H], ps[:, 2, 64 + at:64 + at + H],
                                           ALU.add))
            dve.tensor_scalar(em[:], em[:], -1.0, 85.0, ALU.mult, ALU.min).then_inc(m_ready, 1)
            dve.wait_ge(em_ready, 1)

            def gaps(n):
                h, d = n // 2, n % 2
                r = d * H + h
                dve.wait_ge(mrow_done, n + 1)
                if n >= 2:
                    dve.wait_ge(m_att_ready, n - 1)
                for j in range(J):
                    x = dve.tensor_scalar(ew[:, n % 2, j], ps[:, 4 + n % 2, 0:T], us[:, j, r:r + 1], 0.0, ALU.subtract, ALU.max)
                x.then_inc(gap_ready, 1)

            def weigh(n):
                dve.wait_ge(weight_ready, n + 1)
                dve.wait_ge(qk_done, n // 2 + 1)
                if n >= 2:
                    dve.wait_ge(num_done, n - 1)
                dve.scalar_tensor_tensor(att[:, n % 2].rearrange("p j t -> p (j t)"), ps[:, 0:2].rearrange("p b n -> p (b n)"),
                                         M_DK ** -0.5, ew[:, n % 2].rearrange("p j t -> p (j t)"), ALU.mult,
                                         ALU.mult).then_inc(m_att_ready, 1)

            def divide(n):
                h, d = n // 2, n % 2
                r = d * H + h
                dve.wait_ge(num_done, n + 1)
                for tb in range(TB):
                    raw_den = ps[:, 6 + tb, M_DV:M_DV + 1]
                    step(dve.tensor_scalar(den[:, tb, 0:1], raw_den, -1.0, em[:, tb, r:r + 1], ALU.mult, ALU.max))
                    step(dve.tensor_tensor(den[:, tb, 0:1], raw_den, den[:, tb, 0:1], ALU.max))
                    step(dve.reciprocal(den[:, tb, 1:2], den[:, tb, 0:1]))
                    num, rec, out = ps[:, 6 + tb, 0:M_DV], den[:, tb, 1:2], hs[:, tb, h]
                    if d == 0:
                        x = dve.tensor_scalar(out, num, rec, None, ALU.mult)
                    else:
                        x = dve.scalar_tensor_tensor(out, num, rec, out, ALU.mult, ALU.add)
                    if tb == 0:
                        step(x)
                x.then_inc(h_ready, 1)

            gaps(0)
            for n in range(R):
                if n + 1 < R:
                    gaps(n + 1)
                weigh(n)
                divide(n)
            dve.wait_ge(h_ready, R)
            head_norm_on_vector(dve, step, e, hs[:].rearrange("p b h e -> p (b h) e"), sq[:], stat[:], M_DV)
            dve.wait_ge(o_ready, 1)
            step(dve.tensor_tensor(lat_o, lat_o, hs[:].rearrange("p b h e -> p b (h e)"), ALU.mult))

        @block.gpsimd
        def _(pool):
            pool.wait_ge(tables, 48)
            for n in range(R):
                pool.wait_ge(exp_ready, n + 1)
                d = n % 2
                pool.tensor_tensor(ew[:, n % 2, 0:TB], ew[:, n % 2, 0:TB], causal[:, :, d * T:(d + 1) * T],
                                   ALU.mult).then_inc(weight_ready, 1)

        @block.tensor
        def _(pe):
            for n, (src, col, _, _) in enumerate(convs):
                if n >= 2:
                    pe.wait_ge(conv_ready, n - 1)
                for tb in range(TB):
                    tr = pe.transpose(ps[:, n % 2, tb * P:(tb + 1) * P], src[:, tb, col:col + P], e.ident[:])
                tr.then_inc(conv_in, 1)
            pe.wait_ge(tables, 48)
            pe.wait_ge(lf_ready, 1)
            for d in range(2):
                for at, j in enumerate(seq[d]):
                    out = ps[:, 2, j * R + d * H:j * R + (d + 1) * H]
                    for i in seq[d][:at + 1]:
                        mm = pe.matmul(out, ltri[:, d if i == j else 2], lf[:, i, d * H:(d + 1) * H],
                                       start=(d == 0 and at == 0), stop=(i == j), skip_group_check=True)
            mm.then_inc(sums_done, 1)
            pe.wait_ge(u_ready, 1)
            for j in range(J):
                tr = pe.transpose(ps[0:R, 3, j * P:(j + 1) * P], us[:, j], e.ident[:])
            tr.then_inc(u_turned, 1)
            pe.wait_ge(max_ready, 1)
            for d in range(2):
                for tb in range(TB):
                    at = 64 + (d * TB + tb) * R
                    tr = pe.transpose(ps[:, 2, at:at + R], M[:, d, tb * P:(tb + 1) * P], e.ident[0:R, 0:R])
            tr.then_inc(max_turned, 1)
            pe.wait_ge(silu_out, len(convs))

            def max_row(n):
                h, d = n // 2, n % 2
                if n >= 2:
                    pe.wait_ge(gap_ready, n - 1)
                pe.matmul(ps[:, 4 + n % 2, 0:T], pick[:, d * H + h], M[:, d], start=True, stop=True).then_inc(mrow_done, 1)

            max_row(0)
            for n in range(R):
                h, d = n // 2, n % 2
                if n + 1 < R:
                    max_row(n + 1)
                if d == 0:
                    if n:
                        pe.wait_ge(m_att_ready, n)
                    for j in range(J):
                        mm = pe.matmul(ps[:, j // 2, (j % 2) * T:(j % 2 + 1) * T], kT[:, h, j * P:(j + 1) * P], qT[:, h], start=True, stop=True)
                    mm.then_inc(qk_done, 1)
                pe.wait_ge(m_att_ready, n + 1)
                if n:
                    pe.wait_ge(h_ready, n)
                for tb in range(TB):
                    blocks = [j for j in range(J) if j >= TB or j == tb or (j > tb) == (d == 1)]
                    for i, j in enumerate(blocks):
                        stat_op = att[:, n % 2, j, tb * P:(tb + 1) * P]
                        v = (e.lat[:, j, MV + h * M_DV:MV + (h + 1) * M_DV] if j < TB else
                             e.cxt[:, j - TB, 2048 + h * M_DV:2048 + (h + 1) * M_DV])
                        pe.matmul(ps[:, 6 + tb, 0:M_DV], stat_op, v, start=(i == 0), stop=(i == len(blocks) - 1), skip_group_check=True)
                        mm = pe.matmul(ps[:, 6 + tb, M_DV:M_DV + 1], stat_op, ltri[:, 2, 0:1], start=False,
                                       stop=(i == len(blocks) - 1), skip_group_check=True)
                mm.then_inc(num_done, 1)


def load_tiles(sp, ring, sources, turn, skip=0):
    for n, src in enumerate(sources):
        if n >= skip:
            ring.load(sp, n % SLOTS, src, turn + n // SLOTS)


def pieces_of(first, count, turn):
    return [(n % SLOTS, turn + n // SLOTS) for n in range(first, first + count)]


def used_after(tiles, turn):
    return turn * SLOTS + tiles


class WeightSplit:
    HALF = TILE_K // 2

    def __init__(self, nc, ctx, sem, name):
        self.hi, self.lo = (ctx.enter_context(nc.sbuf_tensor(f"{name}_{part}", [P, 4, self.HALF, CG], F32R)) for part in ("hi", "lo"))
        self.hi_ready, self.first_ready, self.free = sem(f"{name}_hi_ready"), sem(f"{name}_first_ready"), sem(f"{name}_free")

    def place(self, slot, h):
        return (2 * slot + h) % 4

    def free_after(self, tiles):
        return tiles * 2 + 4

    def write_hi(self, act, ring, piece, m):
        slot, turn = piece
        ring.arrived(act, slot, turn)
        for h in range(2):
            act.wait_ge(self.free, m * 2 + (h + 1))
            act.activation(self.hi[:, self.place(slot, h)], ring.tile[:, slot, h * self.HALF:(h + 1) * self.HALF], ACT.Copy).then_inc(self.hi_ready, 1)

    def write_lo(self, pool, ring, piece, m):
        slot, _ = piece
        for h in range(2):
            at = self.place(slot, h)
            pool.wait_ge(self.hi_ready, m * 2 + (h + 1))
            pool.tensor_tensor(self.lo[:, at], ring.tile[:, slot, h * self.HALF:(h + 1) * self.HALF], self.hi[:, at],
                               ALU.subtract).then_inc(ring.used if h else self.first_ready, 1)


def gemm_split(pe, ring, split, pieces, m, lhs, banks, wait_free, tb_done):
    n = len(pieces) * TILE_K
    for t, (slot, turn) in enumerate(pieces):
        for h in range(2):
            at = split.place(slot, h)
            if h == 0:
                pe.wait_ge(split.first_ready, m + (t + 1))
            else:
                pe.wait_ge(ring.used, turn * SLOTS + (slot + 1))
            for tb, out in enumerate(banks):
                if t == 0 and h == 0:
                    wait_free(tb)
                for kk in range(split.HALF):
                    k = t * TILE_K + h * split.HALF + kk
                    (hi, lo), w_hi, w_lo = lhs(k, tb), split.hi[:, at, kk], split.lo[:, at, kk]
                    pe.matmul(out, hi, w_hi, start=(k == 0), stop=False)
                    pe.matmul(out, hi, w_lo, start=False, stop=False)
                    mm = pe.matmul(out, lo, w_hi, start=False, stop=(k == n - 1))
                if tb == len(banks) - 1:
                    mm.then_inc(split.free, 1)
                elif t == len(pieces) - 1 and h == 1:
                    mm.then_inc(tb_done, 1)


def turn_blocks(pe, e, n_blocks, source, banks, done, freed, wait_freed):
    for f in range(n_blocks // 2):
        if f >= len(banks):
            pe.wait_ge(freed, wait_freed + f - len(banks) + 1)
        bank = banks[f % len(banks)]
        for a in range(2):
            for tb in range(TB):
                at = (a * TB + tb) * P
                tr = pe.transpose(e.ps[:, bank, at:at + P], source(2 * f + a, tb), e.ident[:])
        tr.then_inc(done, 1)


def bank_blocks(e, bank):
    return e.ps[:, bank].rearrange("p (a b t) -> p a b t", a=2, b=TB)


def phase_merge(nc, e):
    ring, ps, io, lat = e.ring, e.ps, e.io, e.lat
    with ExitStack() as ctx:
        sem = phase_semaphores(nc, ctx)
        sb = lambda name, shape: ctx.enter_context(nc.sbuf_tensor(name, shape, F32))
        sig = sb("gates_sigmoid", [P, 2, TB, CG])
        gt1 = sb("gt1", [P, D])
        prod = sb("merge_product", [P, TB, CG])
        turned, turned_out, tb_done = sem("merge_turned"), sem("merge_turned_out"), sem("merge_tb_done")
        sig_ready, merged_out, gt1_in = sem("sig_ready"), sem("merged_out"), sem("gt1_in")
        prod_ready, x_out = sem("prod_ready"), sem("x_out")
        base, N = ring.turn, D // CG
        y_src = lambda k, tb: lat[:, tb, (RG if k < 8 else MO - 1024) + k * P:][:, 0:P]
        yT = lambda k, tb: lat[:, tb, k * P:(k + 1) * P]
        merged = lat[:, :, MQ:MQ + D]
        mT_at = lambda k: (RG if k < 8 else MO - 1024) + k * P
        mT = lambda k, tb: lat[:, tb, mT_at(k):mT_at(k) + P]
        w_in = io["w_in"][0]

        def sources(n):
            cols = ds(n * CG, CG)
            return ([k_tile(w_in[:, GR:GR + D], s, cols) for s in range(4)] + [k_tile(io["w_ret_out"][0], s, cols) for s in range(2)]
                    + [k_tile(w_in[:, GM:GM + D], s, cols) for s in range(4)] + [k_tile(io["w_mlstm_out"][0], s, cols) for s in range(2)])

        block = ctx.enter_context(nc.Block())

        @block.sync
        def _(sp):
            load_tiles(sp, ring, sources(0), base, SLOTS)
            with sp.Fori(1, N) as n:
                load_tiles(sp, ring, sources(n), n * 3 + base)
            with sp.Fori(0, N) as n:
                load_tiles(sp, ring, turn_of(io["w_out"][0], ds(n * CG, CG)), n + (base + 3 * N))
            load_tiles(sp, ring, turn_of(io["peer_query"][0], slice(0, CG)), base + 4 * N)

        @block.tensor
        def _(pe):
            turn_blocks(pe, e, KB, y_src, (6, 7), turned, turned_out, 0)
            pe.wait_ge(turned_out, KB // 2)
            h_of = lambda k, tb: e.hT[:, k, tb * P:(tb + 1) * P]
            with pe.Fori(0, N) as n:
                t = n * 3 + base
                for b in range(2):
                    gemm_token_major(pe, ring, pieces_of(6 * b, 4, t), h_of, [ps[:, 4 * b], ps[:, 4 * b + 1]],
                                     lambda tb: pe.wait_ge(sig_ready, n * 4 + (2 * b + 1)) if tb == 0 else None, tb_done)
                    gemm_token_major(pe, ring, pieces_of(6 * b + 4, 2, t), lambda k, tb: yT(8 * b + k, tb),
                                     [ps[:, 4 * b + 2], ps[:, 4 * b + 3]],
                                     lambda tb: pe.wait_ge(merged_out, n * 4 + (2 * b + 1)) if tb == 0 else None, tb_done)
            pe.wait_ge(merged_out, 4 * N + 1)
            turn_blocks(pe, e, KB, lambda k, tb: merged[:, tb, k * P:(k + 1) * P], (6, 7), turned, turned_out, KB // 2)
            pe.wait_ge(turned_out, KB)
            with pe.Fori(0, N) as n:
                gemm_token_major(pe, ring, pieces_of(0, 4, n + (base + 3 * N)), mT, [ps[:, 0], ps[:, 1]],
                                 lambda tb: pe.wait_ge(prod_ready, n * 2 + (tb + 1)), tb_done)

        @block.scalar
        def _(act):
            act.sem_inc(sig_ready, 1)
            act.dma_start(gt1[:], e.mod_rows[0, 0:D].partition_broadcast(P)).then_inc(gt1_in, 16)
            for f in range(KB // 2):
                act.wait_ge(turned, f + 1)
                act.activation(lat[:, :, 2 * f * P:(2 * f + 2) * P].rearrange("p b (a t) -> p a b t", a=2), bank_blocks(e, 6 + f % 2),
                               ACT.Copy).then_inc(turned_out, 1)
            with act.Fori(0, N) as n:
                for b in range(2):
                    act.wait_ge(merged_out, n * 4 + (2 * b + 1))
                    for tb in range(TB):
                        if tb == 0:
                            act.wait_ge(tb_done, n * 4 + (2 * b + 1))
                        else:
                            act.wait_ge(ring.used, n * 12 + used_after(6 * b + 4, base))
                        act.activation(sig[:, b, tb], ps[:, 4 * b + tb], ACT.Sigmoid).then_inc(sig_ready, 1)
            for f in range(KB // 2):
                act.wait_ge(turned, KB // 2 + f + 1)
                at = mT_at(2 * f)
                act.activation(lat[:, :, at:at + 2 * P].rearrange("p b (a t) -> p a b t", a=2), bank_blocks(e, 6 + f % 2),
                               ACT.Copy).then_inc(turned_out, 1)

        @block.vector
        def _(dve):
            step = e.dve_step
            for freed in (merged_out, prod_ready, x_out):
                dve.sem_inc(freed, 1)
            with dve.Fori(0, N) as n:
                step.enter(n, TB)
                for b in range(2):
                    for tb in range(TB):
                        dve.wait_ge(sig_ready, n * 4 + (2 * b + tb + 2))
                        if tb == 0:
                            dve.wait_ge(tb_done, n * 4 + (2 * b + 2))
                        else:
                            dve.wait_ge(ring.used, n * 12 + used_after(6 * b + 6, base))
                        out, y = merged[:, tb, ds(n * CG, CG)], ps[:, 4 * b + 2 + tb]
                        if b == 0:
                            dve.tensor_tensor(out, sig[:, b, tb], y, ALU.mult).then_inc(merged_out, 1)
                        else:
                            step(dve.tensor_tensor(sig[:, b, tb], sig[:, b, tb], y, ALU.mult))
                            dve.tensor_tensor(out, out, sig[:, b, tb], ALU.add).then_inc(merged_out, 1)
            step.leave(N)
            dve.wait_ge(gt1_in, 16)
            with dve.Fori(0, N) as n:
                cols = ds(n * CG, CG)
                for tb in range(TB):
                    if tb == 0:
                        dve.wait_ge(tb_done, n + (4 * N + 1))
                    else:
                        dve.wait_ge(ring.used, n * SLOTS + used_after(SLOTS, base + 3 * N))
                    if tb == 0:
                        dve.wait_ge(x_out, n * 2 + 1)
                    dve.tensor_tensor(prod[:, tb], ps[:, tb], gt1[:, cols], ALU.mult).then_inc(prod_ready, 1)
                    dve.wait_ge(prod_ready, n * 2 + (tb + 2))
                    dve.tensor_tensor(e.x[:, tb, cols], e.x[:, tb, cols], prod[:, tb], ALU.add).then_inc(x_out, 1)
    ring.turn += 4 * N


def rms_stats_on_scalar(act, ps_row, sources, ss, rstd, squares, var_ready, root_ready):
    for j, t in enumerate(sources):
        if j:
            act.wait_ge(squares, j)
        act.activation(ps_row, t, ACT.Square, accum_out=ss[:, j:j + 1]).then_inc(squares, 1)
    act.wait_ge(var_ready, 1)
    act.activation(rstd, rstd, ACT.Sqrt).then_inc(root_ready, 1)


def rms_stats_on_vector(dve, step, count, ss, rstd, squares, var_ready, root_ready):
    dve.wait_ge(squares, count)
    dve.tensor_scalar(rstd, ss, 1.0 / D, EPS, ALU.mult, ALU.add).then_inc(var_ready, 1)
    dve.wait_ge(root_ready, 1)
    step(dve.reciprocal(rstd, rstd))


def top16(dve, step, values, scratch, best, index):
    step(dve.max(best[:, 0:8], values))
    step(dve.max_index(index[:, 0:8], best[:, 0:8], values))
    step(dve.match_replace(scratch, best[:, 0:8], values, -3.0e38))
    step(dve.max(best[:, 8:16], scratch))
    step(dve.max_index(index[:, 8:16], best[:, 8:16], scratch))


def phase_routing(nc, e):
    ring, ps, io, H, TOP = e.ring, e.ps, e.io, PEER_H, PEER_TOP
    with ExitStack() as ctx:
        sem = phase_semaphores(nc, ctx)
        sb = lambda name, shape, dt=F32: ctx.enter_context(nc.sbuf_tensor(name, shape, dt))
        scale2, shift2 = sb("scale2", [P, D]), sb("shift2", [P, D])
        g2 = sb("norm2_row", [P, D])
        ss, rstd = sb("ss2", [P, TB]), sb("rstd2", [P, TB])
        keys, keysT = sb("keys", [P, HP, P]), sb("keys_T", [P, HP, P])
        qT = sb("peer_q_T", [P, HP, T])
        scores = sb("key_scores", [P, TB, HP, PEER_K])
        left = sb("scores_left", [P, T])
        top, top_at = sb("key_top", [P, TB, HP, TOP]), sb("key_top_at", [P, TB, HP, TOP], U32)
        top_key = sb("key_top_number", [P, TB, HP, TOP])
        pairs = sb("pair_scores", [P, H, TOP * TOP])
        best, best_at = sb("pair_top", [P, TB, H, TOP]), sb("pair_top_at", [P, TB, H, TOP], U32)
        half = sb("pair_half", [P, 2, PICKS], U32)
        half_f = sb("pair_half_f", [P, 2, PICKS])
        hot = sb("pair_one_hot", [P, PICKS, TOP])
        key_of = sb("picked_key", [P, 2, PICKS])
        iota16 = sb("iota16", [P, TOP])
        total = sb("softmax_sum", [P, TB * H])
        rows_in, keys_in, iota_in = sem("rows2_in"), sem("keys_in"), sem("iota_in")
        squares, var_ready, root_ready = sem("squares2"), sem("var2_ready"), sem("root2_ready")
        h2_ready, turned, turned_out = sem("h2_ready"), sem("h2_turned"), sem("h2_turned_out")
        q_done, q_out, s_done, s_out = sem("q_done"), sem("q_out"), sem("s_done"), sem("s_out")
        shifted, exp_done = sem("softmax_shifted"), sem("softmax_exp")
        base, N = ring.turn, 2 * PEER_H * PEER_K // CG
        NB = CG // P
        FILLS = KB // 2 + HP // 4
        block = ctx.enter_context(nc.Block())

        @block.sync
        def _(sp):
            with sp.Fori(1, N) as n:
                load_tiles(sp, ring, turn_of(io["peer_query"][0], ds(n * CG, CG)), n + base)
            load_tiles(sp, ring, turn_of(io["w_mem_kv_2"][0], slice(0, CG)), base + N)

        @block.scalar
        def _(act):
            act.dma_start(shift2[:], e.mod_rows[0, D:2 * D].partition_broadcast(P)).then_inc(rows_in, 16)
            act.dma_start(scale2[:], e.mod_rows[0, 2 * D:3 * D].partition_broadcast(P)).then_inc(rows_in, 16)
            act.dma_start(g2[:], io["norm2_g"][0].partition_broadcast(P)).then_inc(rows_in, 16)
            act.dma_start(keys[:], io["peer_keys"][0].rearrange("h a k d -> k (h a) d")).then_inc(keys_in, 16)
            act.dma_start(iota16[:], io["k_iota16"]).then_inc(iota_in, 16)
            rms_stats_on_scalar(act, ps[:, 0:4].rearrange("p b n -> p (b n)"), [e.x[:, 0], e.x[:, 1]], ss, rstd[:], squares,
                                var_ready, root_ready)
            for f in range(FILLS):
                act.wait_ge(turned, f + 1)
                if f < HP // 4:
                    act.activation(keysT[:, 4 * f:4 * f + 4].rearrange("p a k -> p (a k)"), ps[:, 4 + f % 2], ACT.Copy).then_inc(turned_out, 1)
                else:
                    g = f - HP // 4
                    act.activation(e.hT[:, 2 * g:2 * g + 2].rearrange("p a t -> p (a t)"), ps[:, 4 + f % 2], ACT.Copy).then_inc(turned_out, 1)
            for tb in range(TB):
                for f in range(HP // 4):
                    n = tb * (HP // 4) + f
                    act.wait_ge(s_done, n + 1)
                    act.activation(scores[:, tb, 4 * f:4 * f + 4].rearrange("p a k -> p (a k)"), ps[:, 4 + n % 4], ACT.Copy).then_inc(s_out, 1)
            act.wait_ge(shifted, 1)
            act.activation(e.weight[:], e.weight[:], ACT.Exp).then_inc(exp_done, 1)

        @block.vector
        def _(dve):
            step = e.dve_step
            rms_stats_on_vector(dve, step, TB, ss[:], rstd[:], squares, var_ready, root_ready)
            dve.wait_ge(rows_in, 48)
            step(dve.scalar_tensor_tensor(scale2[:], scale2[:], 1.0, g2[:], ALU.add, ALU.mult))
            for tb in range(TB):
                step(dve.scalar_tensor_tensor(e.h2[:, tb], e.x[:, tb], rstd[:, tb:tb + 1], scale2[:], ALU.mult, ALU.mult))
                dve.tensor_tensor(e.h2[:, tb], e.h2[:, tb], shift2[:], ALU.add).then_inc(h2_ready, 1)
            dve.sem_inc(q_out, 1)
            with dve.Fori(0, N) as n:
                for nb in range(NB):
                    if nb < NB - 1:
                        dve.wait_ge(q_done, n * (NB - 1) + (nb + 1))
                    else:
                        dve.wait_ge(ring.used, n * SLOTS + used_after(SLOTS, base))
                    dve.tensor_scalar(qT[:, ds(n * NB + nb, 1)].rearrange("p a t -> p (a t)"), ps[:, nb, 0:T], 1.0, None, ALU.mult).then_inc(q_out, 1)
            for tb in range(TB):
                for hp in range(HP):
                    dve.wait_ge(s_out, tb * (HP // 4) + hp // 4 + 1)
                    top16(dve, step, scores[:, tb, hp], left[:, 0:PEER_K], top[:, tb, hp], top_at[:, tb, hp])
            step(dve.tensor_copy(top_key[:], top_at[:]))
            dve.wait_ge(iota_in, 16)
            for tb in range(TB):
                two = top[:, tb].rearrange("p (h a) k -> p h a k", a=2)
                wide = [P, H, TOP, TOP]
                step(dve.tensor_tensor(pairs[:].rearrange("p h (i j) -> p h i j", i=TOP), two[:, :, 0].unsqueeze(3).to_broadcast(wide),
                                       two[:, :, 1].unsqueeze(2).to_broadcast(wide), ALU.add))
                for h in range(H):
                    top16(dve, step, pairs[:, h], left[:], best[:, tb, h], best_at[:, tb, h])
                at = best_at[:, tb].rearrange("p h k -> p (h k)")
                step(dve.tensor_scalar(half[:, 0], at, 4, None, ALU.logical_shift_right))
                step(dve.tensor_scalar(half[:, 1], at, TOP - 1, None, ALU.bitwise_and))
                step(dve.tensor_copy(half_f[:], half[:]))
                numbers = top_key[:, tb].rearrange("p (h a) k -> p h a k", a=2)
                for a in range(2):
                    flat = [P, PICKS, TOP]
                    step(dve.tensor_tensor(hot[:], iota16[:].unsqueeze(1).to_broadcast(flat), half_f[:, a].unsqueeze(2).to_broadcast(flat),
                                           ALU.is_equal))
                    by_head = hot[:].rearrange("p (h s) k -> p h s k", h=H)
                    step(dve.tensor_tensor(by_head, by_head, numbers[:, :, a].unsqueeze(2).to_broadcast([P, H, TOP, TOP]), ALU.mult))
                    step(dve.tensor_reduce(key_of[:, a], hot[:], AX, ALU.add))
                step(dve.scalar_tensor_tensor(key_of[:, 0], key_of[:, 0], float(PEER_K), key_of[:, 1], ALU.mult, ALU.add))
                for rep in range(2):
                    step(dve.tensor_copy(e.expert[:, (rep * TB + tb) * PICKS:(rep * TB + tb + 1) * PICKS], key_of[:, 0]))
            step(dve.memset(e.expert[:, 2 * TB * PICKS:], 0))
            w = e.weight[:].rearrange("p (g k) -> p g k", k=TOP)
            g = best[:].rearrange("p b h k -> p (b h) k")
            n_groups = TB * H
            dve.tensor_tensor(w, g, g[:, :, 0:1].to_broadcast([P, n_groups, TOP]), ALU.subtract).then_inc(shifted, 1)
            dve.wait_ge(exp_done, 1)
            step(dve.tensor_reduce(total[:], w, AX, ALU.add))
            step(dve.reciprocal(total[:], total[:]))
            step(dve.tensor_tensor(w, w, total[:].unsqueeze(2).to_broadcast([P, n_groups, TOP]), ALU.mult))

        @block.tensor
        def _(pe):
            pe.wait_ge(keys_in, 16)
            for f in range(FILLS):
                if f >= 2:
                    pe.wait_ge(turned_out, f - 1)
                if f == HP // 4:
                    pe.wait_ge(h2_ready, TB)
                for a in range(4):
                    if f < HP // 4:
                        src = keys[:, 4 * f + a]
                    else:
                        src = e.h2[:, a % 2, (2 * (f - HP // 4) + a // 2) * P:][:, 0:P]
                    tr = pe.transpose(ps[:, 4 + f % 2, a * P:(a + 1) * P], src, e.ident[:])
                tr.then_inc(turned, 1)
            pe.wait_ge(turned_out, FILLS)
            with pe.Fori(0, N) as n:
                for nb in range(NB):
                    if nb == 0:
                        pe.wait_ge(q_out, n * NB + 1)
                    for s in range(SLOTS):
                        if nb == 0:
                            ring.arrived(pe, s, n + base)
                        for kk in range(TILE_K):
                            k = s * TILE_K + kk
                            mm = pe.matmul(ps[:, nb, 0:T], ring.tile[:, s, kk, nb * P:(nb + 1) * P], e.hT[:, k], start=(k == 0), stop=(k == KB - 1))
                        if nb == NB - 1:
                            mm.then_inc(ring.used, 1)
                    if nb < NB - 1:
                        mm.then_inc(q_done, 1)
            pe.wait_ge(q_out, N * NB + 1)
            for tb in range(TB):
                for hp in range(HP):
                    n = tb * (HP // 4) + hp // 4
                    if hp % 4 == 0 and n >= 4:
                        pe.wait_ge(s_out, n - 3)
                    mm = pe.matmul(ps[:, 4 + n % 4, (hp % 4) * P:(hp % 4 + 1) * P], qT[:, hp, tb * P:(tb + 1) * P], keysT[:, hp],
                                   start=True, stop=True)
                    if hp % 4 == 3:
                        mm.then_inc(s_done, 1)
    ring.turn += N


def phase_experts(nc, e):
    ring, ps, io = e.ring, e.ps, e.io
    with ExitStack() as ctx:
        sem = phase_semaphores(nc, ctx)
        sb = lambda name, shape, dt=F32: ctx.enter_context(nc.sbuf_tensor(name, shape, dt))
        GROUP, GROUPS = 4, 2
        RING = GROUP * GROUPS
        rows = sb("expert_rows", [P, RING, D])
        number = sb("expert_numbers", [P, GROUPS, GROUP], U32)
        dots = sb("expert_dots", [P, TB * PICKS])
        few = sb("expert_few", [P, RING])
        acc = sb("expert_sum", [P, TB, D])
        gt2, final_g = sb("gt2", [P, D]), sb("final_g_row", [P, D])
        ss, rstd = sb("ss3", [P, TB]), sb("rstd3", [P, TB])
        landed = [sem(f"expert_landed{s}") for s in range(RING)]
        number_ready, row_free, go, dots_ready, gelu_done = sem("number_ready"), sem("row_free"), sem("gather_go"), sem("dots_ready"), sem("gelu_done")
        rows_in, squares, var_ready, root_ready, x2_ready = sem("rows3_in"), sem("squares3"), sem("var3_ready"), sem("root3_ready"), sem("x2_ready")
        ROUNDS = PICKS // RING
        mem, mem_ss, mem_rstd = sb("mem_tokens", [P, TB, D]), sb("mem_ss", [P, TB]), sb("mem_rstd", [P, TB])
        memT, N_KV, base = e.hT, 2 * MEM_W // CG, ring.turn
        mem_in, mem_squares, mem_var, mem_root = sem("mem_in"), sem("mem_squares"), sem("mem_var"), sem("mem_root")
        mem_inverse, mem_normed, mem_turned, mem_turned_out = sem("mem_inverse"), sem("mem_normed"), sem("mem_turned"), sem("mem_turned_out")
        kv_tb_done, kv_out = sem("kv_tb_done"), sem("kv_out")
        block = ctx.enter_context(nc.Block())

        @block.sync
        def _(sp):
            for n in range(1, N_KV):
                load_tiles(sp, ring, turn_of(io["w_mem_kv_2"][0], slice(n * CG, (n + 1) * CG)), base + n)
            load_tiles(sp, ring, turn_of(io["w_in_2"][0], slice(0, CG)), base + N_KV)

        @block.tensor
        def _(pe):
            pe.wait_ge(mem_normed, TB)
            for k in range(KB):
                if k >= 2:
                    pe.wait_ge(mem_turned_out, k - 1)
                for tb in range(TB):
                    tr = pe.transpose(ps[:, 4 + k % 2, tb * P:(tb + 1) * P], mem[:, tb, k * P:(k + 1) * P], e.ident[:])
                tr.then_inc(mem_turned, 1)
            pe.wait_ge(mem_turned_out, KB)
            for n in range(N_KV):
                gemm_token_major(pe, ring, pieces_of(0, SLOTS, base + n), lambda k, tb: memT[:, k, tb * P:(tb + 1) * P],
                                 [ps[:, 2 * n], ps[:, 2 * n + 1]], lambda tb: None, kv_tb_done)

        @block.gpsimd
        def _(pool):
            for table, src in enumerate((io["peer_down"][0], io["peer_up"][0])):
                first = table * TB * ROUNDS
                with pool.Fori(0, TB * ROUNDS) as i:
                    for p in range(GROUPS):
                        pool.wait_ge(number_ready, i * GROUPS + (first * GROUPS + p + 1))
                        for j in range(GROUP):
                            s = p * GROUP + j
                            pool.wait_ge(row_free, i * RING + (first * RING + s + 1))
                            pool.sem_inc(go, 1)
                            pool.indirect_dma_start(rows[:, s], None, src, bass.IndirectOffsetOnAxis(ap=number[:, p, j:j + 1], axis=0)).then_inc(landed[s], 16)

        @block.vector
        def _(dve):
            step = e.dve_step
            step(dve.memset(acc[:].rearrange("p b d -> p (b d)"), 0.0))
            for p in range(GROUPS):
                dve.tensor_copy(number[:, p], e.expert[:, p * GROUP:(p + 1) * GROUP]).then_inc(number_ready, 1)
            dve.sem_inc(row_free, RING)

            def next_numbers(i, p, first):
                dve.tensor_scalar(number[:, p], e.expert[:, ds((i + (first + 1)) * RING + p * GROUP, GROUP)], 0, None,
                                  ALU.bitwise_or).then_inc(number_ready, 1)

            for tb in range(TB):
                first = tb * ROUNDS
                with dve.Fori(0, ROUNDS) as i:
                    for p in range(GROUPS):
                        for j in range(GROUP):
                            s = p * GROUP + j
                            dve.wait_ge(landed[s], (i + (first + 1)) * 16)
                            dve.tensor_tensor_reduce(rows[:, s], rows[:, s], e.h2[:, tb], 1.0, 0.0, ALU.mult, ALU.add,
                                                     few[:, s:s + 1]).then_inc(row_free, 1)
                        next_numbers(i, p, first)
                    dve.wait_ge(row_free, (i + (first + 2)) * RING)
                    dve.tensor_scalar(dots[:, ds((i + first) * RING, RING)], few[:], 1.0, None, ALU.mult).then_inc(dots_ready, 1)
                    dve.wait_ge(dots_ready, i + (first + 1))
                if tb == 0:
                    dve.wait_ge(mem_squares, TB)
                    dve.tensor_scalar(mem_rstd[:], mem_ss[:], 1.0 / D, EPS, ALU.mult, ALU.add).then_inc(mem_var, 1)
                    dve.wait_ge(mem_root, 1)
                    dve.reciprocal(mem_rstd[:], mem_rstd[:]).then_inc(mem_inverse, 1)
            dve.wait_ge(gelu_done, 1)
            step(dve.tensor_tensor(dots[:], dots[:], e.weight[:], ALU.mult))
            for tb in range(TB):
                first = (TB + tb) * ROUNDS
                with dve.Fori(0, ROUNDS) as i:
                    step.enter(i, 1)
                    step(dve.tensor_scalar(few[:], dots[:, ds((i + tb * ROUNDS) * RING, RING)], 1.0, None, ALU.mult))
                    for p in range(GROUPS):
                        for j in range(GROUP):
                            s = p * GROUP + j
                            dve.wait_ge(landed[s], (i + (first + 1)) * 16)
                            dve.scalar_tensor_tensor(acc[:, tb], rows[:, s], few[:, s:s + 1], acc[:, tb], ALU.mult, ALU.add).then_inc(row_free, 1)
                            dve.wait_ge(row_free, i * RING + ((first + 1) * RING + s + 1))
                        next_numbers(i, p, first)
                step.leave(ROUNDS)
            dve.wait_ge(rows_in, 32)
            for tb in range(TB):
                step(dve.tensor_tensor(acc[:, tb], acc[:, tb], gt2[:], ALU.mult))
                dve.tensor_tensor(e.x[:, tb], e.x[:, tb], acc[:, tb], ALU.add).then_inc(x2_ready, 1)
            rms_stats_on_vector(dve, step, TB, ss[:], rstd[:], squares, var_ready, root_ready)
            for tb in range(TB):
                step(dve.scalar_tensor_tensor(e.x[:, tb], e.x[:, tb], rstd[:, tb:tb + 1], final_g[:], ALU.mult, ALU.mult))

        @block.scalar
        def _(act):
            act.dma_start(gt2[:], e.mod_rows[0, 3 * D:4 * D].partition_broadcast(P)).then_inc(rows_in, 16)
            act.dma_start(final_g[:], io["final_g"].partition_broadcast(P)).then_inc(rows_in, 16)
            act.dma_start(mem[:], tokens_of(io["mem_2"][0])).then_inc(mem_in, 16)
            act.wait_ge(mem_in, 16)
            rms_stats_on_scalar(act, ps[:, 0:4].rearrange("p b n -> p (b n)"), [mem[:, 0], mem[:, 1]], mem_ss, mem_rstd[:],
                                mem_squares, mem_var, mem_root)
            act.wait_ge(mem_inverse, 1)
            for tb in range(TB):
                act.activation(mem[:, tb], mem[:, tb], ACT.Copy, scale=mem_rstd[:, tb:tb + 1]).then_inc(mem_normed, 1)
            for k in range(KB):
                act.wait_ge(mem_turned, k + 1)
                act.activation(memT[:, k], ps[:, 4 + k % 2, 0:T], ACT.Copy, scale=e.cols_b[:, 72 + k:73 + k]).then_inc(mem_turned_out, 1)
            for n in range(N_KV):
                for tb in range(TB):
                    if tb == 0:
                        act.wait_ge(kv_tb_done, n + 1)
                    else:
                        act.wait_ge(ring.used, used_after((n + 1) * SLOTS, base))
                    act.activation(e.kv[:, tb, n * CG:(n + 1) * CG], ps[:, 2 * n + tb], ACT.Copy).then_inc(kv_out, 1)
            act.wait_ge(dots_ready, TB * ROUNDS)
            act.activation(dots[:], dots[:], ACT.Gelu).then_inc(gelu_done, 1)
            act.wait_ge(kv_out, N_KV * TB)
            act.wait_ge(x2_ready, TB)
            rms_stats_on_scalar(act, ps[:, 0:4].rearrange("p b n -> p (b n)"), [e.x[:, 0], e.x[:, 1]], ss, rstd[:], squares,
                                var_ready, root_ready)
    ring.turn += N_KV


def phase_second_projection(nc, e):
    ring, ps, io = e.ring, e.ps, e.io
    with ExitStack() as ctx:
        sem = phase_semaphores(nc, ctx)
        sb = lambda name, shape: ctx.enter_context(nc.sbuf_tensor(name, shape, F32))
        split = WeightSplit(nc, ctx, sem, "in2_weights")
        xn = e.p2[:, :, 0:D]
        w_lr = sb("w_lr", [P, KB, 16])
        hT = sb("lr_h_T", [P, 2, T])
        ss, rstd = sb("ss4", [P, TB]), sb("rstd4", [P, TB])
        lr_in, squares, var_ready, root_ready, x_kept = sem("lr_in"), sem("squares4"), sem("var4_ready"), sem("root4_ready"), sem("x_kept")
        normed, turned, lo_out, h_out = sem("normed"), sem("in2_turned"), sem("in2_lo_out"), sem("in2_h_out")
        tb_done, bank_free, lr_done, lr_used = sem("in2_tb_done"), sem("in2_bank_free"), sem("lr_done"), sem("lr_used")
        base = ring.turn
        w_in = io["w_in_2"][0]
        runs = ((0, C_LR // CG), (MEMQ, (G_LOGIT - MEMQ) // CG))
        n_turns = sum(n for _, n in runs)
        block = ctx.enter_context(nc.Block())

        @block.sync
        def _(sp):
            sp.dma_start(e.x_rows, e.x[:]).then_inc(x_kept, 16)
            turn = base
            for first, n in runs:
                with sp.Fori(1 if turn == base else 0, n) as i:
                    load_tiles(sp, ring, turn_of(w_in[:, first:first + n * CG], ds(i * CG, CG)), i + turn)
                turn += n
            load_tiles(sp, ring, turn_of(w_in, slice(G_LOGIT, G_LOGIT + CG)), turn)
            sp.wait_ge(x_kept, 16)

        @block.gpsimd
        def _(pool):
            pool.dma_start(w_lr[:], w_in[:, C_LR:MEMQ].rearrange("(k p) n -> p k n", p=P)).then_inc(lr_in, 16)
            turn = base
            for _, n in runs:
                with pool.Fori(0, n) as i:
                    for s in range(SLOTS):
                        split.write_lo(pool, ring, (s, i + turn), i * SLOTS + ((turn - base) * SLOTS + s))
                turn += n

        @block.scalar
        def _(act):
            rms_stats_on_scalar(act, ps[:, 0:4].rearrange("p b n -> p (b n)"), [e.x[:, 0], e.x[:, 1]], ss, rstd[:], squares, var_ready, root_ready)
            for k in range(KB):
                act.wait_ge(turned, k + 1)
                gain = e.cols_b[:, 56 + k:57 + k]
                act.activation(e.hT_hi[:, k], ps[:, 4 + k % 2, 0:T], ACT.Copy, scale=gain)
                if k >= 2:
                    act.wait_ge(lr_used, k - 1)
                act.activation(hT[:, k % 2], ps[:, 4 + k % 2, 0:T], ACT.Copy, scale=gain).then_inc(h_out, 1)
            turn = base
            for _, n in runs:
                with act.Fori(0, n) as i:
                    for s in range(SLOTS):
                        split.write_hi(act, ring, (s, i + turn), i * SLOTS + ((turn - base) * SLOTS + s))
                turn += n

        @block.vector
        def _(dve):
            step = e.dve_step
            dve.sem_inc(bank_free, TB)
            rms_stats_on_vector(dve, step, TB, ss[:], rstd[:], squares, var_ready, root_ready)
            for tb in range(TB):
                dve.tensor_scalar(xn[:, tb], e.x[:, tb], rstd[:, tb:tb + 1], None, ALU.mult).then_inc(normed, 1)
            dve.wait_ge(normed, TB)
            dve.wait_ge(x_kept, 16)
            for k in range(KB):
                dve.wait_ge(h_out, k + 1)
                dve.scalar_tensor_tensor(e.hT_lo[:, k], ps[:, 4 + k % 2, 0:T], e.cols_b[:, 56 + k:57 + k], e.hT_hi[:, k],
                                         ALU.mult, ALU.subtract).then_inc(lo_out, 1)
            dve.wait_ge(lr_done, 1)
            step(dve.tensor_copy(e.lrT[:], ps[0:16, 2, 0:T]))
            turn, done = base, 0
            for first, n in runs:
                with dve.Fori(0, n) as i:
                    for tb in range(TB):
                        if tb == 0:
                            dve.wait_ge(tb_done, i + (done + 1))
                        else:
                            dve.wait_ge(split.free, i * (2 * SLOTS) + split.free_after((done + 1) * SLOTS))
                        dve.tensor_scalar(e.p2[:, tb, ds(i * CG + first, CG)], ps[:, tb], 1.0, None, ALU.mult).then_inc(bank_free, 1)
                done += n

        @block.tensor
        def _(pe):
            pe.sem_inc(split.free, split.free_after(0))
            pe.wait_ge(normed, TB)
            pe.wait_ge(lr_in, 16)

            def low_rank(k):
                pe.wait_ge(h_out, k + 1)
                return pe.matmul(ps[0:16, 2, 0:T], w_lr[:, k], hT[:, k % 2], start=(k == 0), stop=(k == KB - 1))

            for k in range(KB):
                if k >= 2:
                    pe.wait_ge(h_out, k - 1)
                    pe.wait_ge(lo_out, k - 1)
                for tb in range(TB):
                    tr = pe.transpose(ps[:, 4 + k % 2, tb * P:(tb + 1) * P], xn[:, tb, k * P:(k + 1) * P], e.ident[:])
                tr.then_inc(turned, 1)
                if k >= 1:
                    low_rank(k - 1).then_inc(lr_used, 1)
            low_rank(KB - 1).then_inc(lr_done, 1)
            pe.wait_ge(lo_out, KB)
            turn, uses = base, 0
            for _, n in runs:
                with pe.Fori(0, n) as i:
                    gemm_split(pe, ring, split, pieces_of(0, SLOTS, i + turn), i * SLOTS + (turn - base) * SLOTS, e.h_split, [ps[:, 0], ps[:, 1]],
                               lambda tb: pe.wait_ge(bank_free, i * TB + (uses + tb + 1)), tb_done)
                turn, uses = turn + n, uses + n * TB
    ring.turn += n_turns


def phase_pool(nc, e):
    ps, io, p2 = e.ps, e.io, e.p2
    with ExitStack() as ctx:
        sem = phase_semaphores(nc, ctx)
        sb = lambda name, shape: ctx.enter_context(nc.sbuf_tensor(name, shape, F32))
        G, W = len(POOL_WINDOWS), 2 * P
        windows, w_pool = sb("windows", [P, TB, G * T]), sb("w_pool", [P, 2 * G, W])
        scale = sb("pool_scale_row", [P, G * W])
        pooledT = sb("pooled_T", [P, 2 * G, T])
        mixed = sb("pool_mixed", [P, TB, G * W])
        tables, pooled, pooled_out, mix_done, gate_ready = sem("pool_tables"), sem("pooled"), sem("pooled_out"), sem("mix_done"), sem("pool_gate")
        gate = p2[:, :, A_GATE:A_GATE + G * W]
        block = ctx.enter_context(nc.Block())

        @block.scalar
        def _(act):
            act.dma_start(windows[:], io["k_pool"]).then_inc(tables, 16)
            act.dma_start(w_pool[:], io["w_pool_2"][0].rearrange("g (b c) d -> c (g b) d", c=P)).then_inc(tables, 16)
            act.dma_start(scale[:], io["pool_scale_2"][0].partition_broadcast(P)).then_inc(tables, 16)
            act.activation(gate, gate, ACT.Silu).then_inc(gate_ready, 1)
            for g in range(G):
                act.wait_ge(pooled, g + 1)
                act.activation(pooledT[:, 2 * g:2 * g + 2].rearrange("p a t -> p (a t)"), ps[:, g], ACT.Copy).then_inc(pooled_out, 1)

        @block.tensor
        def _(pe):
            pe.wait_ge(tables, 48)
            for g in range(G):
                for cb in range(2):
                    at = A_VAL + (2 * g + cb) * P
                    for tb in range(TB):
                        mm = pe.matmul(ps[:, g, cb * T:(cb + 1) * T], p2[:, tb, at:at + P], windows[:, tb, g * T:(g + 1) * T],
                                       start=(tb == 0), stop=(tb == TB - 1))
                mm.then_inc(pooled, 1)
            pe.wait_ge(pooled_out, G)
            for tb in range(TB):
                for g in range(G):
                    for cb in range(2):
                        mm = pe.matmul(ps[:, 4 + 2 * tb + g // 2, (g % 2) * W:(g % 2 + 1) * W], pooledT[:, 2 * g + cb, tb * P:(tb + 1) * P],
                                       w_pool[:, 2 * g + cb], start=(cb == 0), stop=(cb == 1))
                mm.then_inc(mix_done, 1)

        @block.vector
        def _(dve):
            step = e.dve_step
            dve.wait_ge(tables, 48)
            dve.wait_ge(gate_ready, 1)
            for tb in range(TB):
                dve.wait_ge(mix_done, tb + 1)
                step(dve.tensor_tensor(mixed[:, tb], ps[:, 4 + 2 * tb:6 + 2 * tb].rearrange("p b n -> p (b n)"), scale[:], ALU.mult))
                step(dve.tensor_tensor(gate[:, tb], gate[:, tb], mixed[:, tb], ALU.mult))


def phase_attention(nc, e):
    ps, io, p2 = e.ps, e.io, e.p2
    with ExitStack() as ctx:
        sem = phase_semaphores(nc, ctx)
        sb = lambda name, shape: ctx.enter_context(nc.sbuf_tensor(name, shape, F32))
        NG, PER, NM = len(SWA_CFG), 4, 4
        NSWA = NG * PER
        NH = NSWA + NM
        dist = sb("dist", [P, TB, NG * T])
        bias = sb("att_bias", [P, 2, TB, T])
        qk = sb("att_qk_T", [P, 2, 2 * T])
        sc, ex, exT = sb("att_scores", [P, 2, TB, T]), sb("att_exp", [P, 2, TB, T]), sb("att_exp_T", [P, 2, TB, T])
        top, neg = sb("att_max", [P, NH, TB]), sb("att_neg_max", [P, NH, TB])
        den = sb("att_den", [P, NH, TB])
        o = sb("att_out", [P, TB, NH, P])
        lse, mx, wt, tot = sb("lse", [P, NSWA, TB]), sb("lse_max", [P, PER, TB]), sb("lse_weight", [P, NSWA, TB]), sb("lse_sum", [P, PER, TB])
        tables, bias_ready, qk_done, qk_out, s_done, sc_ready = sem("dist_in"), sem("bias_ready"), sem("qk_turned"), sem("qk_out"), sem("att_s_done"), sem("sc_ready")
        neg_ready, exp_ready, ex_turned, ex_out, o_done, o_out = sem("neg_ready"), sem("att_exp_ready"), sem("ex_turned"), sem("ex_out"), sem("att_o_done"), sem("att_o_out")
        ln_done, shifted, wt_exp, gates_ready = sem("lse_ln"), sem("lse_shifted"), sem("lse_exp"), sem("att_gates")
        SCALE = float(P) ** -0.5
        slope = [2.0 ** (-8.0 * (h + 1.0) / NSWA) for h in range(NSWA)]
        s_gate, m_gate = p2[:, :, S_GATE:S_GATE + PER * P], p2[:, :, MEM_GATE:MEM_GATE + NM * P]
        q_at = lambda n: (SQ + n * P) if n < NSWA else MEMQ + (n - NSWA) * P
        key = lambda n, b: p2[:, b, SK + n * P:SK + (n + 1) * P] if n < NSWA else e.kv[:, b, (n - NSWA) * P:(n - NSWA + 1) * P]
        value = lambda n, b: p2[:, b, SV + n * P:SV + (n + 1) * P] if n < NSWA else e.kv[:, b, 512 + (n - NSWA) * P:512 + (n - NSWA + 1) * P]
        block = ctx.enter_context(nc.Block())

        @block.gpsimd
        def _(pool):
            pool.wait_ge(tables, 16)
            for n in range(NSWA):
                if n >= 2:
                    pool.wait_ge(sc_ready, n - 1)
                pool.tensor_scalar(bias[:, n % 2], dist[:, :, (n // PER) * T:(n // PER + 1) * T], -slope[n], None, ALU.mult).then_inc(bias_ready, 1)

        @block.scalar
        def _(act):
            act.dma_start(dist[:], io["k_dist"]).then_inc(tables, 16)
            act.activation(s_gate, s_gate, ACT.Silu).then_inc(gates_ready, 1)
            act.activation(m_gate, m_gate, ACT.Silu).then_inc(gates_ready, 1)

            def copy_qk(n):
                act.wait_ge(qk_done, n + 1)
                if n >= 2:
                    act.wait_ge(s_done, n - 1)
                act.activation(qk[:, n % 2], ps[:, n % 2], ACT.Copy).then_inc(qk_out, 1)

            copy_qk(0)
            for n in range(NH):
                if n + 1 < NH:
                    copy_qk(n + 1)
                act.wait_ge(neg_ready, n + 1)
                if n >= 2:
                    act.wait_ge(ex_turned, n - 1)
                for tb in range(TB):
                    act.activation(ex[:, n % 2, tb], sc[:, n % 2, tb], ACT.Exp, bias=neg[:, n, tb:tb + 1],
                                   accum_out=den[:, n, tb:tb + 1]).then_inc(exp_ready, 1)
                act.wait_ge(ex_turned, n + 1)
                if n >= 2:
                    act.wait_ge(o_done, n - 1)
                act.activation(exT[:, n % 2].rearrange("p s t -> p (s t)"), ps[:, 4 + n % 2], ACT.Copy).then_inc(ex_out, 1)
                act.wait_ge(o_done, n + 1)
                act.activation(o[:, :, n], ps[:, 6 + n % 2, 0:T].rearrange("p (b c) -> p b c", b=TB), ACT.Copy).then_inc(o_out, 1)
            act.wait_ge(o_out, NH)
            act.activation(lse[:], den[:, 0:NSWA], ACT.Ln).then_inc(ln_done, 1)
            act.wait_ge(shifted, 1)
            act.activation(wt[:], wt[:], ACT.Exp).then_inc(wt_exp, 1)

        @block.vector
        def _(dve):
            step = e.dve_step
            for n in range(NH):
                dve.wait_ge(s_done, n + 1)
                if n >= 2:
                    dve.wait_ge(exp_ready, 2 * (n - 1))
                flat = sc[:, n % 2].rearrange("p b s -> p (b s)")
                if n < NSWA:
                    dve.wait_ge(bias_ready, n + 1)
                    x = dve.scalar_tensor_tensor(flat, ps[:, 2 + n % 2], SCALE, bias[:, n % 2].rearrange("p b s -> p (b s)"), ALU.mult, ALU.add)
                else:
                    x = dve.tensor_scalar(flat, ps[:, 2 + n % 2], SCALE, None, ALU.mult)
                x.then_inc(sc_ready, 1)
                dve.wait_ge(sc_ready, n + 1)
                step(dve.tensor_reduce(top[:, n], sc[:, n % 2], AX, ALU.max))
                dve.tensor_scalar(neg[:, n], top[:, n], -1.0, None, ALU.mult).then_inc(neg_ready, 1)
            dve.wait_ge(ln_done, 1)
            grouped = lambda t: t[:].rearrange("p (g h) b -> p g h b", g=NG)
            step(dve.tensor_tensor(lse[:], lse[:], top[:, 0:NSWA], ALU.add))
            step(dve.tensor_tensor(mx[:], grouped(lse)[:, 0], grouped(lse)[:, 1], ALU.max))
            step(dve.tensor_tensor(mx[:], mx[:], grouped(lse)[:, 2], ALU.max))
            for g in range(NG):
                x = dve.tensor_tensor(grouped(wt)[:, g], grouped(lse)[:, g], mx[:], ALU.subtract)
                if g < NG - 1:
                    step(x)
            x.then_inc(shifted, 1)
            dve.wait_ge(wt_exp, 1)
            step(dve.tensor_tensor(tot[:], grouped(wt)[:, 0], grouped(wt)[:, 1], ALU.add))
            step(dve.tensor_tensor(tot[:], tot[:], grouped(wt)[:, 2], ALU.add))
            step(dve.reciprocal(tot[:], tot[:]))
            step(dve.reciprocal(den[:], den[:]))
            for g in range(NG):
                step(dve.tensor_tensor(grouped(wt)[:, g], grouped(wt)[:, g], tot[:], ALU.mult))
            step(dve.tensor_tensor(den[:, 0:NSWA], den[:, 0:NSWA], wt[:], ALU.mult))
            dve.wait_ge(gates_ready, 2)
            for tb in range(TB):
                step(dve.tensor_tensor(o[:, tb], o[:, tb], den[:, :, tb:tb + 1].to_broadcast([P, NH, P]), ALU.mult))
                for g in range(1, NG):
                    step(dve.tensor_tensor(o[:, tb, 0:PER], o[:, tb, 0:PER], o[:, tb, g * PER:(g + 1) * PER], ALU.add))
                step(dve.tensor_tensor(s_gate[:, tb], s_gate[:, tb], o[:, tb, 0:PER].rearrange("p h c -> p (h c)"), ALU.mult))
                step(dve.tensor_tensor(m_gate[:, tb], m_gate[:, tb], o[:, tb, NSWA:NH].rearrange("p h c -> p (h c)"), ALU.mult))

        @block.tensor
        def _(pe):
            def turn_qk(n):
                if n >= 2:
                    pe.wait_ge(qk_out, n - 1)
                for b in range(TB):
                    pe.transpose(ps[:, n % 2, b * P:(b + 1) * P], p2[:, b, q_at(n):q_at(n) + P], e.ident[:])
                for b in range(TB):
                    tr = pe.transpose(ps[:, n % 2, T + b * P:T + (b + 1) * P], key(n, b), e.ident[:])
                tr.then_inc(qk_done, 1)

            def scores(n):
                pe.wait_ge(qk_out, n + 1)
                if n >= 2:
                    pe.wait_ge(sc_ready, n - 1)
                for tb in range(TB):
                    mm = pe.matmul(ps[:, 2 + n % 2, tb * T:(tb + 1) * T], qk[:, n % 2, tb * P:(tb + 1) * P], qk[:, n % 2, T:2 * T], start=True, stop=True)
                mm.then_inc(s_done, 1)

            turn_qk(0)
            turn_qk(1)
            scores(0)
            for n in range(NH):
                if n + 2 < NH:
                    turn_qk(n + 2)
                if n + 1 < NH:
                    scores(n + 1)
                pe.wait_ge(exp_ready, 2 * (n + 1))
                if n >= 2:
                    pe.wait_ge(ex_out, n - 1)
                for b in range(TB):
                    for tb in range(TB):
                        tr = pe.transpose(ps[:, 4 + n % 2, b * T + tb * P:b * T + (tb + 1) * P], ex[:, n % 2, tb, b * P:(b + 1) * P], e.ident[:])
                tr.then_inc(ex_turned, 1)
                pe.wait_ge(ex_out, n + 1)
                if n >= 2:
                    pe.wait_ge(o_out, n - 1)
                for tb in range(TB):
                    keys = range(tb + 1) if n < NSWA else range(TB)
                    for i, b in enumerate(keys):
                        mm = pe.matmul(ps[:, 6 + n % 2, tb * P:(tb + 1) * P], exT[:, n % 2, b, tb * P:(tb + 1) * P], value(n, b),
                                       start=(i == 0), stop=(i == len(keys) - 1))
                mm.then_inc(o_done, 1)


def phase_gla(nc, e):
    ps, io, p2 = e.ps, e.io, e.p2
    with ExitStack() as ctx:
        sem = phase_semaphores(nc, ctx)
        sb = lambda name, shape: ctx.enter_context(nc.sbuf_tensor(name, shape, F32))
        H, DV, C = 4, 256, 64
        NC = T // C
        TAU = 16.0
        w_alpha = sb("w_alpha", [16, H * P])
        seg, clip = sb("chunk_starts", [P, H * T]), sb("chunk_clip", [P, 2, P])
        gain = sb("g_gla_row", [P, H * DV])
        z, u, w, ls = (sb(f"ls_gla_{n}", [P, H, T]) for n in "zuwl")
        grow, shrink, rest = u, w, z
        b = sb("gla_sums", [P, H, T])
        qt, kt, kd = sb("gla_q", [P, H, T]), sb("gla_k", [P, H, T]), sb("gla_k_rest", [P, H, T])
        aT = sb("gla_att", [P, 2, P])
        qpad = [p2[:, h // 2, A_VAL:A_GATE].rearrange("p (h c n) -> p h c n", c=NC, n=P)[:, h % 2] for h in range(H)]
        at = SQ + H * (NC - 1) * DV
        state = p2[:, 0, SQ:at].rearrange("p (h c e) -> p h c e", c=NC - 1, e=DV)
        kd_tok = p2[:, 0, at:at + TB * H * P].rearrange("p (b h n) -> p b h n", b=TB, n=P)
        o, sq = (p2[:, 1, SQ + i * TB * H * DV:SQ + (i + 1) * TB * H * DV].rearrange("p (n e) -> p n e", e=DV) for i in range(2))
        stat = sb("gla_stat", [P, TB * H])
        tables, z_done, b_ready, exps, pad_ready = sem("gla_tables"), sem("z_done"), sem("b_ready"), sem("gla_exps"), sem("pad_zero")
        rest_ready, qk_turned, qk_ready, pad_done = sem("rest_ready"), sem("gla_turned"), sem("gla_qk_ready"), sem("pad_done")
        kd_turned, kd_out, kv_done, state_ready = sem("kd_turned"), sem("kd_out"), sem("kv_done"), sem("state_ready")
        a_done, a_ready, o_done, o_out = sem("a_done"), sem("a_ready"), sem("gla_o_done"), sem("gla_o_out")
        sq_ready, var_ready, root_ready, gate_ready = sem("gla_sq"), sem("gla_var"), sem("gla_root"), sem("gla_gate")
        use = e.ls_uses + 1
        gate = p2[:, :, C_GATE:C_GATE + H * DV]
        chunks = lambda t: t[:].rearrange("p h (c n) -> p (h c) n", n=C)
        flat = lambda t: t[:].rearrange("p h t -> p (h t)")
        block = ctx.enter_context(nc.Block())

        @block.scalar
        def _(act):
            act.dma_start(w_alpha[:], io["w_alpha_2"][0]).then_inc(tables, 16)
            act.dma_start(seg[:], io["k_seg"]).then_inc(tables, 16)
            act.dma_start(clip[:], io["k_chunk"]).then_inc(tables, 16)
            act.dma_start(gain[:], io["g_gla_2"][0].partition_broadcast(P)).then_inc(tables, 16)
            log_sigmoid_on_scalar(act, e, use, u[:], w[:], ls[:])
            act.wait_ge(b_ready, 1)
            act.activation(shrink[:], b[:], ACT.Exp, scale=1.0 / TAU).then_inc(exps, 1)
            act.activation(grow[:], b[:], ACT.Exp, scale=-1.0 / TAU).then_inc(exps, 1)
            act.wait_ge(rest_ready, 1)
            act.activation(rest[:], rest[:], ACT.Exp, scale=1.0 / TAU).then_inc(exps, 1)
            for f in range(2):
                act.wait_ge(kd_turned, f + 1)
                act.activation(kd_tok[:, f].rearrange("p h d -> p (h d)"), ps[:, 4 + f], ACT.Copy).then_inc(kd_out, 1)
            for n in range(TB * H):
                act.wait_ge(o_done, n + 1)
                act.activation(o[:, n], ps[:, 6 + n % 2, 0:DV], ACT.Copy).then_inc(o_out, 1)
            act.wait_ge(o_out, TB * H)
            act.activation(sq, o, ACT.Square).then_inc(sq_ready, 1)
            act.wait_ge(var_ready, 1)
            act.activation(stat[:], stat[:], ACT.Sqrt).then_inc(root_ready, 1)
            act.activation(gate, gate, ACT.Silu).then_inc(gate_ready, 1)

        @block.gpsimd
        def _(pool):
            pool.memset(p2[:, :, A_VAL:A_GATE], 0.0).then_inc(pad_ready, 1)
            pool.wait_ge(pad_ready, 1)
            for h in range(H):
                pool.wait_ge(qk_ready, 3 * h + 1)
                for r in range(2):
                    pool.tensor_copy(qpad[h][:, r::2, r * C:(r + 1) * C], qt[:, h].rearrange("p (b r n) -> p r b n", r=2, n=C)[:, r]).then_inc(pad_done, 1)

        @block.vector
        def _(dve):
            step = e.dve_step
            dve.wait_ge(z_done, 1)
            for h in range(H):
                step(dve.tensor_scalar(z[:, h], ps[:, h // 2, (h % 2) * T:(h % 2 + 1) * T], e.cols_b[:, 88 + h:89 + h], None, ALU.add))
            log_sigmoid_on_vector(dve, step, e, z[:], u[:], w[:], ls[:])
            dve.wait_ge(tables, 64)
            dve.tensor_tensor_scan(flat(b), seg[:], flat(ls), 0.0, ALU.mult, ALU.add).then_inc(b_ready, 1)
            dve.wait_ge(b_ready, 1)
            last = chunks(b)[:, :, C - 1:C].to_broadcast([P, H * NC, C])
            dve.tensor_tensor(chunks(rest), last, chunks(b), ALU.subtract).then_inc(rest_ready, 1)
            dve.wait_ge(exps, 3)
            for h in range(H):
                dve.wait_ge(qk_turned, h + 1)
                q, k = ps[:, h, 0:T], ps[:, h, T:2 * T]
                dve.scalar_tensor_tensor(qt[:, h], q, float(P) ** -0.5, shrink[:, h], ALU.mult, ALU.mult).then_inc(qk_ready, 1)
                dve.tensor_tensor(kt[:, h], k, grow[:, h], ALU.mult).then_inc(qk_ready, 1)
                dve.tensor_tensor(kd[:, h], k, rest[:, h], ALU.mult).then_inc(qk_ready, 1)
            for h in range(H):
                for c in range(NC - 1):
                    n = h * (NC - 1) + c
                    dve.wait_ge(kv_done, n + 1)
                    kv, s = ps[:, 2 + n % 2, 0:DV], state[:, h, c]
                    if c == 0:
                        x = dve.tensor_copy(s, kv)
                    else:
                        at = c * C + C - 1
                        x = dve.scalar_tensor_tensor(s, state[:, h, c - 1], shrink[:, h, at:at + 1], kv, ALU.mult, ALU.add)
                    x.then_inc(state_ready, 1)
                    dve.wait_ge(state_ready, n + 1)
            for n in range(TB * H):
                dve.wait_ge(a_done, n + 1)
                if n >= 2:
                    dve.wait_ge(o_done, n - 1)
                step(dve.tensor_tensor(aT[:, n % 2], ps[:, 4 + n % 2, 0:P], clip[:, 0], ALU.min))
                dve.tensor_tensor(aT[:, n % 2], aT[:, n % 2], clip[:, 1], ALU.max).then_inc(a_ready, 1)
            dve.wait_ge(sq_ready, 1)
            step(dve.tensor_reduce(stat[:], sq, AX, ALU.add))
            dve.tensor_scalar(stat[:], stat[:], 1.0 / DV, EPS, ALU.mult, ALU.add).then_inc(var_ready, 1)
            dve.wait_ge(root_ready, 1)
            step(dve.reciprocal(stat[:], stat[:]))
            step(dve.tensor_tensor(o, o, stat[:].unsqueeze(2).to_broadcast([P, TB * H, DV]), ALU.mult))
            dve.wait_ge(gate_ready, 1)
            for tb in range(TB):
                flat_o = o[:, tb * H:(tb + 1) * H].rearrange("p h e -> p (h e)")
                step(dve.tensor_tensor(flat_o, flat_o, gain[:], ALU.mult))
                step(dve.tensor_tensor(gate[:, tb], gate[:, tb], flat_o, ALU.mult))

        @block.tensor
        def _(pe):
            pe.wait_ge(tables, 64)
            for h in range(H):
                mm = pe.matmul(ps[:, h // 2, (h % 2) * T:(h % 2 + 1) * T], w_alpha[:, h * P:(h + 1) * P], e.lrT[:], start=True, stop=True)
            mm.then_inc(z_done, 1)
            pe.wait_ge(b_ready, 1)
            for h in range(H):
                for a, first in enumerate((CQ, CK)):
                    for tb in range(TB):
                        at = first + h * P
                        tr = pe.transpose(ps[:, h, a * T + tb * P:a * T + (tb + 1) * P], p2[:, tb, at:at + P], e.ident[:])
                tr.then_inc(qk_turned, 1)
            pe.wait_ge(qk_ready, 3 * H)
            for tb in range(TB):
                for h in range(H):
                    tr = pe.transpose(ps[:, 4 + tb, h * P:(h + 1) * P], kd[:, h, tb * P:(tb + 1) * P], e.ident[:])
                tr.then_inc(kd_turned, 1)
            pe.wait_ge(kd_out, 2)
            for h in range(H):
                for c in range(NC - 1):
                    n = h * (NC - 1) + c
                    if n >= 2:
                        pe.wait_ge(state_ready, n - 1)
                    lo = (c % 2) * C
                    pe.matmul(ps[:, 2 + n % 2, 0:DV], kd_tok[lo:lo + C, c // 2, h], p2[lo:lo + C, c // 2, CV + h * DV:CV + (h + 1) * DV],
                              start=True, stop=True).then_inc(kv_done, 1)
            pe.wait_ge(state_ready, H * (NC - 1))
            pe.wait_ge(pad_done, 2 * H)

            def scores(n):
                h, tb = n % H, n // H
                if n >= 2:
                    pe.wait_ge(a_ready, n - 1)
                pe.matmul(ps[:, 4 + n % 2, 0:P], kt[:, h, tb * P:(tb + 1) * P], qt[:, h, tb * P:(tb + 1) * P], start=True, stop=True).then_inc(a_done, 1)

            scores(0)
            for n in range(TB * H):
                h, tb = n % H, n // H
                if n + 1 < TB * H:
                    scores(n + 1)
                pe.wait_ge(a_ready, n + 1)
                if n >= 2:
                    pe.wait_ge(o_out, n - 1)
                out = ps[:, 6 + n % 2, 0:DV]
                mm = pe.matmul(out, aT[:, n % 2], p2[:, tb, CV + h * DV:CV + (h + 1) * DV], start=True, stop=False)
                for c in (2 * tb, 2 * tb + 1):
                    if c:
                        mm = pe.matmul(out, qpad[h][:, c], state[:, h, c - 1], start=False, stop=(c % 2 == 1))
                mm.then_inc(o_done, 1)


def phase_second_merge(nc, e):
    ring, ps, io, p2 = e.ring, e.ps, e.io, e.p2
    with ExitStack() as ctx:
        sem = phase_semaphores(nc, ctx)
        sb = lambda name, shape: ctx.enter_context(nc.sbuf_tensor(name, shape, F32))
        split = WeightSplit(nc, ctx, sem, "merge2_weights")
        sig = sb("gate2", [P, 2, TB, CG])
        ss, rstd = sb("ss5", [P, TB]), sb("rstd5", [P, TB])
        turned, hi_out, lo_out, tb_done = sem("m2_turned"), sem("m2_hi_out"), sem("m2_lo_out"), sem("m2_tb_done")
        b_in = [sem(f"b_merge_in{j}") for j in range(2)]
        logit_ready, sig_ready, merged_out = sem("logit_ready"), sem("gate2_ready"), sem("merged2_out")
        post_in, o_ready, squares, var_ready, root_ready = sem("g_post_in"), sem("product_out"), sem("squares5"), sem("var5_ready"), sem("root5_ready")
        x_back, out_ready, stored = sem("x_back"), sem("out_ready"), sem("stored")
        base, N = ring.turn, D // CG
        w_in = io["w_in_2"][0]
        branches = ((io["w_br_pool_2"][0], 0, 8), (io["w_br_swa_2"][0], 8, 4), (io["w_br_gla_2"][0], 12, 8), (io["w_br_mem_2"][0], 20, 4))
        first_tile, tiles = [], 0
        for _, _, blocks in branches:
            first_tile.append(tiles)
            tiles += KB // TILE_K + blocks // TILE_K
        ROUND = 2 * tiles // SLOTS
        assert ROUND * SLOTS == 2 * tiles
        y_at = [A_GATE + k * P for k in range(8)] + [S_GATE + k * P for k in range(4)] + [C_GATE + k * P for k in range(8)] + [MEM_GATE + k * P for k in range(4)]
        YB = len(y_at)
        FILLS_Y, FILLS = YB // 2, (YB + KB) // 2
        merged, x_again = p2[:, :, 0:D], p2[:, :, 0:D]
        Y_HI, Y_LO, M_HI, M_LO = SQ, SQ + YB * P, SQ + YB * P, SQ + (YB + KB) * P
        BIAS, POST = Y_LO + YB * P, Y_LO + YB * P + N_BRANCH * CG
        o = p2[:, :, Y_HI:Y_HI + D]
        b_row = [p2[:, j, BIAS:POST].rearrange("p (b n) -> p b n", b=N_BRANCH) for j in range(2)]
        g_post = p2[:, :, POST:POST + D // 2]
        block_of = lambda at, k, tb: e.p2_split[:, tb, at + k * P:at + (k + 1) * P]
        y_split = lambda k, tb: (block_of(Y_HI, k, tb), block_of(Y_LO, k, tb))
        m_split = lambda k, tb: (block_of(M_HI, k, tb), block_of(M_LO, k, tb))
        two_blocks = lambda at, f: e.p2_split[:, :, at + 2 * f * P:at + (2 * f + 2) * P].rearrange("p b (a t) -> p a b t", a=2)
        fills = [(f, Y_HI, Y_LO) for f in range(FILLS_Y)] + [(f, M_HI, M_LO) for f in range(KB // 2)]
        AHEAD = N_BRANCH * TB + 1
        PER = 2 * N_BRANCH * TB

        def sources(n):
            out, cols = [], ds(n * CG, CG)
            for b, (w, _, blocks) in enumerate(branches):
                logits = w_in[:, G_LOGIT + b * D:G_LOGIT + (b + 1) * D]
                out += [k_tile(logits, s, cols) for s in range(KB // TILE_K)] + [k_tile(w, s, cols) for s in range(blocks // TILE_K)]
            return out

        block = ctx.enter_context(nc.Block())

        @block.sync
        def _(sp):
            load_tiles(sp, ring, sources(0) + sources(1), base, SLOTS)
            with sp.Fori(1, N // 2) as i:
                load_tiles(sp, ring, sources(i * 2) + sources(i * 2 + 1), i * ROUND + base)
            with sp.Fori(0, N) as n:
                load_tiles(sp, ring, turn_of(io["w_out_2"][0], ds(n * CG, CG)), n + (base + N // 2 * ROUND))
            sp.wait_ge(turned, FILLS)
            sp.dma_start(x_again, e.x_rows).then_inc(x_back, 16)
            for tb in range(TB):
                sp.wait_ge(out_ready, tb + 1)
                sp.dma_start(tokens_of(e.out[0])[:, tb], o[:, tb]).then_inc(stored, 16)
            sp.wait_ge(stored, 16 * TB)

        @block.gpsimd
        def _(pool):
            with pool.Fori(0, N // 2) as i:
                for m, piece in enumerate(pieces_of(0, 2 * tiles, i * ROUND + base)):
                    split.write_lo(pool, ring, piece, i * (2 * tiles) + m)
            with pool.Fori(0, N) as n:
                for s, piece in enumerate(pieces_of(0, SLOTS, n + (base + N // 2 * ROUND))):
                    split.write_lo(pool, ring, piece, n * SLOTS + (N * tiles + s))

        @block.tensor
        def _(pe):
            pe.sem_inc(split.free, split.free_after(0))

            def turn(fill, f, source):
                if fill >= 2:
                    pe.wait_ge(lo_out, fill - 1)
                for a in range(2):
                    for tb in range(TB):
                        at = (a * TB + tb) * P
                        tr = pe.transpose(ps[:, 6 + fill % 2, at:at + P], source(2 * f + a, tb), e.ident[:])
                tr.then_inc(turned, 1)

            for f in range(FILLS_Y):
                turn(f, f, lambda k, tb: p2[:, tb, y_at[k]:y_at[k] + P])
            pe.wait_ge(lo_out, FILLS_Y)
            with pe.Fori(0, N // 2) as i:
                t = i * ROUND + base
                for j in range(2):
                    for b, (_, first, blocks) in enumerate(branches):
                        at, half = j * tiles + first_tile[b], 4 * (b % 2)
                        n = j * N_BRANCH + b
                        free = i * PER + (2 * max(n - 1, 0) + 1)
                        gemm_split(pe, ring, split, pieces_of(at, KB // TILE_K, t), i * (2 * tiles) + at, e.h_split, [ps[:, half], ps[:, half + 1]],
                                   lambda tb: pe.wait_ge(merged_out, free) if tb == 0 else None, tb_done)
                        gemm_split(pe, ring, split, pieces_of(at + KB // TILE_K, blocks // TILE_K, t), i * (2 * tiles) + (at + KB // TILE_K), lambda k, tb: y_split(first + k, tb),
                                   [ps[:, half + 2], ps[:, half + 3]], lambda tb: None, tb_done)
            pe.wait_ge(merged_out, 2 * N * N_BRANCH + 1)
            for f in range(KB // 2):
                turn(FILLS_Y + f, f, lambda k, tb: merged[:, tb, k * P:(k + 1) * P])
            pe.wait_ge(lo_out, FILLS)
            with pe.Fori(0, N) as n:
                gemm_split(pe, ring, split, pieces_of(0, SLOTS, n + (base + N // 2 * ROUND)), n * SLOTS + N * tiles, m_split, [ps[:, 0], ps[:, 1]],
                           lambda tb: pe.wait_ge(o_ready, n * TB + (tb + 1)), tb_done)

        @block.scalar
        def _(act):
            def copy_hi(fill):
                f, hi, _ = fills[fill]
                act.wait_ge(turned, fill + 1)
                act.activation(two_blocks(hi, f), bank_blocks(e, 6 + fill % 2), ACT.Copy).then_inc(hi_out, 1)

            def sigmoid(i, n):
                for tb in range(TB):
                    act.wait_ge(logit_ready, i * PER + (n * TB + tb + 1 + AHEAD))
                    act.activation(sig[:, n % 2, tb], sig[:, n % 2, tb], ACT.Sigmoid).then_inc(sig_ready, 1)

            for fill in range(FILLS_Y):
                copy_hi(fill)
            act.dma_start(g_post, io["g_post_2"][0].rearrange("(a n) -> a n", a=2).partition_broadcast(P)).then_inc(post_in, 16)
            after = {}
            for n in range(2 * N_BRANCH):
                last = n // N_BRANCH * tiles + first_tile[n % N_BRANCH] + KB // TILE_K - 1
                after.setdefault(min(last + 2, 2 * tiles - 1), []).append(n)
            with act.Fori(0, N // 2) as i:
                pieces = pieces_of(0, 2 * tiles, i * ROUND + base)
                for m in range(2 * tiles):
                    for j in range(2):
                        if m == 6 * j:
                            act.wait_ge(logit_ready, i * PER + (AHEAD - (1 - j) * N_BRANCH * TB))
                            act.dma_start(b_row[j], io["b_merge_2"][0][:, ds((i * 2 + j) * CG, CG)].partition_broadcast(P)).then_inc(b_in[j], 16)
                    split.write_hi(act, ring, pieces[m], i * (2 * tiles) + m)
                    for n in after.get(m, []):
                        sigmoid(i, n)
            first = N // 2 * ROUND + base
            for s in range(2):
                split.write_hi(act, ring, (s, first), N * tiles + s)
            for f in range(KB // 2):
                copy_hi(FILLS_Y + f)
            for s in range(2, SLOTS):
                split.write_hi(act, ring, (s, first), N * tiles + s)
            with act.Fori(1, N) as n:
                for s, piece in enumerate(pieces_of(0, SLOTS, n + first)):
                    split.write_hi(act, ring, piece, n * SLOTS + (N * tiles + s))
            act.wait_ge(o_ready, TB * N + TB)
            rms_stats_on_scalar(act, ps[:, 2:6].rearrange("p b n -> p (b n)"), [o[:, 0], o[:, 1]], ss, rstd[:], squares, var_ready, root_ready)

        @block.vector
        def _(dve):
            step = e.dve_step

            def copy_lo(fill):
                f, hi, lo = fills[fill]
                dve.wait_ge(hi_out, fill + 1)
                dve.tensor_tensor(two_blocks(lo, f), bank_blocks(e, 6 + fill % 2), two_blocks(hi, f), ALU.subtract).then_inc(lo_out, 1)

            dve.sem_inc(logit_ready, AHEAD)
            dve.sem_inc(merged_out, 1)
            dve.sem_inc(o_ready, TB)
            for fill in range(FILLS_Y):
                copy_lo(fill)
            with dve.Fori(0, N // 2) as i:
                step.enter(i, 2 * (N_BRANCH - 1) * TB)
                for j in range(2):
                    dve.wait_ge(b_in[j], (i + 1) * 16)
                    for b, (_, _, blocks) in enumerate(branches):
                        n, half = j * N_BRANCH + b, 4 * (b % 2)
                        done = j * tiles + first_tile[b] + KB // TILE_K
                        for tb in range(TB):
                            if tb == 0:
                                dve.wait_ge(tb_done, i * (4 * N_BRANCH) + (2 * n + 1))
                            else:
                                dve.wait_ge(split.free, i * (4 * tiles) + split.free_after(done))
                            dve.tensor_tensor(sig[:, n % 2, tb], ps[:, half + tb], b_row[j][:, b], ALU.add).then_inc(logit_ready, 1)
                        for tb in range(TB):
                            dve.wait_ge(sig_ready, i * PER + (n * TB + tb + 1))
                            if tb == 0:
                                dve.wait_ge(tb_done, i * (4 * N_BRANCH) + (2 * n + 2))
                            else:
                                dve.wait_ge(split.free, i * (4 * tiles) + split.free_after(done + blocks // TILE_K))
                            out, y = merged[:, tb, ds((i * 2 + j) * CG, CG)], ps[:, half + 2 + tb]
                            if b == 0:
                                dve.tensor_tensor(out, sig[:, n % 2, tb], y, ALU.mult).then_inc(merged_out, 1)
                            else:
                                step(dve.tensor_tensor(sig[:, n % 2, tb], sig[:, n % 2, tb], y, ALU.mult))
                                dve.tensor_tensor(out, out, sig[:, n % 2, tb], ALU.add).then_inc(merged_out, 1)
                        dve.wait_ge(merged_out, i * PER + ((n + 1) * TB + 1))
            step.leave(N // 2)
            for f in range(KB // 2):
                copy_lo(FILLS_Y + f)
            with dve.Fori(0, N) as n:
                for tb in range(TB):
                    if tb == 0:
                        dve.wait_ge(tb_done, n + (4 * N_BRANCH * (N // 2) + 1))
                    else:
                        dve.wait_ge(split.free, n * (2 * SLOTS) + split.free_after(N * tiles + SLOTS))
                    dve.tensor_scalar(o[:, tb, ds(n * CG, CG)], ps[:, tb], 1.0, None, ALU.mult).then_inc(o_ready, 1)
            rms_stats_on_vector(dve, step, TB, ss[:], rstd[:], squares, var_ready, root_ready)
            dve.wait_ge(post_in, 16)
            dve.wait_ge(x_back, 16)
            for tb in range(TB):
                halves = o[:, tb].rearrange("p (a n) -> p a n", a=2)
                step(dve.scalar_tensor_tensor(halves, halves, rstd[:, tb:tb + 1], g_post, ALU.mult, ALU.mult))
                dve.tensor_tensor(o[:, tb], o[:, tb], x_again[:, tb], ALU.add).then_inc(out_ready, 1)
    ring.turn += N // 2 * ROUND + N


class Shared:
    pass


def next_place(nc):
    return -(-nc.sbuf_base // 32) * 32


def build(nc, io, out):
    with ExitStack() as ctx:
        sb = lambda name, shape, dt=F32: ctx.enter_context(nc.sbuf_tensor(name, shape, dt))
        rounded = lambda name, shape, at: nc.alloc_sbuf_tensor_at(name, shape, F32R, offset=at)
        sem = lambda name: ctx.enter_context(nc.semaphore(name))
        e = Shared()
        e.io, e.out = io, out
        e.ps = ctx.enter_context(nc.psum_tensor("banks", [P, 8, CG], F32))
        e.ring = WeightRing(nc, ctx)
        e.ident = sb("identity", [P, P])
        e.cols_a, e.cols_b = sb("cols_a", [P, P]), sb("cols_b", [P, 92])
        e.cT, e.ada = sb("cond_T", [P, KB, 2]), sb("modulation_cols", [P, 2 * KB, 2])
        x_at = next_place(nc)
        e.x = sb("x_tokens", [P, TB, D])
        hT_at = next_place(nc)
        e.hT = sb("h_T", [P, KB, T])
        e.gates, e.gate_bias = sb("gates", [P, 2 * TB, N_GATES]), sb("gate_bias", [P, N_GATES])
        e.dve_step = Steps(nc.vector, sem("dve_steps"))
        e.pool_step = Steps(nc.gpsimd, sem("pool_steps"))
        e.mod_rows = nc.dram_tensor("mod_rows", (1, 4 * D), F32, kind="Internal").ap()
        e.x_rows = nc.dram_tensor("x_rows", (P, TB, D), F32, kind="Internal").ap()
        e.gate_bias_in, e.gates_ready = sem("gate_bias_in"), sem("gates_ready")
        e.ls_uses = e.hn_uses = 0
        e.ls_neg_abs, e.ls_exp, e.ls_one_plus, e.ls_ln = sem("ls_neg_abs"), sem("ls_exp"), sem("ls_one_plus"), sem("ls_ln")
        e.hn_centred, e.hn_squared, e.hn_var, e.hn_root = sem("hn_centred"), sem("hn_squared"), sem("hn_var"), sem("hn_root")
        with ExitStack() as block1:
            sb1 = lambda name, shape: block1.enter_context(nc.sbuf_tensor(name, shape, F32))
            e.lat = sb1("lat_cols", [P, TB, MG])
            e.cxt = sb1("ctx_cols", [P, TB, 3072])
            with ExitStack() as proj:
                e.chT = proj.enter_context(nc.sbuf_tensor("ctx_h_T", [P, KB, T], F32))
                phase_modulation(nc, e)
                phase_projection(nc, e)
            phase_retention(nc, e)
            phase_mlstm(nc, e)
            phase_merge(nc, e)
        e.kv = sb("mem_kv", [P, TB, 2 * MEM_W])
        with ExitStack() as peer:
            sbp = lambda name, shape, dt=F32: peer.enter_context(nc.sbuf_tensor(name, shape, dt))
            e.h2 = sbp("h2_tokens", [P, TB, D])
            e.expert = sbp("picked_experts", [P, 2 * TB * PICKS + 8], U32)
            e.weight = sbp("picked_weights", [P, TB * PICKS])
            phase_routing(nc, e)
            phase_experts(nc, e)
        with ExitStack() as block2:
            sb2 = lambda name, shape: block2.enter_context(nc.sbuf_tensor(name, shape, F32))
            p2_at = next_place(nc)
            e.p2, e.lrT = sb2("p2_cols", [P, TB, P2_COLS]), sb2("lr_T", [16, T])
            e.hT_hi, e.hT_lo = rounded("h_T_hi", [P, KB, T], hT_at), rounded("h_T_lo", [P, KB, T], x_at)
            e.p2_split = rounded("p2_split", [P, TB, P2_COLS], p2_at)
            e.h_split = lambda k, tb: tuple(h[:, k, tb * P:(tb + 1) * P] for h in (e.hT_hi, e.hT_lo))
            phase_second_projection(nc, e)
            phase_pool(nc, e)
            phase_attention(nc, e)
            phase_gla(nc, e)
            phase_second_merge(nc, e)


INPUTS = ["x", "c", "ctx", "c_ctx", "w_ada", "b_ada", "norm1_g", "w_in", "ret_decay", "m_conv", "m_gate_bias", "w_ret_out",
          "w_mlstm_out", "w_out", "norm2_g", "peer_query", "peer_keys", "peer_down", "peer_up", "final_g", "mem_2",
          "g_pre_2", "g_post_2", "g_mem_2", "w_in_2", "b_merge_2", "w_pool_2", "pool_scale_2", "w_alpha_2", "b_alpha_2",
          "g_gla_2", "w_mem_kv_2", "w_br_pool_2", "w_br_swa_2", "w_br_gla_2", "w_br_mem_2", "w_out_2"]


def kernel(**inputs):
    import concourse.bacc as bacc
    from concourse.bass_utils import run_bass_kernel_spmd

    nc = bacc.Bacc("TRN2", target_bir_lowering=False, num_devices=1)
    arrays = {name: np.ascontiguousarray(inputs[name]) for name in INPUTS}
    arrays.update(shape_constants())
    io = {
        name: nc.dram_tensor(name, a.shape, mybir.dt.from_np(a.dtype), kind="ExternalInput").ap() for name, a in arrays.items()}
    out = nc.dram_tensor("y_out", (1, T, D), F32, kind="ExternalOutput").ap()
    build(nc, io, out)
    r = run_bass_kernel_spmd(nc, [arrays], core_ids=[0])
    return r.results[0]["y_out"]
```

```python
from contextlib import ExitStack

import numpy as np

import concourse.bass as bass
from concourse import mybir

F32 = mybir.dt.float32
F32R = mybir.dt.float32r
U32 = mybir.dt.uint32
ALU = mybir.AluOpType
ACT = mybir.ActivationFunctionType
AX = mybir.AxisListType.X
ds = bass.ds

P = 128
T = 256
TB = T // P
D = 2048
KB = D // P
CG = 512
EPS = 1e-6
SLOTS = 4
TILE_K = 4

R_HEADS, R_DK, R_DV = 8, 64, 128
M_HEADS, M_DK, M_DV = 4, 128, 256
RQ, RK, RV, RG, MQ, MK, MV, MO, MG = 0, 512, 1024, 2048, 3072, 3584, 4096, 5120, 6144
GR, GM = 6160, 8208
N_GATES = 16
PEER_H, PEER_K, PEER_TOP = 8, 128, 16
HP = 2 * PEER_H
PICKS = PEER_H * PEER_TOP
A_VAL, A_GATE, SQ, SK, SV, S_GATE = 0, 1024, 2048, 3584, 5120, 6656
CQ, CK, CV, C_GATE, C_LR, MEMQ, MEM_GATE, G_LOGIT = 7168, 7680, 8192, 9216, 10240, 10256, 10768, 11280
P2_COLS = 11280
SWA_CFG = ((128, 1), (512, 4), (2048, 16))
POOL_WINDOWS = (2, 4, 8, 16)
N_BRANCH = 4
MEM_W = 512
BIG = 1e33


class Steps:

    def __init__(self, eng, sem):
        self.eng, self.sem, self.n, self.moved = eng, sem, 0, 0

    def __call__(self, ins):
        ins.then_inc(self.sem, 1)
        self.n += 1
        self.eng.wait_ge(self.sem, self.n + self.moved)

    def enter(self, i, per):
        self.first, self.per, self.moved = self.n, per, i * per

    def leave(self, count):
        assert self.n - self.first == self.per, (self.n - self.first, self.per)
        self.n, self.moved = self.first + self.per * count, 0


def phase_semaphores(nc, ctx):
    held = []
    ctx.callback(nc.all_engine_barrier)
    ctx.callback(lambda: nc.clear_and_free_semaphores(held))

    def sem(name):
        held.append(nc.alloc_semaphore(name=name))
        return held[-1]

    return sem


def shape_constants():
    f = np.float32
    t = np.arange(T)
    p = np.arange(P)

    def split(a):
        return np.ascontiguousarray(a.reshape(TB, P, -1).transpose(1, 0, 2), dtype=f)

    n_ax = R_DK // 4
    freq = 10000.0 ** (-np.arange(n_ax, dtype=np.float64) / n_ax)
    freq = freq.astype(f)
    ang = np.concatenate([(t // 64).astype(f)[:, None] * freq, (t % 64).astype(f)[:, None] * freq], axis=1)
    rope = np.stack([np.cos(ang), np.sin(ang)], axis=1).reshape(T, -1)
    s_, t_ = t[:, None], t[None, :]
    rel = np.concatenate([np.maximum(t_ - s_, 0), np.maximum(s_ - t_, 0), t_ == s_], axis=1)
    pos = np.stack([T - 1 - t, t, t + 1, T - t], axis=1)
    causal = np.concatenate([t_ >= s_, t_ <= s_], axis=1)
    ltri = np.stack([p[:, None] <= p[None, :], p[:, None] >= p[None, :], np.ones((P, P))], axis=1)
    pool = []
    for w in POOL_WINDOWS:
        inside = (s_ <= t_) & (s_ > t_ - w)
        pool.append(inside / np.minimum(t_ + 1, w).astype(f) - (s_ == t_))
    pool = np.concatenate(pool, axis=1)
    dist = []
    for w, d in SWA_CFG:
        gap = t[:, None] - t[None, :]
        ok = (gap >= 0) & (gap % d == 0) & (gap <= w)
        dist.append(np.where(ok, gap, BIG))
    dist = np.concatenate(dist, axis=1)
    same = (p[:, None] // 64 == p[None, :] // 64) & (p[None, :] >= p[:, None])
    top = np.finfo(f).max
    chunk = np.stack([np.where(same, top, 0.0), np.where(same, -top, 0.0)], axis=1)
    seg = np.tile((np.arange(4 * T) % 64 != 0).astype(f), (P, 1))
    pick = np.zeros((8, 8, P))
    for r in range(8):
        pick[r, r] = 1.0
    iota16 = np.tile(np.arange(16), (P, 1))
    return {
        "k_ident": np.eye(P, dtype=f), "k_rope": split(rope), "k_rel": split(rel), "k_pos": split(pos),
        "k_causal": split(causal), "k_ltri": np.ascontiguousarray(ltri, f), "k_pool": split(pool),
        "k_dist": split(dist), "k_chunk": np.ascontiguousarray(chunk, f), "k_seg": seg,
        "k_pick": np.ascontiguousarray(pick, f), "k_iota16": iota16.astype(f),
    }


def rows_of(ap):
    return ap.rearrange("(r c) -> r c", c=P)


def tokens_of(ap):
    return ap.rearrange("(b p) d -> p b d", p=P)


def k_tile(w, s, cols):
    return w[s * TILE_K * P:(s + 1) * TILE_K * P, cols].rearrange("(k p) n -> p k n", p=P)


class WeightRing:

    def __init__(self, nc, ctx):
        self.tile = ctx.enter_context(nc.sbuf_tensor("weight_ring", [P, SLOTS, TILE_K, CG], F32))
        self.landed = [ctx.enter_context(nc.semaphore(f"weight_landed{s}")) for s in range(SLOTS)]
        self.used = ctx.enter_context(nc.semaphore("weight_used"))
        self.granted = ctx.enter_context(nc.semaphore("weight_slot_granted"))
        self.turn = 0

    def load(self, sp, s, src, turn):
        if not (isinstance(turn, int) and turn == 0):
            sp.wait_ge(self.used, (turn - 1) * SLOTS + (s + 1))
            sp.sem_inc(self.granted, 1)
        sp.dma_start(self.tile[:, s], src).then_inc(self.landed[s], 16)

    def load_turn(self, sp, sources, turn):
        for s in range(SLOTS):
            self.load(sp, s, sources[s], turn)

    def arrived(self, pe, s, turn):
        pe.wait_ge(self.landed[s], (turn + 1) * 16)


def turn_of(w, cols):
    return [k_tile(w, s, cols) for s in range(SLOTS)]


def gemm_token_major(pe, ring, pieces, lhs, outs, before, tb_done):
    n = len(pieces) * TILE_K
    last_tb = len(outs) - 1
    for tb, out in enumerate(outs):
        before(tb)
        for i, (slot, turn) in enumerate(pieces):
            if tb == 0:
                ring.arrived(pe, slot, turn)
            for kk in range(TILE_K):
                k = i * TILE_K + kk
                mm = pe.matmul(out, lhs(k, tb), ring.tile[:, slot, kk, :], start=(k == 0), stop=(k == n - 1))
            if tb == last_tb:
                mm.then_inc(ring.used, 1)
        if tb != last_tb:
            mm.then_inc(tb_done, 1)


def phase_modulation(nc, e):
    ring, ps = e.ring, e.ps
    with ExitStack() as ctx:
        sb = lambda name, shape: ctx.enter_context(nc.sbuf_tensor(name, shape, F32))
        sem = phase_semaphores(nc, ctx)
        rows_a = sb("rows_a", [P, P])
        rows_b = sb("rows_b", [92, P])
        raw = sb("ctx_tokens", [P, TB, D])
        xn = sb("normed_tokens", [P, TB, D])
        ss = sb("square_sums", [P, 4])
        rstd = sb("rstd", [P, 4])
        scale1 = sb("scale1", [P, KB, 2])
        h_now = sb("h_now", [P, 2, 2, T])
        lo_out = sem("h1_lo_out")
        rows_in, x_in, ctx_in = sem("rows_in"), sem("x_in"), sem("ctx_in")
        silu_done, rows_turned, cols_ready = sem("silu_done"), sem("rows_turned"), sem("cols_ready")
        squares, var_ready, root_ready, xn_ready = sem("squares"), sem("var_ready"), sem("root_ready"), sem("xn_ready")
        scale1_ready, x_turned, h_out = sem("scale1_ready"), sem("x_turned"), sem("h_out")
        cond_bank_free, cond_turned = sem("cond_bank_free"), sem("cond_turned")
        cond_rows = e.lat[0:2, 0, 0:2 * D]
        ADA1 = 2 * D // CG
        normed = [xn[:, 0], xn[:, 1], raw[:, 0], raw[:, 1]]
        block = ctx.enter_context(nc.Block())

        @block.sync
        def _(sp):
            ring.load_turn(sp, turn_of(e.io["w_ada"][0], slice(0, CG)), 0)
            with sp.Fori(1, ADA1) as g:
                ring.load_turn(sp, turn_of(e.io["w_ada"][0], ds(g * CG, CG)), g)
            ring.load_turn(sp, turn_of(e.io["w_in"][0], slice(RK, RK + CG)), ADA1)

        @block.scalar
        def _(act):
            io = e.io
            for dst, vec in ((rows_b[0:16], io["c"][0]), (rows_b[16:32], io["c_ctx"]), (rows_b[56:72], io["g_pre_2"][0]),
                             (rows_b[72:88], io["g_mem_2"][0]), (rows_b[88:92], io["b_alpha_2"][0]),
                             (rows_a[0:96], io["b_ada"][0]), (rows_a[96:112], io["norm1_g"][0]),
                             (rows_a[112:128], io["norm2_g"][0])):
                act.dma_start(dst, rows_of(vec)).then_inc(rows_in, 16)
            act.dma_start(rows_b[32:56], io["m_conv"][0].rearrange("j (r c) -> (j r) c", c=P)).then_inc(rows_in, 16)
            act.dma_start(e.ident[:], io["k_ident"]).then_inc(rows_in, 16)
            act.dma_start(e.x[:], tokens_of(io["x"][0])).then_inc(x_in, 16)
            act.dma_start(raw[:], tokens_of(io["ctx"][0])).then_inc(ctx_in, 16)
            act.wait_ge(rows_in, 160)
            act.activation(rows_b[0:32], rows_b[0:32], ACT.Silu).then_inc(silu_done, 1)
            act.wait_ge(x_in, 16)
            act.wait_ge(ctx_in, 16)
            for j, t in enumerate((e.x[:, 0], e.x[:, 1], raw[:, 0], raw[:, 1])):
                if j:
                    act.wait_ge(squares, j)
                act.activation(ps[:, 2:6].rearrange("p b n -> p (b n)"), t, ACT.Square, accum_out=ss[:, j:j + 1]).then_inc(squares, 1)
            act.wait_ge(var_ready, 1)
            act.activation(rstd[:], rstd[:], ACT.Sqrt).then_inc(root_ready, 1)
            act.wait_ge(scale1_ready, 1)
            for k in range(KB):
                act.wait_ge(x_turned, k + 1)
                bank = ps[:, 4 + k % 2]
                if k >= 2:
                    act.wait_ge(lo_out, 2 * (k - 1))
                for j in range(2):
                    act.activation(h_now[:, k % 2, j], bank[:, j * T:(j + 1) * T], ACT.Identity, scale=scale1[:, k, j:j + 1],
                                   bias=e.ada[:, k, j:j + 1]).then_inc(h_out, 1)

        @block.vector
        def _(dve):
            step = e.dve_step
            dve.sem_inc(cond_bank_free, 2)
            dve.wait_ge(rows_turned, 1)
            step(dve.tensor_copy(e.cols_b[:], ps[:, 6, 0:92]))
            dve.tensor_copy(e.cT[:], ps[:, 6, 0:32].rearrange("p (v k) -> p k v", v=2)).then_inc(cols_ready, 1)
            dve.wait_ge(rows_turned, 2)
            step(dve.tensor_copy(e.cols_a[:], ps[:, 7, 0:P]))
            dve.wait_ge(squares, 4)
            dve.tensor_scalar(rstd[:], ss[:], 1.0 / D, EPS, ALU.mult, ALU.add).then_inc(var_ready, 1)
            dve.wait_ge(root_ready, 1)
            step(dve.reciprocal(rstd[:], rstd[:]))
            for j, t in enumerate((e.x[:, 0], e.x[:, 1], raw[:, 0], raw[:, 1])):
                dve.tensor_scalar(normed[j], t, rstd[:, j:j + 1], None, ALU.mult).then_inc(xn_ready, 1)
            with dve.Fori(0, ADA1 // 2) as i:
                for j in range(2):
                    dve.wait_ge(ring.used, (i * 2 + (j + 1)) * SLOTS)
                    dve.tensor_scalar(cond_rows[:, ds((i * 2 + j) * CG, CG)], ps[0:2, j], 1.0, None, ALU.mult).then_inc(cond_bank_free, 1)
            dve.wait_ge(cond_turned, 1)
            step(dve.tensor_tensor(e.ada[:], ps[:, 6, 0:4 * KB].rearrange("p (n v) -> p n v", v=2),
                                   e.cols_a[:, 0:2 * KB].unsqueeze(2).to_broadcast([P, 2 * KB, 2]), ALU.add))
            dve.scalar_tensor_tensor(scale1[:], e.ada[:, KB:2 * KB], 1.0,
                                     e.cols_a[:, 96:112].unsqueeze(2).to_broadcast([P, KB, 2]),
                                     ALU.add, ALU.mult).then_inc(scale1_ready, 1)
            for k in range(KB):
                for j, (hi, lo) in enumerate(((e.hT_hi[:, k], e.hT_lo[:, k]), (e.chT_hi[:, k], e.chT_lo[k]))):
                    dve.wait_ge(h_out, 2 * k + j + 1)
                    step(dve.tensor_copy(hi, h_now[:, k % 2, j]))
                    dve.tensor_tensor(lo, h_now[:, k % 2, j], hi, ALU.subtract).then_inc(lo_out, 1)

        @block.tensor
        def _(pe):
            pe.wait_ge(rows_in, 160)
            pe.wait_ge(silu_done, 1)
            pe.transpose(ps[:, 6, 0:92], rows_b[:], e.ident[0:92, 0:92]).then_inc(rows_turned, 1)
            pe.transpose(ps[:, 7, 0:P], rows_a[:], e.ident[:]).then_inc(rows_turned, 1)
            pe.wait_ge(cols_ready, 1)
            with pe.Fori(0, ADA1 // 2) as i:
                for j in range(2):
                    pe.wait_ge(cond_bank_free, i * 2 + (j + 1))
                    for s in range(SLOTS):
                        ring.arrived(pe, s, i * 2 + j)
                        for kk in range(TILE_K):
                            k = s * TILE_K + kk
                            mm = pe.matmul(ps[0:2, j], e.cT[:, k], ring.tile[:, s, kk], start=(k == 0), stop=(k == KB - 1))
                        mm.then_inc(ring.used, 1)
            pe.wait_ge(cond_bank_free, ADA1 + 2)
            for n in range(2 * KB):
                tr = pe.transpose(ps[:, 6, 2 * n:2 * n + 2], cond_rows[:, n * P:(n + 1) * P], e.ident[0:2, 0:2])
            tr.then_inc(cond_turned, 1)
            pe.wait_ge(xn_ready, 4)
            for k in range(KB):
                if k >= 2:
                    pe.wait_ge(h_out, 2 * (k - 1))
                for j in range(4):
                    tr = pe.transpose(ps[:, 4 + k % 2, j * P:(j + 1) * P], normed[j][:, k * P:(k + 1) * P], e.ident[:])
                tr.then_inc(x_turned, 1)
    ring.turn += ADA1


def phase_projection(nc, e):
    ring, ps, io = e.ring, e.ps, e.io
    with ExitStack() as ctx:
        sem = phase_semaphores(nc, ctx)
        sb = lambda name, shape, dt=F32: ctx.enter_context(nc.sbuf_tensor(name, shape, dt))
        tb_done, bank_free, gates_in, gates_done = sem("tb_done"), sem("bank_free"), sem("gates_in"), sem("gates_done")
        split = WeightSplit(nc, ctx, sem, "in_weights")
        w_gate = sb("w_gate", [P, KB, N_GATES])
        w_gate_hi, w_gate_lo = sb("w_gate_hi", [P, KB, N_GATES], F32R), sb("w_gate_lo", [P, KB, N_GATES], F32R)
        w_in, base = io["w_in"][0], ring.turn
        runs = ((1, 3, 4, 2), (7, 3, 4, 2), (4, 3, 2, 1), (10, 1, 2, 1), (11, 1, 2, 0), (0, 1, 2, 0))
        LAST_CONTEXT = 1
        n_turns = sum(n for _, n, _, _ in runs)
        ADA1, ADA2 = 2 * D // CG, 4 * D // CG
        assert sum(n * m for _, n, _, m in runs) == ADA2
        COND_SLOTS, SUB = 2, CG // P
        cond_tile = sb("cond_ring", [P, COND_SLOTS, TILE_K, CG])
        cond_acc = e.lat[:, :, 11 * CG:12 * CG]
        pick = sb("cond_pick", [P, 2 * ADA2])
        cond_cols, cond_bias, cond_rows = sb("cond_cols", [P, SUB * ADA2]), sb("cond_bias", [SUB * ADA2, P]), sb("cond_rows", [SUB * ADA2, P])
        gate_rows, gates_out, gates_turned = e.lat[0:N_GATES, 0, 0:2 * T], sem("gates_out"), sem("gates_turned")
        cond_landed = [sem(f"cond_landed{s}") for s in range(COND_SLOTS)]
        cond_bias_in, cond_used, cond_summed, cond_done = sem("cond_bias_in"), sem("cond_used"), sem("cond_summed"), sem("cond_done")
        cond_cols_out, cond_turned, cond_ready, cond_stored = sem("cond_cols_out"), sem("cond_rows_turned"), sem("cond_rows_ready"), sem("cond_stored")
        pick_ready, pick_zero, gate_hi_ready, gate_lo_ready = sem("pick_ready"), sem("pick_zero"), sem("gate_hi_ready"), sem("gate_lo_ready")
        by_row = lambda ap: ap.rearrange("(g s p) -> s g p", s=SUB, p=P)
        block = ctx.enter_context(nc.Block())

        @block.sync
        def _(sp):
            def load_cond(g):
                for s in range(SLOTS):
                    at = s % COND_SLOTS
                    sp.wait_ge(cond_used, g * SLOTS + (s + 1))
                    sp.sem_inc(ring.granted, 1)
                    sp.dma_start(cond_tile[:, at], k_tile(io["w_ada"][0], s, ds((g + ADA1) * CG, CG))).then_inc(cond_landed[at], 16)

            for s in range(SUB):
                sp.dma_start(cond_bias[s * ADA2:(s + 1) * ADA2], by_row(io["b_ada"][0, 2 * D:6 * D])[s]).then_inc(cond_bias_in, 16)
            turn, summed = base, 0
            for first, n, _, m in runs:
                skip = 1 if turn == base else 0
                if skip:
                    for j in range(m):
                        load_cond(j)
                with sp.Fori(skip, n) as i:
                    ring.load_turn(sp, turn_of(w_in, ds((i + first) * CG, CG)), i + turn)
                    for j in range(m):
                        load_cond(i * m + (summed + j))
                turn, summed = turn + n, summed + n * m
            ring.load_turn(sp, turn_of(w_in, slice(GR, GR + CG)), turn)
            sp.wait_ge(cond_ready, 1)
            for s in range(SUB):
                sp.dma_start(by_row(e.mod_rows[0])[s], cond_rows[s * ADA2:(s + 1) * ADA2]).then_inc(cond_stored, 16)
            sp.wait_ge(cond_stored, SUB * 16)

        @block.scalar
        def _(act):
            act.dma_start(e.gate_bias[:], io["m_gate_bias"][0].rearrange("a b c -> (a b c)").partition_broadcast(P)).then_inc(e.gate_bias_in, 16)
            act.dma_start(w_gate[:], w_in[:, MG:MG + N_GATES].rearrange("(k p) n -> p k n", p=P)).then_inc(gates_in, 16)
            turn = base
            for r, (_, n, _, _) in enumerate(runs):
                with act.Fori(0, n) as i:
                    for s in range(SLOTS):
                        split.write_hi(act, ring, (s, i + turn), i * SLOTS + ((turn - base) * SLOTS + s))
                turn += n
                if r == 0:
                    act.wait_ge(gates_in, 16)
                    act.activation(w_gate_hi[:], w_gate[:], ACT.Copy).then_inc(gate_hi_ready, 1)

        @block.gpsimd
        def _(pool):
            pool.memset(pick[:], 0.0).then_inc(pick_zero, 1)
            pool.wait_ge(pick_zero, 1)
            pool.memset(pick[:, ADA2:ADA2 + 1], 1.0).then_inc(pick_ready, 1)
            turn = base
            for r, (_, n, _, _) in enumerate(runs):
                with pool.Fori(0, n) as i:
                    for s in range(SLOTS):
                        split.write_lo(pool, ring, (s, i + turn), i * SLOTS + ((turn - base) * SLOTS + s))
                turn += n
                if r == 0:
                    pool.wait_ge(gate_hi_ready, 1)
                    pool.tensor_tensor(w_gate_lo[:], w_gate[:], w_gate_hi[:], ALU.subtract).then_inc(gate_lo_ready, 1)

        @block.tensor
        def _(pe):
            pe.sem_inc(split.free, split.free_after(0))

            def lhs(k, j):
                if j < TB:
                    return e.h_split(k, j)
                cols = slice((j - TB) * P, (j - TB + 1) * P)
                return e.chT_hi[:, k, cols], e.chT_lo[k][:, cols]

            sums = lambda s: ps[:, 0, s * ADA2:(s + 1) * ADA2]
            turn, used, summed = base, 0, 0
            pe.wait_ge(pick_ready, 1)
            for s in range(SUB):
                pe.matmul(sums(s), e.ident[:], pick[:, 0:ADA2], start=(s == 0), stop=False, skip_group_check=True)
            for r, (first, n, ntb, m) in enumerate(runs):
                with pe.Fori(0, n) as i:
                    gemm_split(pe, ring, split, pieces_of(0, SLOTS, i + turn), i * SLOTS + (turn - base) * SLOTS, lhs,
                               [ps[:, 2 + j] for j in range(ntb)], lambda j: pe.wait_ge(bank_free, i * ntb + (used + j + 1 + 4 - ntb)), tb_done)
                    for j in range(m):
                        g = i * m + (summed + j)
                        pe.wait_ge(cond_summed, g + 1)
                        for s in range(SUB):
                            mm = pe.matmul(sums(s), cond_acc[:, j, s * P:(s + 1) * P], pick[:, ds(g + 1, ADA2)],
                                           start=False, stop=False, skip_group_check=True)
                        mm.then_inc(cond_done, 1)
                turn, used, summed = turn + n, used + n * ntb, summed + n * m
                if r == LAST_CONTEXT:
                    pe.wait_ge(gate_lo_ready, 1)
                    for j, (hi, lo) in enumerate(((lambda k: e.hT_hi[:, k], lambda k: e.hT_lo[:, k]), (lambda k: e.chT_hi[:, k], lambda k: e.chT_lo[k]))):
                        out = ps[0:N_GATES, 6 + j, 0:T]
                        for k in range(KB):
                            pe.matmul(out, w_gate_hi[:, k], hi(k), start=(k == 0), stop=False)
                            pe.matmul(out, w_gate_lo[:, k], hi(k), start=False, stop=False)
                            mm = pe.matmul(out, w_gate_hi[:, k], lo(k), start=False, stop=(k == KB - 1))
                    mm.then_inc(gates_done, 1)
                    pe.wait_ge(gates_out, 1)
                    for j in range(2 * TB):
                        tr = pe.transpose(ps[:, 1, j * N_GATES:(j + 1) * N_GATES], gate_rows[:, j * P:(j + 1) * P], e.ident[0:N_GATES, 0:N_GATES])
                    tr.then_inc(gates_turned, 1)
            pe.wait_ge(cond_cols_out, 1)
            pe.transpose(ps[0:SUB * ADA2, 1, 0:P], cond_cols[:], e.ident[:]).then_inc(cond_turned, 1)

        @block.vector
        def _(dve):
            step = e.dve_step
            dve.sem_inc(bank_free, 4)
            dve.sem_inc(cond_used, COND_SLOTS)
            dve.sem_inc(cond_done, 1)
            done, summed, tiles = 0, 0, 0
            for r, (first, n, ntb, m) in enumerate(runs):
                if r == LAST_CONTEXT + 1:
                    dve.wait_ge(gates_done, 1)
                    dve.tensor_copy(gate_rows.rearrange("p (j t) -> p j t", j=2), ps[0:N_GATES, 6:8, 0:T]).then_inc(gates_out, 1)
                    dve.wait_ge(gates_turned, 1)
                    dve.wait_ge(e.gate_bias_in, 16)
                    dve.tensor_tensor(e.gates[:], ps[:, 1, 0:4 * N_GATES].rearrange("p (j g) -> p j g", j=4),
                                      e.gate_bias[:].unsqueeze(1).to_broadcast([P, 4, N_GATES]), ALU.add).then_inc(e.gates_ready, 1)
                with dve.Fori(0, n) as i:
                    step.enter(i, m * SLOTS * (TILE_K - 1))
                    for j in range(m):
                        g = i * m + (summed + j)
                        if j == 0:
                            dve.wait_ge(cond_done, g + 1)
                        for s in range(SLOTS):
                            at = s % COND_SLOTS
                            dve.wait_ge(cond_landed[at], g * (16 * SLOTS // COND_SLOTS) + (s // COND_SLOTS + 1) * 16)
                            for kk in range(TILE_K):
                                k, acc = s * TILE_K + kk, cond_acc[:, j]
                                if k == 0:
                                    x = dve.tensor_scalar(acc, cond_tile[:, at, kk], e.cT[:, k, 0:1], None, ALU.mult)
                                else:
                                    x = dve.scalar_tensor_tensor(acc, cond_tile[:, at, kk], e.cT[:, k, 0:1], acc, ALU.mult, ALU.add)
                                if kk < TILE_K - 1:
                                    step(x)
                            x.then_inc(cond_used, 1)
                            dve.wait_ge(cond_used, g * SLOTS + (s + 1 + COND_SLOTS))
                        dve.sem_inc(cond_summed, 1)
                    for j in range(ntb):
                        if j < ntb - 1:
                            dve.wait_ge(tb_done, i * (ntb - 1) + (done + j + 1))
                        else:
                            dve.wait_ge(split.free, i * (2 * SLOTS) + split.free_after(tiles + SLOTS))
                        if j < TB:
                            dst = e.lat[:, j, ds((i + first) * CG, CG)]
                        else:
                            dst = e.cxt[:, j - TB, ds((i + (0 if first == 1 else 3)) * CG, CG)]
                        dve.tensor_scalar(dst, ps[:, 2 + j], 1.0, None, ALU.mult).then_inc(bank_free, 1)
                step.leave(n)
                done, summed, tiles = done + n * (ntb - 1), summed + n * m, tiles + n * SLOTS
                if m and not runs[r + 1][3]:
                    dve.wait_ge(cond_done, ADA2 + 1)
                    in_order = ps[:, 0, 0:SUB * ADA2].rearrange("p (s g) -> p s g", s=SUB)[:, :, ::-1]
                    dve.tensor_copy(cond_cols[:].rearrange("p (s g) -> p s g", s=SUB), in_order).then_inc(cond_cols_out, 1)
            dve.wait_ge(cond_turned, 1)
            dve.wait_ge(cond_bias_in, SUB * 16)
            dve.tensor_tensor(cond_rows[:], ps[0:SUB * ADA2, 1, 0:P], cond_bias[:], ALU.add).then_inc(cond_ready, 1)
    ring.turn += n_turns


def log_sigmoid_on_vector(dve, step, e, z, u, w, out):
    e.ls_uses += 1
    dve.scalar_tensor_tensor(u, z, -1.0, z, ALU.mult, ALU.min).then_inc(e.ls_neg_abs, 1)
    dve.wait_ge(e.ls_exp, e.ls_uses)
    dve.tensor_scalar(w, u, 1.0, None, ALU.add).then_inc(e.ls_one_plus, 1)
    dve.wait_ge(e.ls_ln, e.ls_uses)
    step(dve.scalar_tensor_tensor(u, w, -1.0, u, ALU.add, ALU.subtract))
    step(dve.reciprocal(w, w))
    step(dve.tensor_tensor(u, u, w, ALU.mult))
    step(dve.tensor_tensor(out, out, u, ALU.subtract))
    step(dve.scalar_tensor_tensor(out, z, 0.0, out, ALU.min, ALU.subtract))


def log_sigmoid_on_scalar(act, e, use, u, w, out):
    act.wait_ge(e.ls_neg_abs, use)
    act.activation(u, u, ACT.Exp).then_inc(e.ls_exp, 1)
    act.wait_ge(e.ls_one_plus, use)
    act.activation(out, w, ACT.Ln).then_inc(e.ls_ln, 1)


def head_norm_on_vector(dve, step, e, y, sq, stat, width):
    e.hn_uses += 1
    n = y.shape[1]
    wide = [P, n, width]
    step(dve.tensor_reduce(stat, y, AX, ALU.add))
    step(dve.tensor_scalar(stat, stat, 1.0 / width, None, ALU.mult))
    dve.tensor_tensor(y, y, stat.unsqueeze(2).to_broadcast(wide), ALU.subtract).then_inc(e.hn_centred, 1)
    dve.wait_ge(e.hn_squared, e.hn_uses)
    step(dve.tensor_reduce(stat, sq, AX, ALU.add))
    dve.tensor_scalar(stat, stat, 1.0 / width, EPS, ALU.mult, ALU.add).then_inc(e.hn_var, 1)
    dve.wait_ge(e.hn_root, e.hn_uses)
    step(dve.reciprocal(stat, stat))
    step(dve.tensor_tensor(y, y, stat.unsqueeze(2).to_broadcast(wide), ALU.mult))


def head_norm_on_scalar(act, e, use, y, sq, stat):
    act.wait_ge(e.hn_centred, use)
    act.activation(sq, y, ACT.Square).then_inc(e.hn_squared, 1)
    act.wait_ge(e.hn_var, use)
    act.activation(stat, stat, ACT.Sqrt).then_inc(e.hn_root, 1)


def phase_retention(nc, e):
    ps, io, H = e.ps, e.io, R_HEADS
    with ExitStack() as ctx:
        sb = lambda name, shape: ctx.enter_context(nc.sbuf_tensor(name, shape, F32))
        sem = phase_semaphores(nc, ctx)
        rope, rel, pos = sb("rope", [P, TB, 64]), sb("rel", [P, TB, 3 * T]), sb("pos", [P, TB, 4])
        z, u, w, lg = (sb(f"ls_ret_{n}", [P, 2 * H]) for n in "zuwl")
        dec = sb("decays", [P, TB, 4, H])
        rot = sb("rotated_qk", [P, TB, 2 * H, 2, 32])
        tmp = sb("rotary_tmp", [P, TB, 2 * H, 32])
        kdec = sb("k_decayed", [P, TB, H, 2, R_DK])
        qdec = sb("q_decayed", [P, TB, H, 2, R_DK])
        turned = sb("turned_qk", [P, 8, 2, T])
        state = sb("ret_state", [P, H, R_DV])
        dti = sb("decay_matrix", [P, 2, TB, T])
        att = sb("ret_att", [P, 2, TB, T])
        y = rot[:].rearrange("p b g a n -> p (b g a n)").rearrange("p (h e) -> p h e", e=R_DV)
        sq = kdec[:].rearrange("p b h a n -> p (b h a n)").rearrange("p (h e) -> p h e", e=R_DV)
        stat = sb("ret_stat", [P, TB * H])
        tables, expo_ready, dec_ready = sem("tables"), sem("expo_ready"), sem("dec_ready")
        rot1_ready, qdec_ready, kdec_ready, rot0_ready = sem("rot1_ready"), sem("qdec_ready"), sem("kdec_ready"), sem("rot0_ready")
        state_done, state_out = sem("state_done"), sem("state_out")
        turn_done, turn_out = sem("turn_done"), sem("turn_out")
        dlog_ready, dexp_ready, decay_ready = sem("dlog_ready"), sem("dexp_ready"), sem("decay_ready")
        att_done, att_ready, y_done, y_out, gate_ready = sem("att_done"), sem("att_ready"), sem("y_done"), sem("y_out"), sem("gate_ready")
        q_cols = lambda tb: rot[:, tb, 0:H].rearrange("p h a n -> p h (a n)")
        use = e.ls_uses + 1
        hn_use = e.hn_uses + 1
        lat_gate = e.lat[:, :, RG:RG + H * R_DV]
        FILLS = 8

        def rotary(eng, step, tb, ready):
            v = e.lat[:, tb, RQ:RQ + 2 * H * R_DK].rearrange("p (h a n) -> p h a n", a=2, n=32)
            cos, sin = (rope[:, tb, c:c + 32].unsqueeze(1).to_broadcast([P, 2 * H, 32]) for c in (0, 32))
            t1, t2, o = v[:, :, 0], v[:, :, 1], rot[:, tb]
            step(eng.tensor_tensor(o[:, :, 0], t1, cos, ALU.mult))
            step(eng.tensor_tensor(tmp[:, tb], t2, sin, ALU.mult))
            step(eng.tensor_tensor(o[:, :, 0], o[:, :, 0], tmp[:, tb], ALU.subtract))
            step(eng.tensor_tensor(o[:, :, 1], t2, cos, ALU.mult))
            step(eng.tensor_tensor(tmp[:, tb], t1, sin, ALU.mult))
            eng.tensor_tensor(o[:, :, 1], o[:, :, 1], tmp[:, tb], ALU.add).then_inc(ready, 1)

        block = ctx.enter_context(nc.Block())

        @block.scalar
        def _(act):
            act.dma_start(z[:], io["ret_decay"][0].rearrange("a h -> (a h)").partition_broadcast(P)).then_inc(tables, 16)
            act.dma_start(rope[:], io["k_rope"]).then_inc(tables, 16)
            act.dma_start(pos[:], io["k_pos"]).then_inc(tables, 16)
            act.dma_start(rel[:], io["k_rel"]).then_inc(tables, 16)
            log_sigmoid_on_scalar(act, e, use, u[:], w[:], lg[:])
            act.wait_ge(expo_ready, 1)
            act.activation(dec[:], dec[:], ACT.Exp).then_inc(dec_ready, 1)
            act.wait_ge(state_done, 1)
            act.activation(state[:], ps[:, 0:2].rearrange("p b (h e) -> p (b h) e", e=R_DV), ACT.Copy).then_inc(state_out, 1)
            for f in range(FILLS):
                act.wait_ge(turn_done, f + 1)
                act.activation(turned[:, f].rearrange("p a t -> p (a t)"), ps[:, 2 + f % 2], ACT.Copy,
                               scale=R_DK ** -0.5 if f in (2, 3) else 1.0).then_inc(turn_out, 1)
            for h in range(H):
                act.wait_ge(dlog_ready, h + 1)
                act.activation(dti[:, h % 2], dti[:, h % 2], ACT.Exp).then_inc(dexp_ready, 1)
            for tb in range(TB):
                act.wait_ge(y_done, H)
                act.activation(y[:, tb * H:(tb + 1) * H], ps[:, 2 * tb:2 * tb + 2].rearrange("p b (h e) -> p (b h) e", e=R_DV),
                               ACT.Copy).then_inc(y_out, 1)
            head_norm_on_scalar(act, e, hn_use, y, sq, stat[:])
            act.activation(lat_gate, lat_gate, ACT.Silu).then_inc(gate_ready, 1)

        @block.vector
        def _(dve):
            step = e.dve_step
            dve.wait_ge(tables, 64)
            log_sigmoid_on_vector(dve, step, e, z[:], u[:], w[:], lg[:])
            for tb in range(TB):
                for kind in range(4):
                    d = kind % 2
                    x = dve.tensor_scalar(dec[:, tb, kind], lg[:, d * H:(d + 1) * H], pos[:, tb, kind:kind + 1], None, ALU.mult)
                    if (tb, kind) != (TB - 1, 3):
                        step(x)
            x.then_inc(expo_ready, 1)
            rotary(dve, step, 0, rot0_ready)
            dve.wait_ge(dec_ready, 1)
            for tb in range(TB):
                for d in range(2):
                    dve.scalar_tensor_tensor(kdec[:, tb, :, d], e.cxt[:, tb, 0:H * R_DK].rearrange("p (h n) -> p h n", h=H),
                                             R_DK ** -0.5, dec[:, tb, d].unsqueeze(2).to_broadcast([P, H, R_DK]),
                                             ALU.mult, ALU.mult).then_inc(kdec_ready, 1)
            for h in range(H + 1):
                if h < H:
                    if h >= 2:
                        dve.wait_ge(att_ready, h - 1)
                    step(dve.tensor_scalar(dti[:, h % 2], rel[:, :, 0:T], lg[:, h:h + 1], None, ALU.mult))
                    dve.scalar_tensor_tensor(dti[:, h % 2], rel[:, :, T:2 * T], lg[:, H + h:H + h + 1], dti[:, h % 2],
                                             ALU.mult, ALU.add).then_inc(dlog_ready, 1)
                if h >= 1:
                    g = h - 1
                    dve.wait_ge(decay_ready, g + 1)
                    dve.wait_ge(att_done, g + 1)
                    if g >= 2:
                        dve.wait_ge(y_done, g - 1)
                    dve.tensor_tensor(att[:, g % 2], ps[:, 4 + g % 2].rearrange("p (s t) -> p s t", s=TB), dti[:, g % 2],
                                      ALU.mult).then_inc(att_ready, 1)
            dve.wait_ge(y_out, TB)
            head_norm_on_vector(dve, step, e, y, sq, stat[:], R_DV)
            dve.wait_ge(gate_ready, 1)
            step(dve.tensor_tensor(lat_gate, lat_gate, y.rearrange("p (b h) e -> p b (h e)", b=TB), ALU.mult))

        @block.gpsimd
        def _(pool):
            step = e.pool_step
            pool.wait_ge(tables, 64)
            rotary(pool, step, 1, rot1_ready)
            pool.wait_ge(rot1_ready, 1)
            pool.wait_ge(dec_ready, 1)
            pool.wait_ge(rot0_ready, 1)
            for tb in range(TB):
                for d in range(2):
                    pool.tensor_tensor(qdec[:, tb, :, d], q_cols(tb),
                                       dec[:, tb, 2 + d].unsqueeze(2).to_broadcast([P, H, R_DK]), ALU.mult).then_inc(qdec_ready, 1)
            for h in range(H):
                pool.wait_ge(dexp_ready, h + 1)
                pool.tensor_tensor(dti[:, h % 2], dti[:, h % 2], rel[:, :, 2 * T:3 * T], ALU.add).then_inc(decay_ready, 1)

        @block.tensor
        def _(pe):
            pe.wait_ge(kdec_ready, 4)
            for h in range(H):
                for tb in range(TB):
                    mm = pe.matmul(ps[:, h // 4, (h % 4) * P:(h % 4 + 1) * P],
                                   kdec[:, tb, h].rearrange("p a n -> p (a n)"),
                                   e.cxt[:, tb, 512 + h * R_DV:512 + (h + 1) * R_DV], start=(tb == 0), stop=(tb == TB - 1))
            mm.then_inc(state_done, 1)
            pe.wait_ge(rot0_ready, 1)
            pe.wait_ge(rot1_ready, 1)
            for f in range(FILLS):
                if f == 4:
                    pe.wait_ge(qdec_ready, 4)
                if f >= 2:
                    pe.wait_ge(turn_out, f - 1)
                for a in range(2):
                    for tb in range(TB):
                        if f < 4:
                            j = 2 * f + a
                            src = rot[:, tb, 2 * j:2 * j + 2].rearrange("p h a n -> p (h a n)")
                        else:
                            src = qdec[:, tb, 2 * (f - 4) + a].rearrange("p a n -> p (a n)")
                        tr = pe.transpose(ps[:, 2 + f % 2, a * T + tb * P:a * T + (tb + 1) * P], src, e.ident[:])
                tr.then_inc(turn_done, 1)
            pe.wait_ge(turn_out, FILLS)
            pe.wait_ge(state_out, 1)

            def scores(h):
                lo, pair = (h % 2) * R_DK, h // 2
                if h >= 2:
                    pe.wait_ge(att_ready, h - 1)
                for s in range(TB):
                    mm = pe.matmul(ps[:, 4 + h % 2, s * T:(s + 1) * T], turned[lo:lo + R_DK, 2 + pair // 2, pair % 2, s * P:(s + 1) * P],
                                   turned[lo:lo + R_DK, pair // 2, pair % 2, :], start=True, stop=True)
                mm.then_inc(att_done, 1)

            scores(0)
            for h in range(H):
                if h + 1 < H:
                    scores(h + 1)
                pe.wait_ge(att_ready, h + 1)
                for tb in range(TB):
                    out = ps[:, 2 * tb + h // 4, (h % 4) * P:(h % 4 + 1) * P]
                    for s in range(TB):
                        pe.matmul(out, att[:, h % 2, s, tb * P:(tb + 1) * P], e.lat[:, s, RV + h * R_DV:RV + (h + 1) * R_DV],
                                  start=(s == 0), stop=False)
                    mm = pe.matmul(out, turned[:, 4 + h // 2, h % 2, tb * P:(tb + 1) * P], state[:, h], start=False, stop=True)
                mm.then_inc(y_done, 1)


def phase_mlstm(nc, e):
    ps, io, H = e.ps, e.io, M_HEADS
    J, R = 2 * TB, 2 * M_HEADS
    with ExitStack() as ctx:
        sb = lambda name, shape: ctx.enter_context(nc.sbuf_tensor(name, shape, F32))
        sem = phase_semaphores(nc, ctx)
        causal = sb("causal", [P, TB, 2 * T])
        ltri = sb("ltri", [P, 3, P])
        pick = sb("pick", [8, 8, P])
        qT, kT = sb("mq_T", [P, H, T]), sb("mk_T", [P, H, 2 * T])
        z, u, w, lf = (sb(f"ls_gate_{n}", [P, J, R]) for n in "zuwl")
        G, us = sb("gate_sums", [P, J, R]), sb("u_cols", [P, J, R])
        urow = sb("u_rows", [R, J * P])
        mctx = sb("ctx_max", [R, 1])
        M = sb("running_max", [R, 2, T])
        em = sb("exp_minus_m", [P, TB, R])
        ew = sb("weights_exp", [P, 2, J, T])
        att = sb("m_att", [P, 2, J, T])
        den = sb("den", [P, TB, 2])
        hs = sb("m_y", [P, TB, H, M_DV])
        sq = sb("m_squares", [P, TB * H, M_DV])
        stat = sb("m_stat", [P, TB * H])
        tables, conv_in, conv_out, conv_ready, silu_out = sem("m_tables"), sem("conv_in"), sem("conv_out"), sem("conv_ready"), sem("silu_out")
        lf_ready, sums_done, u_ready, u_turned = sem("lf_ready"), sem("sums_done"), sem("u_ready"), sem("u_turned")
        max_ready, max_turned, m_ready, em_ready = sem("max_ready"), sem("max_turned"), sem("m_ready"), sem("em_ready")
        mrow_done, gap_ready, exp_ready, weight_ready = sem("mrow_done"), sem("gap_ready"), sem("exp_ready"), sem("weight_ready")
        qk_done, m_att_ready, num_done, h_ready, o_ready = sem("qk_done"), sem("m_att_ready"), sem("num_done"), sem("h_ready"), sem("o_ready")
        use = e.ls_uses + 1
        hn_use = e.hn_uses + 1
        num_bank = lambda n: 6 if n % 2 == 0 else 2
        lat_o = e.lat[:, :, MO:MO + H * M_DV]
        seq = ((2, 3, 0, 1), (3, 2, 1, 0))
        convs = [(e.lat, MQ + h * P, h, qT[:, h]) for h in range(H)]
        convs += [(e.lat, MK + h * P, H + h, kT[:, h, 0:T]) for h in range(H)]
        convs += [(e.cxt, 1536 + h * P, H + h, kT[:, h, T:2 * T]) for h in range(H)]
        block = ctx.enter_context(nc.Block())

        @block.scalar
        def _(act):
            act.dma_start(ltri[:], io["k_ltri"]).then_inc(tables, 16)
            act.dma_start(causal[:], io["k_causal"]).then_inc(tables, 16)
            act.dma_start(pick[:], io["k_pick"]).then_inc(tables, 16)
            log_sigmoid_on_scalar(act, e, use, u[:], w[:], lf[:])
            for n, (_, _, _, dst) in enumerate(convs):
                act.wait_ge(conv_ready, n + 1)
                act.activation(dst, dst, ACT.Silu).then_inc(silu_out, 1)
            act.wait_ge(m_ready, 1)
            act.activation(em[:], em[:], ACT.Exp).then_inc(em_ready, 1)
            for n in range(R):
                act.wait_ge(gap_ready, n + 1)
                act.activation(ew[:, n % 2], ew[:, n % 2], ACT.Exp, scale=-1.0).then_inc(exp_ready, 1)
            head_norm_on_scalar(act, e, hn_use, hs[:].rearrange("p b h e -> p (b h) e"), sq[:], stat[:])
            act.activation(lat_o, lat_o, ACT.Sigmoid).then_inc(o_ready, 1)

        @block.vector
        def _(dve):
            step = e.dve_step
            gates = e.gates[:].rearrange("p j (d k h) -> p j d k h", d=2, k=2)
            by_dir = lambda t: t[:].rearrange("p j (d h) -> p j d h", d=2)
            step(dve.tensor_copy(by_dir(z), gates[:, :, :, 1]))
            log_sigmoid_on_vector(dve, step, e, z[:], u[:], w[:], lf[:])
            dve.sem_inc(lf_ready, 1)
            for n, (_, _, r, dst) in enumerate(convs):
                dve.wait_ge(conv_in, n + 1)
                x = ps[:, n % 2, 0:T]
                tap = [e.cols_b[:, 32 + 8 * j + r:33 + 8 * j + r] for j in range(3)]
                step(dve.tensor_scalar(dst, x, tap[1], None, ALU.mult))
                step(dve.scalar_tensor_tensor(dst[:, 1:T], x[:, 0:T - 1], tap[0], dst[:, 1:T], ALU.mult, ALU.add))
                dve.scalar_tensor_tensor(dst[:, 0:T - 1], x[:, 1:T], tap[2], dst[:, 0:T - 1], ALU.mult,
                                         ALU.add).then_inc(conv_ready, 1)
            dve.wait_ge(sums_done, 1)
            step(dve.tensor_copy(G[:], ps[:, 2, 0:J * R].rearrange("p (j r) -> p j r", j=J)))
            dve.tensor_tensor(by_dir(us), gates[:, :, :, 0], by_dir(G), ALU.subtract).then_inc(u_ready, 1)
            dve.wait_ge(u_turned, 1)
            step(dve.tensor_copy(urow[:], ps[0:R, 3]))
            step(dve.tensor_reduce(mctx[:], urow[:, T:2 * T], AX, ALU.max))
            step(dve.tensor_scalar(mctx[:], mctx[:], 0.0, None, ALU.max))
            step(dve.tensor_tensor_scan(M[:, 0], urow[:, 0:T], urow[:, 0:T], mctx[:], ALU.max, ALU.max))
            dve.tensor_tensor_scan(M[:, 1, ::-1], urow[:, 0:T][:, ::-1], urow[:, 0:T][:, ::-1], mctx[:], ALU.max,
                                   ALU.max).then_inc(max_ready, 1)
            dve.wait_ge(max_turned, 1)
            for d in range(2):
                for tb in range(TB):
                    at = (d * TB + tb) * R + d * H
                    step(dve.tensor_tensor(em[:, tb, d * H:(d + 1) * H], G[:, tb, d * H:(d + 1) * H], ps[:, 2, 64 + at:64 + at + H],
                                           ALU.add))
            dve.tensor_scalar(em[:], em[:], -1.0, 85.0, ALU.mult, ALU.min).then_inc(m_ready, 1)
            dve.wait_ge(em_ready, 1)

            def gaps(n):
                h, d = n // 2, n % 2
                r = d * H + h
                dve.wait_ge(mrow_done, n + 1)
                if n >= 2:
                    dve.wait_ge(m_att_ready, n - 1)
                for j in range(J):
                    x = dve.tensor_scalar(ew[:, n % 2, j], ps[:, 4 + n % 2, 0:T], us[:, j, r:r + 1], 0.0, ALU.subtract, ALU.max)
                x.then_inc(gap_ready, 1)

            def weigh(n):
                dve.wait_ge(weight_ready, n + 1)
                dve.wait_ge(qk_done, n // 2 + 1)
                if n >= 2:
                    dve.wait_ge(num_done, n - 1)
                dve.scalar_tensor_tensor(att[:, n % 2].rearrange("p j t -> p (j t)"), ps[:, 0:2].rearrange("p b n -> p (b n)"),
                                         M_DK ** -0.5, ew[:, n % 2].rearrange("p j t -> p (j t)"), ALU.mult,
                                         ALU.mult).then_inc(m_att_ready, 1)

            def divide(n):
                h, d = n // 2, n % 2
                r = d * H + h
                dve.wait_ge(num_done, n + 1)
                for tb in range(TB):
                    raw_den = ps[:, num_bank(n) + tb, M_DV:M_DV + 1]
                    step(dve.tensor_scalar(den[:, tb, 0:1], raw_den, -1.0, em[:, tb, r:r + 1], ALU.mult, ALU.max))
                    step(dve.tensor_tensor(den[:, tb, 0:1], raw_den, den[:, tb, 0:1], ALU.max))
                    step(dve.reciprocal(den[:, tb, 1:2], den[:, tb, 0:1]))
                    num, rec, out = ps[:, num_bank(n) + tb, 0:M_DV], den[:, tb, 1:2], hs[:, tb, h]
                    if d == 0:
                        x = dve.tensor_scalar(out, num, rec, None, ALU.mult)
                    else:
                        x = dve.scalar_tensor_tensor(out, num, rec, out, ALU.mult, ALU.add)
                    if tb == 0:
                        step(x)
                x.then_inc(h_ready, 1)

            gaps(0)
            for n in range(R):
                if n + 1 < R:
                    gaps(n + 1)
                weigh(n)
                if n:
                    divide(n - 1)
            divide(R - 1)
            dve.wait_ge(h_ready, R)
            head_norm_on_vector(dve, step, e, hs[:].rearrange("p b h e -> p (b h) e"), sq[:], stat[:], M_DV)
            dve.wait_ge(o_ready, 1)
            step(dve.tensor_tensor(lat_o, lat_o, hs[:].rearrange("p b h e -> p b (h e)"), ALU.mult))

        @block.gpsimd
        def _(pool):
            pool.wait_ge(tables, 48)
            for n in range(R):
                pool.wait_ge(exp_ready, n + 1)
                d = n % 2
                pool.tensor_tensor(ew[:, n % 2, 0:TB], ew[:, n % 2, 0:TB], causal[:, :, d * T:(d + 1) * T],
                                   ALU.mult).then_inc(weight_ready, 1)

        @block.tensor
        def _(pe):
            for n, (src, col, _, _) in enumerate(convs):
                if n >= 2:
                    pe.wait_ge(conv_ready, n - 1)
                for tb in range(TB):
                    tr = pe.transpose(ps[:, n % 2, tb * P:(tb + 1) * P], src[:, tb, col:col + P], e.ident[:])
                tr.then_inc(conv_in, 1)
            pe.wait_ge(tables, 48)
            pe.wait_ge(lf_ready, 1)
            for d in range(2):
                for at, j in enumerate(seq[d]):
                    out = ps[:, 2, j * R + d * H:j * R + (d + 1) * H]
                    for i in seq[d][:at + 1]:
                        mm = pe.matmul(out, ltri[:, d if i == j else 2], lf[:, i, d * H:(d + 1) * H],
                                       start=(d == 0 and at == 0), stop=(i == j), skip_group_check=True)
            mm.then_inc(sums_done, 1)
            pe.wait_ge(u_ready, 1)
            for j in range(J):
                tr = pe.transpose(ps[0:R, 3, j * P:(j + 1) * P], us[:, j], e.ident[:])
            tr.then_inc(u_turned, 1)
            pe.wait_ge(max_ready, 1)
            for d in range(2):
                for tb in range(TB):
                    at = 64 + (d * TB + tb) * R
                    tr = pe.transpose(ps[:, 2, at:at + R], M[:, d, tb * P:(tb + 1) * P], e.ident[0:R, 0:R])
            tr.then_inc(max_turned, 1)
            pe.wait_ge(silu_out, len(convs))

            def max_row(n):
                h, d = n // 2, n % 2
                if n >= 2:
                    pe.wait_ge(gap_ready, n - 1)
                pe.matmul(ps[:, 4 + n % 2, 0:T], pick[:, d * H + h], M[:, d], start=True, stop=True).then_inc(mrow_done, 1)

            def scores(h):
                for j in range(J):
                    mm = pe.matmul(ps[:, j // 2, (j % 2) * T:(j % 2 + 1) * T], kT[:, h, j * P:(j + 1) * P], qT[:, h], start=True, stop=True)
                mm.then_inc(qk_done, 1)

            max_row(0)
            scores(0)
            for n in range(R):
                h, d = n // 2, n % 2
                if n + 1 < R:
                    max_row(n + 1)
                pe.wait_ge(m_att_ready, n + 1)
                if d == 1 and h + 1 < H:
                    scores(h + 1)
                if n >= 2:
                    pe.wait_ge(h_ready, n - 1)
                for tb in range(TB):
                    blocks = [j for j in range(J) if j >= TB or j == tb or (j > tb) == (d == 1)]
                    for i, j in enumerate(blocks):
                        stat_op = att[:, n % 2, j, tb * P:(tb + 1) * P]
                        v = (e.lat[:, j, MV + h * M_DV:MV + (h + 1) * M_DV] if j < TB else
                             e.cxt[:, j - TB, 2048 + h * M_DV:2048 + (h + 1) * M_DV])
                        pe.matmul(ps[:, num_bank(n) + tb, 0:M_DV], stat_op, v, start=(i == 0), stop=(i == len(blocks) - 1), skip_group_check=True)
                        mm = pe.matmul(ps[:, num_bank(n) + tb, M_DV:M_DV + 1], stat_op, ltri[:, 2, 0:1], start=False,
                                       stop=(i == len(blocks) - 1), skip_group_check=True)
                mm.then_inc(num_done, 1)


def load_tiles(sp, ring, sources, turn, skip=0):
    for n, src in enumerate(sources):
        if n >= skip:
            ring.load(sp, n % SLOTS, src, turn + n // SLOTS)


def pieces_of(first, count, turn):
    return [(n % SLOTS, turn + n // SLOTS) for n in range(first, first + count)]


def used_after(tiles, turn):
    return turn * SLOTS + tiles


class WeightSplit:
    HALF = TILE_K // 2

    def __init__(self, nc, ctx, sem, name):
        self.hi, self.lo = (ctx.enter_context(nc.sbuf_tensor(f"{name}_{part}", [P, 4, self.HALF, CG], F32R)) for part in ("hi", "lo"))
        self.hi_ready, self.first_ready, self.free = sem(f"{name}_hi_ready"), sem(f"{name}_first_ready"), sem(f"{name}_free")

    def place(self, slot, h):
        return (2 * slot + h) % 4

    def free_after(self, tiles):
        return tiles * 2 + 4

    def write_hi(self, act, ring, piece, m):
        slot, turn = piece
        ring.arrived(act, slot, turn)
        for h in range(2):
            act.wait_ge(self.free, m * 2 + (h + 1))
            act.activation(self.hi[:, self.place(slot, h)], ring.tile[:, slot, h * self.HALF:(h + 1) * self.HALF], ACT.Copy).then_inc(self.hi_ready, 1)

    def write_lo(self, pool, ring, piece, m):
        slot, _ = piece
        for h in range(2):
            at = self.place(slot, h)
            pool.wait_ge(self.hi_ready, m * 2 + (h + 1))
            pool.tensor_tensor(self.lo[:, at], ring.tile[:, slot, h * self.HALF:(h + 1) * self.HALF], self.hi[:, at],
                               ALU.subtract).then_inc(ring.used if h else self.first_ready, 1)


def gemm_split(pe, ring, split, pieces, m, lhs, banks, wait_free, tb_done):
    n = len(pieces) * TILE_K
    for t, (slot, turn) in enumerate(pieces):
        for h in range(2):
            at = split.place(slot, h)
            if h == 0:
                pe.wait_ge(split.first_ready, m + (t + 1))
            else:
                pe.wait_ge(ring.used, turn * SLOTS + (slot + 1))
            for tb, out in enumerate(banks):
                if t == 0 and h == 0:
                    wait_free(tb)
                for kk in range(split.HALF):
                    k = t * TILE_K + h * split.HALF + kk
                    (hi, lo), w_hi, w_lo = lhs(k, tb), split.hi[:, at, kk], split.lo[:, at, kk]
                    pe.matmul(out, hi, w_hi, start=(k == 0), stop=False)
                    pe.matmul(out, hi, w_lo, start=False, stop=False)
                    mm = pe.matmul(out, lo, w_hi, start=False, stop=(k == n - 1))
                if tb == len(banks) - 1:
                    mm.then_inc(split.free, 1)
                elif t == len(pieces) - 1 and h == 1:
                    mm.then_inc(tb_done, 1)


def bank_blocks(e, bank):
    return e.ps[:, bank].rearrange("p (a b t) -> p a b t", a=2, b=TB)


def phase_merge(nc, e):
    ring, ps, io, lat = e.ring, e.ps, e.io, e.lat
    with ExitStack() as ctx:
        sem = phase_semaphores(nc, ctx)
        sb = lambda name, shape, dt=F32: ctx.enter_context(nc.sbuf_tensor(name, shape, dt))
        split = WeightSplit(nc, ctx, sem, "merge_weights")
        sig = sb("gates_sigmoid", [P, 2, TB, CG])
        gt1 = sb("gt1", [P, D])
        prod = sb("merge_product", [P, TB, CG])
        x_again = sb("x_again", [P, TB, D])
        turned, hi_out, lo_out, tb_done = sem("merge_turned"), sem("merge_hi_out"), sem("merge_lo_out"), sem("merge_tb_done")
        x_in = sem("x_again_in")
        sig_ready, merged_out, gt1_in = sem("sig_ready"), sem("merged_out"), sem("gt1_in")
        prod_ready, x_out = sem("prod_ready"), sem("x_out")
        base, N = ring.turn, D // CG
        R_BLOCKS = R_HEADS * R_DV // P
        A_TILES, Y_TILES = KB // TILE_K, R_BLOCKS // TILE_K
        BRANCH = A_TILES + Y_TILES
        TILES = 2 * BRANCH
        ROUND = TILES // SLOTS
        merged = lat[:, :, MQ:MQ + D]
        source_at = lambda k: (RG if k < R_BLOCKS else MO - R_BLOCKS * P) + k * P
        y_lo = lambda k: e.cxt_split[:, k].rearrange("p (b t) -> p b t", b=TB) if k < R_BLOCKS else e.lat_split[:, :, RG + (k - R_BLOCKS) * P:][:, :, 0:P]
        hi_at = lambda k: e.lat_split[:, :, k * P:(k + 1) * P]
        m_lo = lambda k: e.lat_split[:, :, source_at(k):source_at(k) + P]
        y_split = lambda k, tb: (hi_at(k)[:, tb], y_lo(k)[:, tb])
        m_split = lambda k, tb: (hi_at(k)[:, tb], m_lo(k)[:, tb])
        FILLS = KB // 2
        in_bank = lambda fill, a: ps[:, 6 + fill % 2, a * T:(a + 1) * T].rearrange("p (b t) -> p b t", b=TB)
        w_in = io["w_in"][0]

        def sources(n):
            cols = ds(n * CG, CG)
            return ([k_tile(w_in[:, GR:GR + D], s, cols) for s in range(A_TILES)] + [k_tile(io["w_ret_out"][0], s, cols) for s in range(Y_TILES)]
                    + [k_tile(w_in[:, GM:GM + D], s, cols) for s in range(A_TILES)] + [k_tile(io["w_mlstm_out"][0], s, cols) for s in range(Y_TILES)])

        block = ctx.enter_context(nc.Block())

        @block.sync
        def _(sp):
            load_tiles(sp, ring, sources(0), base, SLOTS)
            with sp.Fori(1, N) as n:
                load_tiles(sp, ring, sources(n), n * ROUND + base)
            with sp.Fori(0, N) as n:
                load_tiles(sp, ring, turn_of(io["w_out"][0], ds(n * CG, CG)), n + (base + ROUND * N))
            load_tiles(sp, ring, turn_of(io["peer_query"][0], slice(0, CG)), base + (ROUND + 1) * N)

        @block.gpsimd
        def _(pool):
            with pool.Fori(0, N) as n:
                for m, piece in enumerate(pieces_of(0, TILES, n * ROUND + base)):
                    split.write_lo(pool, ring, piece, n * TILES + m)
            with pool.Fori(0, N) as n:
                for s, piece in enumerate(pieces_of(0, SLOTS, n + (base + ROUND * N))):
                    split.write_lo(pool, ring, piece, n * SLOTS + (N * TILES + s))

        @block.tensor
        def _(pe):
            pe.sem_inc(split.free, split.free_after(0))

            def turn(fill, source):
                if fill >= 2:
                    pe.wait_ge(lo_out, fill - 1)
                for a in range(2):
                    for tb in range(TB):
                        tr = pe.transpose(in_bank(fill, a)[:, tb], source(2 * (fill % FILLS) + a, tb), e.ident[:])
                tr.then_inc(turned, 1)

            for f in range(FILLS):
                turn(f, lambda k, tb: lat[:, tb, source_at(k):source_at(k) + P])
            pe.wait_ge(lo_out, FILLS)
            with pe.Fori(0, N) as n:
                t = n * ROUND + base
                for b in range(2):
                    at = BRANCH * b
                    gemm_split(pe, ring, split, pieces_of(at, A_TILES, t), n * TILES + at, e.h_split, [ps[:, 4 * b], ps[:, 4 * b + 1]],
                               lambda tb: pe.wait_ge(sig_ready, n * 4 + (2 * b + 1)) if tb == 0 else None, tb_done)
                    gemm_split(pe, ring, split, pieces_of(at + A_TILES, Y_TILES, t), n * TILES + (at + A_TILES),
                               lambda k, tb: y_split(R_BLOCKS * b + k, tb), [ps[:, 4 * b + 2], ps[:, 4 * b + 3]],
                               lambda tb: pe.wait_ge(merged_out, n * 4 + (2 * b + 1)) if tb == 0 else None, tb_done)
            pe.wait_ge(merged_out, 4 * N + 1)
            for f in range(FILLS):
                turn(FILLS + f, lambda k, tb: merged[:, tb, k * P:(k + 1) * P])
            pe.wait_ge(lo_out, 2 * FILLS)
            with pe.Fori(0, N) as n:
                gemm_split(pe, ring, split, pieces_of(0, SLOTS, n + (base + ROUND * N)), n * SLOTS + N * TILES, m_split, [ps[:, 0], ps[:, 1]],
                           lambda tb: pe.wait_ge(prod_ready, n * TB + (tb + 1)), tb_done)

        @block.scalar
        def _(act):
            def copy_hi(fill):
                act.wait_ge(turned, fill + 1)
                for a in range(2):
                    x = act.activation(hi_at(2 * (fill % FILLS) + a), in_bank(fill, a), ACT.Copy)
                x.then_inc(hi_out, 1)

            act.sem_inc(sig_ready, 1)
            act.dma_start(gt1[:], e.mod_rows[0, 0:D].partition_broadcast(P)).then_inc(gt1_in, 16)
            act.dma_start(x_again[:], tokens_of(io["x"][0])).then_inc(x_in, 16)
            for f in range(FILLS):
                copy_hi(f)
            with act.Fori(0, N) as n:
                pieces = pieces_of(0, TILES, n * ROUND + base)
                for b in range(2):
                    for m in range(BRANCH * b, BRANCH * (b + 1)):
                        split.write_hi(act, ring, pieces[m], n * TILES + m)
                    act.wait_ge(merged_out, n * 4 + (2 * b + 1))
                    for tb in range(TB):
                        if tb == 0:
                            act.wait_ge(tb_done, n * 4 + (2 * b + 1))
                        else:
                            act.wait_ge(split.free, n * (2 * TILES) + split.free_after(BRANCH * b + A_TILES))
                        act.activation(sig[:, b, tb], ps[:, 4 * b + tb], ACT.Sigmoid).then_inc(sig_ready, 1)
            first = base + ROUND * N
            for s in range(2):
                split.write_hi(act, ring, (s, first), N * TILES + s)
            for f in range(FILLS):
                copy_hi(FILLS + f)
            for s in range(2, SLOTS):
                split.write_hi(act, ring, (s, first), N * TILES + s)
            with act.Fori(1, N) as n:
                for s, piece in enumerate(pieces_of(0, SLOTS, n + first)):
                    split.write_hi(act, ring, piece, n * SLOTS + (N * TILES + s))

        @block.vector
        def _(dve):
            step = e.dve_step

            def copy_lo(fill, place):
                dve.wait_ge(hi_out, fill + 1)
                for a in range(2):
                    k = 2 * (fill % FILLS) + a
                    x = dve.tensor_tensor(place(k), in_bank(fill, a), hi_at(k), ALU.subtract)
                x.then_inc(lo_out, 1)

            dve.sem_inc(merged_out, 1)
            dve.sem_inc(x_out, 1)
            dve.sem_inc(prod_ready, TB)
            for f in range(FILLS):
                copy_lo(f, y_lo)
            with dve.Fori(0, N) as n:
                step.enter(n, TB)
                for b in range(2):
                    for tb in range(TB):
                        dve.wait_ge(sig_ready, n * 4 + (2 * b + tb + 2))
                        if tb == 0:
                            dve.wait_ge(tb_done, n * 4 + (2 * b + 2))
                        else:
                            dve.wait_ge(split.free, n * (2 * TILES) + split.free_after(BRANCH * (b + 1)))
                        out, y = merged[:, tb, ds(n * CG, CG)], ps[:, 4 * b + 2 + tb]
                        if b == 0:
                            dve.tensor_tensor(out, sig[:, b, tb], y, ALU.mult).then_inc(merged_out, 1)
                        else:
                            step(dve.tensor_tensor(sig[:, b, tb], sig[:, b, tb], y, ALU.mult))
                            dve.tensor_tensor(out, out, sig[:, b, tb], ALU.add).then_inc(merged_out, 1)
            step.leave(N)
            for f in range(FILLS):
                copy_lo(FILLS + f, m_lo)
            dve.wait_ge(gt1_in, 16)
            dve.wait_ge(x_in, 16)
            with dve.Fori(0, N) as n:
                cols = ds(n * CG, CG)
                for tb in range(TB):
                    if tb == 0:
                        dve.wait_ge(tb_done, n + (4 * N + 1))
                        dve.wait_ge(x_out, n * 2 + 1)
                    else:
                        dve.wait_ge(split.free, n * (2 * SLOTS) + split.free_after(N * TILES + SLOTS))
                    dve.tensor_tensor(prod[:, tb], ps[:, tb], gt1[:, cols], ALU.mult).then_inc(prod_ready, 1)
                    dve.wait_ge(prod_ready, n * TB + (tb + 1 + TB))
                    dve.tensor_tensor(e.x[:, tb, cols], x_again[:, tb, cols], prod[:, tb], ALU.add).then_inc(x_out, 1)
    ring.turn += (ROUND + 1) * N


def rms_stats_on_scalar(act, ps_row, sources, ss, rstd, squares, var_ready, root_ready):
    for j, t in enumerate(sources):
        if j:
            act.wait_ge(squares, j)
        act.activation(ps_row, t, ACT.Square, accum_out=ss[:, j:j + 1]).then_inc(squares, 1)
    act.wait_ge(var_ready, 1)
    act.activation(rstd, rstd, ACT.Sqrt).then_inc(root_ready, 1)


def rms_stats_on_vector(dve, step, count, ss, rstd, squares, var_ready, root_ready):
    dve.wait_ge(squares, count)
    dve.tensor_scalar(rstd, ss, 1.0 / D, EPS, ALU.mult, ALU.add).then_inc(var_ready, 1)
    dve.wait_ge(root_ready, 1)
    step(dve.reciprocal(rstd, rstd))


def top16(dve, step, values, scratch, best, index):
    step(dve.max(best[:, 0:8], values))
    step(dve.max_index(index[:, 0:8], best[:, 0:8], values))
    step(dve.match_replace(scratch, best[:, 0:8], values, -3.0e38))
    step(dve.max(best[:, 8:16], scratch))
    step(dve.max_index(index[:, 8:16], best[:, 8:16], scratch))


def phase_routing(nc, e):
    ring, ps, io, H, TOP = e.ring, e.ps, e.io, PEER_H, PEER_TOP
    with ExitStack() as ctx:
        sem = phase_semaphores(nc, ctx)
        sb = lambda name, shape, dt=F32: ctx.enter_context(nc.sbuf_tensor(name, shape, dt))
        scale2, shift2 = sb("scale2", [P, D]), sb("shift2", [P, D])
        g2 = sb("norm2_row", [P, D])
        ss, rstd = sb("ss2", [P, TB]), sb("rstd2", [P, TB])
        keys, keysT = sb("keys", [P, HP, P]), sb("keys_T", [P, HP, P])
        base, N = ring.turn, HP * PEER_K // CG
        NB, NH = CG // P, CG // P // 2
        qT = sb("peer_q_T", [P, NB, T])
        scores = sb("key_scores", [P, TB, NB, PEER_K])
        top_now = sb("key_top", [P, TB, NB, TOP])
        left = sb("scores_left", [P, T])
        top_at = sb("key_top_at", [P, TB, HP, TOP], U32)
        top_key = sb("key_top_number", [P, TB, HP, TOP])
        pairs = sb("pair_scores", [P, NH, TOP * TOP])
        best, best_at = sb("pair_top", [P, TB, H, TOP]), sb("pair_top_at", [P, TB, H, TOP], U32)
        half = sb("pair_half", [P, 2, PICKS], U32)
        half_f = sb("pair_half_f", [P, 2, PICKS])
        hot = sb("pair_one_hot", [P, PICKS, TOP])
        key_of = sb("picked_key", [P, 2, PICKS])
        iota16 = sb("iota16", [P, TOP])
        total = sb("softmax_sum", [P, TB * H])
        rows_in, keys_in, iota_in = sem("rows2_in"), sem("keys_in"), sem("iota_in")
        squares, var_ready, root_ready = sem("squares2"), sem("var2_ready"), sem("root2_ready")
        h2_ready, turned, turned_out = sem("h2_ready"), sem("h2_turned"), sem("h2_turned_out")
        q_done, q_out, s_done, s_out = sem("q_done"), sem("q_out"), sem("s_done"), sem("s_out")
        shifted, exp_done = sem("softmax_shifted"), sem("softmax_exp")
        top_done = sem("top_done")
        FILLS = KB // 2 + HP // 4
        block = ctx.enter_context(nc.Block())

        @block.sync
        def _(sp):
            with sp.Fori(1, N) as n:
                load_tiles(sp, ring, turn_of(io["peer_query"][0], ds(n * CG, CG)), n + base)
            load_tiles(sp, ring, turn_of(io["w_mem_kv_2"][0], slice(0, CG)), base + N)

        @block.scalar
        def _(act):
            act.dma_start(shift2[:], e.mod_rows[0, D:2 * D].partition_broadcast(P)).then_inc(rows_in, 16)
            act.dma_start(scale2[:], e.mod_rows[0, 2 * D:3 * D].partition_broadcast(P)).then_inc(rows_in, 16)
            act.dma_start(g2[:], io["norm2_g"][0].partition_broadcast(P)).then_inc(rows_in, 16)
            act.dma_start(keys[:], io["peer_keys"][0].rearrange("h a k d -> k (h a) d")).then_inc(keys_in, 16)
            act.dma_start(iota16[:], io["k_iota16"]).then_inc(iota_in, 16)
            rms_stats_on_scalar(act, ps[:, 0:4].rearrange("p b n -> p (b n)"), [e.x[:, 0], e.x[:, 1]], ss, rstd[:], squares,
                                var_ready, root_ready)
            for f in range(FILLS):
                act.wait_ge(turned, f + 1)
                if f < HP // 4:
                    act.activation(keysT[:, 4 * f:4 * f + 4].rearrange("p a k -> p (a k)"), ps[:, 4 + f % 2], ACT.Copy).then_inc(turned_out, 1)
                else:
                    g = f - HP // 4
                    act.activation(e.hT[:, 2 * g:2 * g + 2].rearrange("p a t -> p (a t)"), ps[:, 4 + f % 2], ACT.Copy).then_inc(turned_out, 1)
            act.sem_inc(s_out, 1)
            with act.Fori(0, N) as n:
                for nb in range(NB):
                    if nb < NB - 1:
                        act.wait_ge(q_done, n * (NB - 1) + (nb + 1))
                    else:
                        act.wait_ge(ring.used, n * SLOTS + used_after(SLOTS, base))
                    act.activation(qT[:, nb], ps[:, nb, 0:T], ACT.Copy).then_inc(q_out, 1)
                for tb in range(TB):
                    act.wait_ge(s_done, n * TB + (tb + 1))
                    act.wait_ge(top_done, n * TB + (tb + 1))
                    act.activation(scores[:, tb].rearrange("p a k -> p (a k)"), ps[:, 4 + tb], ACT.Copy).then_inc(s_out, 1)
            act.wait_ge(shifted, 1)
            act.activation(e.weight[:], e.weight[:], ACT.Exp).then_inc(exp_done, 1)

        @block.vector
        def _(dve):
            step = e.dve_step
            rms_stats_on_vector(dve, step, TB, ss[:], rstd[:], squares, var_ready, root_ready)
            dve.wait_ge(rows_in, 48)
            step(dve.scalar_tensor_tensor(scale2[:], scale2[:], 1.0, g2[:], ALU.add, ALU.mult))
            for tb in range(TB):
                step(dve.scalar_tensor_tensor(e.h2[:, tb], e.x[:, tb], rstd[:, tb:tb + 1], scale2[:], ALU.mult, ALU.mult))
                dve.tensor_tensor(e.h2[:, tb], e.h2[:, tb], shift2[:], ALU.add).then_inc(h2_ready, 1)
            dve.sem_inc(top_done, TB)
            for n in range(N):
                for tb in range(TB):
                    dve.wait_ge(s_out, n * TB + tb + 2)
                    lists, heads = range(n * NB, (n + 1) * NB), range(n * NH, (n + 1) * NH)
                    for nb, hp in enumerate(lists):
                        top16(dve, step, scores[:, tb, nb], left[:, 0:PEER_K], top_now[:, tb, nb], top_at[:, tb, hp])
                    dve.sem_inc(top_done, 1)
                    two = top_now[:, tb].rearrange("p (h a) k -> p h a k", a=2)
                    wide = [P, NH, TOP, TOP]
                    step(dve.tensor_tensor(pairs[:].rearrange("p h (i j) -> p h i j", i=TOP), two[:, :, 0].unsqueeze(3).to_broadcast(wide),
                                           two[:, :, 1].unsqueeze(2).to_broadcast(wide), ALU.add))
                    for j, h in enumerate(heads):
                        top16(dve, step, pairs[:, j], left[:], best[:, tb, h], best_at[:, tb, h])
            step(dve.tensor_copy(top_key[:], top_at[:]))
            dve.wait_ge(iota_in, 16)
            for tb in range(TB):
                at = best_at[:, tb].rearrange("p h k -> p (h k)")
                step(dve.tensor_scalar(half[:, 0], at, 4, None, ALU.logical_shift_right))
                step(dve.tensor_scalar(half[:, 1], at, TOP - 1, None, ALU.bitwise_and))
                step(dve.tensor_copy(half_f[:], half[:]))
                numbers = top_key[:, tb].rearrange("p (h a) k -> p h a k", a=2)
                for a in range(2):
                    flat = [P, PICKS, TOP]
                    step(dve.tensor_tensor(hot[:], iota16[:].unsqueeze(1).to_broadcast(flat), half_f[:, a].unsqueeze(2).to_broadcast(flat),
                                           ALU.is_equal))
                    by_head = hot[:].rearrange("p (h s) k -> p h s k", h=H)
                    step(dve.tensor_tensor(by_head, by_head, numbers[:, :, a].unsqueeze(2).to_broadcast([P, H, TOP, TOP]), ALU.mult))
                    step(dve.tensor_reduce(key_of[:, a], hot[:], AX, ALU.add))
                step(dve.scalar_tensor_tensor(key_of[:, 0], key_of[:, 0], float(PEER_K), key_of[:, 1], ALU.mult, ALU.add))
                for rep in range(2):
                    step(dve.tensor_copy(e.expert[:, (rep * TB + tb) * PICKS:(rep * TB + tb + 1) * PICKS], key_of[:, 0]))
            step(dve.memset(e.expert[:, 2 * TB * PICKS:], 0))
            w = e.weight[:].rearrange("p (g k) -> p g k", k=TOP)
            g = best[:].rearrange("p b h k -> p (b h) k")
            n_groups = TB * H
            dve.tensor_tensor(w, g, g[:, :, 0:1].to_broadcast([P, n_groups, TOP]), ALU.subtract).then_inc(shifted, 1)
            dve.wait_ge(exp_done, 1)
            step(dve.tensor_reduce(total[:], w, AX, ALU.add))
            step(dve.reciprocal(total[:], total[:]))
            step(dve.tensor_tensor(w, w, total[:].unsqueeze(2).to_broadcast([P, n_groups, TOP]), ALU.mult))

        @block.tensor
        def _(pe):
            pe.wait_ge(keys_in, 16)
            for f in range(FILLS):
                if f >= 2:
                    pe.wait_ge(turned_out, f - 1)
                if f == HP // 4:
                    pe.wait_ge(h2_ready, TB)
                for a in range(4):
                    if f < HP // 4:
                        src = keys[:, 4 * f + a]
                    else:
                        src = e.h2[:, a % 2, (2 * (f - HP // 4) + a // 2) * P:][:, 0:P]
                    tr = pe.transpose(ps[:, 4 + f % 2, a * P:(a + 1) * P], src, e.ident[:])
                tr.then_inc(turned, 1)
            pe.wait_ge(turned_out, FILLS)
            with pe.Fori(0, N) as n:
                for nb in range(NB):
                    for s in range(SLOTS):
                        if nb == 0:
                            ring.arrived(pe, s, n + base)
                        for kk in range(TILE_K):
                            k = s * TILE_K + kk
                            mm = pe.matmul(ps[:, nb, 0:T], ring.tile[:, s, kk, nb * P:(nb + 1) * P], e.hT[:, k], start=(k == 0), stop=(k == KB - 1))
                        if nb == NB - 1:
                            mm.then_inc(ring.used, 1)
                    if nb < NB - 1:
                        mm.then_inc(q_done, 1)
                pe.wait_ge(q_out, n * NB + NB)
                pe.wait_ge(s_out, n * TB + 1)
                for tb in range(TB):
                    for nb in range(NB):
                        mm = pe.matmul(ps[:, 4 + tb, nb * P:(nb + 1) * P], qT[:, nb, tb * P:(tb + 1) * P],
                                       keysT[:, ds(n * NB + nb, 1)].rearrange("p a k -> p (a k)"), start=True, stop=True)
                    mm.then_inc(s_done, 1)
    ring.turn += N


def phase_experts(nc, e):
    ring, ps, io = e.ring, e.ps, e.io
    with ExitStack() as ctx:
        sem = phase_semaphores(nc, ctx)
        sb = lambda name, shape, dt=F32: ctx.enter_context(nc.sbuf_tensor(name, shape, dt))
        GROUP, GROUPS = 4, 2
        RING = GROUP * GROUPS
        rows = sb("expert_rows", [P, RING, D])
        number = sb("expert_numbers", [P, GROUPS, GROUP], U32)
        dots = sb("expert_dots", [P, TB * PICKS])
        few = sb("expert_few", [P, RING])
        acc = sb("expert_sum", [P, TB, D])
        gt2, final_g = sb("gt2", [P, D]), sb("final_g_row", [P, D])
        ss, rstd = sb("ss3", [P, TB]), sb("rstd3", [P, TB])
        landed = [sem(f"expert_landed{s}") for s in range(RING)]
        number_ready, row_free, go, dots_ready, gelu_done = sem("number_ready"), sem("row_free"), sem("gather_go"), sem("dots_ready"), sem("gelu_done")
        rows_in, squares, var_ready, root_ready, x2_ready = sem("rows3_in"), sem("squares3"), sem("var3_ready"), sem("root3_ready"), sem("x2_ready")
        ROUNDS = PICKS // RING
        mem, mem_ss, mem_rstd = sb("mem_tokens", [P, TB, D]), sb("mem_ss", [P, TB]), sb("mem_rstd", [P, TB])
        memT, N_KV, base = e.hT, 2 * MEM_W // CG, ring.turn
        mem_in, mem_squares, mem_var, mem_root = sem("mem_in"), sem("mem_squares"), sem("mem_var"), sem("mem_root")
        mem_inverse, mem_normed, mem_turned, mem_turned_out = sem("mem_inverse"), sem("mem_normed"), sem("mem_turned"), sem("mem_turned_out")
        kv_tb_done, kv_out = sem("kv_tb_done"), sem("kv_out")
        block = ctx.enter_context(nc.Block())

        @block.sync
        def _(sp):
            for n in range(1, N_KV):
                load_tiles(sp, ring, turn_of(io["w_mem_kv_2"][0], slice(n * CG, (n + 1) * CG)), base + n)
            load_tiles(sp, ring, turn_of(io["w_in_2"][0], slice(0, CG)), base + N_KV)

        @block.tensor
        def _(pe):
            pe.wait_ge(mem_normed, TB)
            for k in range(KB):
                if k >= 2:
                    pe.wait_ge(mem_turned_out, k - 1)
                for tb in range(TB):
                    tr = pe.transpose(ps[:, 4 + k % 2, tb * P:(tb + 1) * P], mem[:, tb, k * P:(k + 1) * P], e.ident[:])
                tr.then_inc(mem_turned, 1)
            pe.wait_ge(mem_turned_out, KB)
            for n in range(N_KV):
                gemm_token_major(pe, ring, pieces_of(0, SLOTS, base + n), lambda k, tb: memT[:, k, tb * P:(tb + 1) * P],
                                 [ps[:, 2 * n], ps[:, 2 * n + 1]], lambda tb: None, kv_tb_done)

        @block.gpsimd
        def _(pool):
            for table, src in enumerate((io["peer_down"][0], io["peer_up"][0])):
                first = table * TB * ROUNDS
                with pool.Fori(0, TB * ROUNDS) as i:
                    for p in range(GROUPS):
                        pool.wait_ge(number_ready, i * GROUPS + (first * GROUPS + p + 1))
                        for j in range(GROUP):
                            s = p * GROUP + j
                            pool.wait_ge(row_free, i * RING + (first * RING + s + 1))
                            pool.sem_inc(go, 1)
                            pool.indirect_dma_start(rows[:, s], None, src, bass.IndirectOffsetOnAxis(ap=number[:, p, j:j + 1], axis=0)).then_inc(landed[s], 16)

        @block.vector
        def _(dve):
            step = e.dve_step
            step(dve.memset(acc[:].rearrange("p b d -> p (b d)"), 0.0))
            for p in range(GROUPS):
                dve.tensor_copy(number[:, p], e.expert[:, p * GROUP:(p + 1) * GROUP]).then_inc(number_ready, 1)
            dve.sem_inc(row_free, RING)

            def next_numbers(i, p, first):
                dve.tensor_scalar(number[:, p], e.expert[:, ds((i + (first + 1)) * RING + p * GROUP, GROUP)], 0, None,
                                  ALU.bitwise_or).then_inc(number_ready, 1)

            for tb in range(TB):
                first = tb * ROUNDS
                with dve.Fori(0, ROUNDS) as i:
                    for p in range(GROUPS):
                        for j in range(GROUP):
                            s = p * GROUP + j
                            dve.wait_ge(landed[s], (i + (first + 1)) * 16)
                            dve.tensor_tensor_reduce(rows[:, s], rows[:, s], e.h2[:, tb], 1.0, 0.0, ALU.mult, ALU.add,
                                                     few[:, s:s + 1]).then_inc(row_free, 1)
                        next_numbers(i, p, first)
                    dve.wait_ge(row_free, (i + (first + 2)) * RING)
                    dve.tensor_scalar(dots[:, ds((i + first) * RING, RING)], few[:], 1.0, None, ALU.mult).then_inc(dots_ready, 1)
                    dve.wait_ge(dots_ready, i + (first + 1))
                if tb == 0:
                    dve.wait_ge(mem_squares, TB)
                    dve.tensor_scalar(mem_rstd[:], mem_ss[:], 1.0 / D, EPS, ALU.mult, ALU.add).then_inc(mem_var, 1)
                    dve.wait_ge(mem_root, 1)
                    dve.reciprocal(mem_rstd[:], mem_rstd[:]).then_inc(mem_inverse, 1)
            dve.wait_ge(gelu_done, 1)
            step(dve.tensor_tensor(dots[:], dots[:], e.weight[:], ALU.mult))
            for tb in range(TB):
                first = (TB + tb) * ROUNDS
                with dve.Fori(0, ROUNDS) as i:
                    step.enter(i, 1)
                    step(dve.tensor_scalar(few[:], dots[:, ds((i + tb * ROUNDS) * RING, RING)], 1.0, None, ALU.mult))
                    for p in range(GROUPS):
                        for j in range(GROUP):
                            s = p * GROUP + j
                            dve.wait_ge(landed[s], (i + (first + 1)) * 16)
                            dve.scalar_tensor_tensor(acc[:, tb], rows[:, s], few[:, s:s + 1], acc[:, tb], ALU.mult, ALU.add).then_inc(row_free, 1)
                            dve.wait_ge(row_free, i * RING + ((first + 1) * RING + s + 1))
                        next_numbers(i, p, first)
                step.leave(ROUNDS)
            dve.wait_ge(rows_in, 32)
            for tb in range(TB):
                step(dve.tensor_tensor(acc[:, tb], acc[:, tb], gt2[:], ALU.mult))
                dve.tensor_tensor(e.x[:, tb], e.x[:, tb], acc[:, tb], ALU.add).then_inc(x2_ready, 1)
            rms_stats_on_vector(dve, step, TB, ss[:], rstd[:], squares, var_ready, root_ready)
            for tb in range(TB):
                step(dve.scalar_tensor_tensor(e.x[:, tb], e.x[:, tb], rstd[:, tb:tb + 1], final_g[:], ALU.mult, ALU.mult))

        @block.scalar
        def _(act):
            act.dma_start(gt2[:], e.mod_rows[0, 3 * D:4 * D].partition_broadcast(P)).then_inc(rows_in, 16)
            act.dma_start(final_g[:], io["final_g"].partition_broadcast(P)).then_inc(rows_in, 16)
            act.dma_start(mem[:], tokens_of(io["mem_2"][0])).then_inc(mem_in, 16)
            act.wait_ge(mem_in, 16)
            rms_stats_on_scalar(act, ps[:, 0:4].rearrange("p b n -> p (b n)"), [mem[:, 0], mem[:, 1]], mem_ss, mem_rstd[:],
                                mem_squares, mem_var, mem_root)
            act.wait_ge(mem_inverse, 1)
            for tb in range(TB):
                act.activation(mem[:, tb], mem[:, tb], ACT.Copy, scale=mem_rstd[:, tb:tb + 1]).then_inc(mem_normed, 1)
            for k in range(KB):
                act.wait_ge(mem_turned, k + 1)
                act.activation(memT[:, k], ps[:, 4 + k % 2, 0:T], ACT.Copy, scale=e.cols_b[:, 72 + k:73 + k]).then_inc(mem_turned_out, 1)
            for n in range(N_KV):
                for tb in range(TB):
                    if tb == 0:
                        act.wait_ge(kv_tb_done, n + 1)
                    else:
                        act.wait_ge(ring.used, used_after((n + 1) * SLOTS, base))
                    act.activation(e.kv[:, tb, n * CG:(n + 1) * CG], ps[:, 2 * n + tb], ACT.Copy).then_inc(kv_out, 1)
            act.wait_ge(dots_ready, TB * ROUNDS)
            act.activation(dots[:], dots[:], ACT.Gelu).then_inc(gelu_done, 1)
            act.wait_ge(kv_out, N_KV * TB)
            act.wait_ge(x2_ready, TB)
            rms_stats_on_scalar(act, ps[:, 0:4].rearrange("p b n -> p (b n)"), [e.x[:, 0], e.x[:, 1]], ss, rstd[:], squares,
                                var_ready, root_ready)
    ring.turn += N_KV


def phase_second_projection(nc, e):
    ring, ps, io = e.ring, e.ps, e.io
    with ExitStack() as ctx:
        sem = phase_semaphores(nc, ctx)
        sb = lambda name, shape: ctx.enter_context(nc.sbuf_tensor(name, shape, F32))
        split = WeightSplit(nc, ctx, sem, "in2_weights")
        xn = e.p2[:, :, 0:D]
        w_lr = sb("w_lr", [P, KB, 16])
        hT = sb("lr_h_T", [P, 2, T])
        ss, rstd = sb("ss4", [P, TB]), sb("rstd4", [P, TB])
        lr_in, squares, var_ready, root_ready, x_kept = sem("lr_in"), sem("squares4"), sem("var4_ready"), sem("root4_ready"), sem("x_kept")
        normed, turned, lo_out, h_out = sem("normed"), sem("in2_turned"), sem("in2_lo_out"), sem("in2_h_out")
        tb_done, bank_free, lr_done, lr_used = sem("in2_tb_done"), sem("in2_bank_free"), sem("lr_done"), sem("lr_used")
        base = ring.turn
        w_in = io["w_in_2"][0]
        runs = ((0, C_LR // CG), (MEMQ, (G_LOGIT - MEMQ) // CG))
        n_turns = sum(n for _, n in runs)
        block = ctx.enter_context(nc.Block())

        @block.sync
        def _(sp):
            sp.dma_start(e.x_rows, e.x[:]).then_inc(x_kept, 16)
            turn = base
            for first, n in runs:
                with sp.Fori(1 if turn == base else 0, n) as i:
                    load_tiles(sp, ring, turn_of(w_in[:, first:first + n * CG], ds(i * CG, CG)), i + turn)
                turn += n
            load_tiles(sp, ring, turn_of(w_in, slice(G_LOGIT, G_LOGIT + CG)), turn)
            sp.wait_ge(x_kept, 16)

        @block.gpsimd
        def _(pool):
            pool.dma_start(w_lr[:], w_in[:, C_LR:MEMQ].rearrange("(k p) n -> p k n", p=P)).then_inc(lr_in, 16)
            turn = base
            for _, n in runs:
                with pool.Fori(0, n) as i:
                    for s in range(SLOTS):
                        split.write_lo(pool, ring, (s, i + turn), i * SLOTS + ((turn - base) * SLOTS + s))
                turn += n

        @block.scalar
        def _(act):
            rms_stats_on_scalar(act, ps[:, 0:4].rearrange("p b n -> p (b n)"), [e.x[:, 0], e.x[:, 1]], ss, rstd[:], squares, var_ready, root_ready)
            for k in range(KB):
                act.wait_ge(turned, k + 1)
                gain = e.cols_b[:, 56 + k:57 + k]
                act.activation(e.hT_hi[:, k], ps[:, 4 + k % 2, 0:T], ACT.Copy, scale=gain)
                if k >= 2:
                    act.wait_ge(lr_used, k - 1)
                act.activation(hT[:, k % 2], ps[:, 4 + k % 2, 0:T], ACT.Copy, scale=gain).then_inc(h_out, 1)
            turn = base
            for _, n in runs:
                with act.Fori(0, n) as i:
                    for s in range(SLOTS):
                        split.write_hi(act, ring, (s, i + turn), i * SLOTS + ((turn - base) * SLOTS + s))
                turn += n

        @block.vector
        def _(dve):
            step = e.dve_step
            dve.sem_inc(bank_free, TB)
            rms_stats_on_vector(dve, step, TB, ss[:], rstd[:], squares, var_ready, root_ready)
            for tb in range(TB):
                dve.tensor_scalar(xn[:, tb], e.x[:, tb], rstd[:, tb:tb + 1], None, ALU.mult).then_inc(normed, 1)
            dve.wait_ge(normed, TB)
            dve.wait_ge(x_kept, 16)
            for k in range(KB):
                dve.wait_ge(h_out, k + 1)
                dve.scalar_tensor_tensor(e.hT_lo[:, k], ps[:, 4 + k % 2, 0:T], e.cols_b[:, 56 + k:57 + k], e.hT_hi[:, k],
                                         ALU.mult, ALU.subtract).then_inc(lo_out, 1)
            dve.wait_ge(lr_done, 1)
            step(dve.tensor_copy(e.lrT[:], ps[0:16, 2, 0:T]))
            turn, done = base, 0
            for first, n in runs:
                with dve.Fori(0, n) as i:
                    for tb in range(TB):
                        if tb == 0:
                            dve.wait_ge(tb_done, i + (done + 1))
                        else:
                            dve.wait_ge(split.free, i * (2 * SLOTS) + split.free_after((done + 1) * SLOTS))
                        dve.tensor_scalar(e.p2[:, tb, ds(i * CG + first, CG)], ps[:, tb], 1.0, None, ALU.mult).then_inc(bank_free, 1)
                done += n

        @block.tensor
        def _(pe):
            pe.sem_inc(split.free, split.free_after(0))
            pe.wait_ge(normed, TB)
            pe.wait_ge(lr_in, 16)

            def low_rank(k):
                pe.wait_ge(h_out, k + 1)
                return pe.matmul(ps[0:16, 2, 0:T], w_lr[:, k], hT[:, k % 2], start=(k == 0), stop=(k == KB - 1))

            for k in range(KB):
                if k >= 2:
                    pe.wait_ge(h_out, k - 1)
                    pe.wait_ge(lo_out, k - 1)
                for tb in range(TB):
                    tr = pe.transpose(ps[:, 4 + k % 2, tb * P:(tb + 1) * P], xn[:, tb, k * P:(k + 1) * P], e.ident[:])
                tr.then_inc(turned, 1)
                if k >= 1:
                    low_rank(k - 1).then_inc(lr_used, 1)
            low_rank(KB - 1).then_inc(lr_done, 1)
            pe.wait_ge(lo_out, KB)
            turn, uses = base, 0
            for _, n in runs:
                with pe.Fori(0, n) as i:
                    gemm_split(pe, ring, split, pieces_of(0, SLOTS, i + turn), i * SLOTS + (turn - base) * SLOTS, e.h_split, [ps[:, 0], ps[:, 1]],
                               lambda tb: pe.wait_ge(bank_free, i * TB + (uses + tb + 1)), tb_done)
                turn, uses = turn + n, uses + n * TB
    ring.turn += n_turns


def phase_pool(nc, e):
    ps, io, p2 = e.ps, e.io, e.p2
    with ExitStack() as ctx:
        sem = phase_semaphores(nc, ctx)
        sb = lambda name, shape: ctx.enter_context(nc.sbuf_tensor(name, shape, F32))
        G, W = len(POOL_WINDOWS), 2 * P
        windows, w_pool = sb("windows", [P, TB, G * T]), sb("w_pool", [P, 2 * G, W])
        scale = sb("pool_scale_row", [P, G * W])
        pooledT = sb("pooled_T", [P, 2 * G, T])
        mixed = sb("pool_mixed", [P, TB, G * W])
        tables, pooled, pooled_out, mix_done, gate_ready = sem("pool_tables"), sem("pooled"), sem("pooled_out"), sem("mix_done"), sem("pool_gate")
        gate = p2[:, :, A_GATE:A_GATE + G * W]
        block = ctx.enter_context(nc.Block())

        @block.scalar
        def _(act):
            act.dma_start(windows[:], io["k_pool"]).then_inc(tables, 16)
            act.dma_start(w_pool[:], io["w_pool_2"][0].rearrange("g (b c) d -> c (g b) d", c=P)).then_inc(tables, 16)
            act.dma_start(scale[:], io["pool_scale_2"][0].partition_broadcast(P)).then_inc(tables, 16)
            act.activation(gate, gate, ACT.Silu).then_inc(gate_ready, 1)
            for g in range(G):
                act.wait_ge(pooled, g + 1)
                act.activation(pooledT[:, 2 * g:2 * g + 2].rearrange("p a t -> p (a t)"), ps[:, g], ACT.Copy).then_inc(pooled_out, 1)

        @block.tensor
        def _(pe):
            pe.wait_ge(tables, 48)
            for g in range(G):
                for cb in range(2):
                    at = A_VAL + (2 * g + cb) * P
                    for tb in range(TB):
                        mm = pe.matmul(ps[:, g, cb * T:(cb + 1) * T], p2[:, tb, at:at + P], windows[:, tb, g * T:(g + 1) * T],
                                       start=(tb == 0), stop=(tb == TB - 1))
                mm.then_inc(pooled, 1)
            pe.wait_ge(pooled_out, G)
            for tb in range(TB):
                for g in range(G):
                    for cb in range(2):
                        mm = pe.matmul(ps[:, 4 + 2 * tb + g // 2, (g % 2) * W:(g % 2 + 1) * W], pooledT[:, 2 * g + cb, tb * P:(tb + 1) * P],
                                       w_pool[:, 2 * g + cb], start=(cb == 0), stop=(cb == 1))
                mm.then_inc(mix_done, 1)

        @block.vector
        def _(dve):
            step = e.dve_step
            dve.wait_ge(tables, 48)
            dve.wait_ge(gate_ready, 1)
            for tb in range(TB):
                dve.wait_ge(mix_done, tb + 1)
                step(dve.tensor_tensor(mixed[:, tb], ps[:, 4 + 2 * tb:6 + 2 * tb].rearrange("p b n -> p (b n)"), scale[:], ALU.mult))
                step(dve.tensor_tensor(gate[:, tb], gate[:, tb], mixed[:, tb], ALU.mult))


def phase_attention(nc, e):
    ps, io, p2 = e.ps, e.io, e.p2
    with ExitStack() as ctx:
        sem = phase_semaphores(nc, ctx)
        sb = lambda name, shape: ctx.enter_context(nc.sbuf_tensor(name, shape, F32))
        NG, PER, NM = len(SWA_CFG), 4, 4
        NSWA = NG * PER
        NH = NSWA + NM
        dist = sb("dist", [P, TB, NG * T])
        bias = sb("att_bias", [P, 2, TB, T])
        qk = sb("att_qk_T", [P, 2, 2 * T])
        sc, ex, exT = sb("att_scores", [P, 2, TB, T]), sb("att_exp", [P, 2, TB, T]), sb("att_exp_T", [P, 2, TB, T])
        top, neg = sb("att_max", [P, NH, TB]), sb("att_neg_max", [P, NH, TB])
        den = sb("att_den", [P, NH, TB])
        o = sb("att_out", [P, TB, NH, P])
        lse, mx, wt, tot = sb("lse", [P, NSWA, TB]), sb("lse_max", [P, PER, TB]), sb("lse_weight", [P, NSWA, TB]), sb("lse_sum", [P, PER, TB])
        tables, bias_ready, qk_done, qk_out, s_done, sc_ready = sem("dist_in"), sem("bias_ready"), sem("qk_turned"), sem("qk_out"), sem("att_s_done"), sem("sc_ready")
        neg_ready, exp_ready, ex_turned, ex_out, o_done, o_out = sem("neg_ready"), sem("att_exp_ready"), sem("ex_turned"), sem("ex_out"), sem("att_o_done"), sem("att_o_out")
        ln_done, shifted, wt_exp, gates_ready = sem("lse_ln"), sem("lse_shifted"), sem("lse_exp"), sem("att_gates")
        SCALE = float(P) ** -0.5
        slope = [2.0 ** (-8.0 * (h + 1.0) / NSWA) for h in range(NSWA)]
        s_gate, m_gate = p2[:, :, S_GATE:S_GATE + PER * P], p2[:, :, MEM_GATE:MEM_GATE + NM * P]
        q_at = lambda n: (SQ + n * P) if n < NSWA else MEMQ + (n - NSWA) * P
        key = lambda n, b: p2[:, b, SK + n * P:SK + (n + 1) * P] if n < NSWA else e.kv[:, b, (n - NSWA) * P:(n - NSWA + 1) * P]
        value = lambda n, b: p2[:, b, SV + n * P:SV + (n + 1) * P] if n < NSWA else e.kv[:, b, 512 + (n - NSWA) * P:512 + (n - NSWA + 1) * P]
        block = ctx.enter_context(nc.Block())

        @block.gpsimd
        def _(pool):
            pool.wait_ge(tables, 16)
            for n in range(NSWA):
                if n >= 2:
                    pool.wait_ge(sc_ready, n - 1)
                pool.tensor_scalar(bias[:, n % 2], dist[:, :, (n // PER) * T:(n // PER + 1) * T], -slope[n], None, ALU.mult).then_inc(bias_ready, 1)

        @block.scalar
        def _(act):
            act.dma_start(dist[:], io["k_dist"]).then_inc(tables, 16)
            act.activation(s_gate, s_gate, ACT.Silu).then_inc(gates_ready, 1)
            act.activation(m_gate, m_gate, ACT.Silu).then_inc(gates_ready, 1)

            def copy_qk(n):
                act.wait_ge(qk_done, n + 1)
                if n >= 2:
                    act.wait_ge(s_done, n - 1)
                act.activation(qk[:, n % 2], ps[:, n % 2], ACT.Copy).then_inc(qk_out, 1)

            def copy_o(n):
                act.wait_ge(o_done, n + 1)
                act.activation(o[:, :, n], ps[:, 6 + n % 2, 0:T].rearrange("p (b c) -> p b c", b=TB), ACT.Copy).then_inc(o_out, 1)

            copy_qk(0)
            for n in range(NH):
                if n + 1 < NH:
                    copy_qk(n + 1)
                act.wait_ge(neg_ready, n + 1)
                if n >= 2:
                    act.wait_ge(ex_turned, n - 1)
                for tb in range(TB):
                    act.activation(ex[:, n % 2, tb], sc[:, n % 2, tb], ACT.Exp, bias=neg[:, n, tb:tb + 1],
                                   accum_out=den[:, n, tb:tb + 1]).then_inc(exp_ready, 1)
                act.wait_ge(ex_turned, n + 1)
                if n >= 2:
                    act.wait_ge(o_done, n - 1)
                act.activation(exT[:, n % 2].rearrange("p s t -> p (s t)"), ps[:, 4 + n % 2], ACT.Copy).then_inc(ex_out, 1)
                if n >= 1:
                    copy_o(n - 1)
            copy_o(NH - 1)
            act.wait_ge(o_out, NH)
            act.activation(lse[:], den[:, 0:NSWA], ACT.Ln).then_inc(ln_done, 1)
            act.wait_ge(shifted, 1)
            act.activation(wt[:], wt[:], ACT.Exp).then_inc(wt_exp, 1)

        @block.vector
        def _(dve):
            step = e.dve_step
            for n in range(NH):
                dve.wait_ge(s_done, n + 1)
                if n >= 2:
                    dve.wait_ge(exp_ready, 2 * (n - 1))
                flat = sc[:, n % 2].rearrange("p b s -> p (b s)")
                if n < NSWA:
                    dve.wait_ge(bias_ready, n + 1)
                    x = dve.scalar_tensor_tensor(flat, ps[:, 2 + n % 2], SCALE, bias[:, n % 2].rearrange("p b s -> p (b s)"), ALU.mult, ALU.add)
                else:
                    x = dve.tensor_scalar(flat, ps[:, 2 + n % 2], SCALE, None, ALU.mult)
                x.then_inc(sc_ready, 1)
                dve.wait_ge(sc_ready, n + 1)
                step(dve.tensor_reduce(top[:, n], sc[:, n % 2], AX, ALU.max))
                dve.tensor_scalar(neg[:, n], top[:, n], -1.0, None, ALU.mult).then_inc(neg_ready, 1)
            dve.wait_ge(ln_done, 1)
            grouped = lambda t: t[:].rearrange("p (g h) b -> p g h b", g=NG)
            step(dve.tensor_tensor(lse[:], lse[:], top[:, 0:NSWA], ALU.add))
            step(dve.tensor_tensor(mx[:], grouped(lse)[:, 0], grouped(lse)[:, 1], ALU.max))
            step(dve.tensor_tensor(mx[:], mx[:], grouped(lse)[:, 2], ALU.max))
            for g in range(NG):
                x = dve.tensor_tensor(grouped(wt)[:, g], grouped(lse)[:, g], mx[:], ALU.subtract)
                if g < NG - 1:
                    step(x)
            x.then_inc(shifted, 1)
            dve.wait_ge(wt_exp, 1)
            step(dve.tensor_tensor(tot[:], grouped(wt)[:, 0], grouped(wt)[:, 1], ALU.add))
            step(dve.tensor_tensor(tot[:], tot[:], grouped(wt)[:, 2], ALU.add))
            step(dve.reciprocal(tot[:], tot[:]))
            step(dve.reciprocal(den[:], den[:]))
            for g in range(NG):
                step(dve.tensor_tensor(grouped(wt)[:, g], grouped(wt)[:, g], tot[:], ALU.mult))
            step(dve.tensor_tensor(den[:, 0:NSWA], den[:, 0:NSWA], wt[:], ALU.mult))
            dve.wait_ge(gates_ready, 2)
            for tb in range(TB):
                step(dve.tensor_tensor(o[:, tb], o[:, tb], den[:, :, tb:tb + 1].to_broadcast([P, NH, P]), ALU.mult))
                for g in range(1, NG):
                    step(dve.tensor_tensor(o[:, tb, 0:PER], o[:, tb, 0:PER], o[:, tb, g * PER:(g + 1) * PER], ALU.add))
                step(dve.tensor_tensor(s_gate[:, tb], s_gate[:, tb], o[:, tb, 0:PER].rearrange("p h c -> p (h c)"), ALU.mult))
                step(dve.tensor_tensor(m_gate[:, tb], m_gate[:, tb], o[:, tb, NSWA:NH].rearrange("p h c -> p (h c)"), ALU.mult))

        @block.tensor
        def _(pe):
            def turn_qk(n):
                if n >= 2:
                    pe.wait_ge(qk_out, n - 1)
                for b in range(TB):
                    pe.transpose(ps[:, n % 2, b * P:(b + 1) * P], p2[:, b, q_at(n):q_at(n) + P], e.ident[:])
                for b in range(TB):
                    tr = pe.transpose(ps[:, n % 2, T + b * P:T + (b + 1) * P], key(n, b), e.ident[:])
                tr.then_inc(qk_done, 1)

            def scores(n):
                pe.wait_ge(qk_out, n + 1)
                if n >= 2:
                    pe.wait_ge(sc_ready, n - 1)
                for tb in range(TB):
                    mm = pe.matmul(ps[:, 2 + n % 2, tb * T:(tb + 1) * T], qk[:, n % 2, tb * P:(tb + 1) * P], qk[:, n % 2, T:2 * T], start=True, stop=True)
                mm.then_inc(s_done, 1)

            def weigh(n):
                pe.wait_ge(ex_out, n + 1)
                if n >= 2:
                    pe.wait_ge(o_out, n - 1)
                for tb in range(TB):
                    keys = range(tb + 1) if n < NSWA else range(TB)
                    for i, b in enumerate(keys):
                        mm = pe.matmul(ps[:, 6 + n % 2, tb * P:(tb + 1) * P], exT[:, n % 2, b, tb * P:(tb + 1) * P], value(n, b),
                                       start=(i == 0), stop=(i == len(keys) - 1))
                mm.then_inc(o_done, 1)

            turn_qk(0)
            turn_qk(1)
            scores(0)
            for n in range(NH):
                if n + 2 < NH:
                    turn_qk(n + 2)
                if n + 1 < NH:
                    scores(n + 1)
                pe.wait_ge(exp_ready, 2 * (n + 1))
                if n >= 2:
                    pe.wait_ge(ex_out, n - 1)
                for b in range(TB):
                    for tb in range(TB):
                        tr = pe.transpose(ps[:, 4 + n % 2, b * T + tb * P:b * T + (tb + 1) * P], ex[:, n % 2, tb, b * P:(b + 1) * P], e.ident[:])
                tr.then_inc(ex_turned, 1)
                if n >= 1:
                    weigh(n - 1)
            weigh(NH - 1)


def phase_gla(nc, e):
    ps, io, p2 = e.ps, e.io, e.p2
    with ExitStack() as ctx:
        sem = phase_semaphores(nc, ctx)
        sb = lambda name, shape: ctx.enter_context(nc.sbuf_tensor(name, shape, F32))
        H, DV, C = 4, 256, 64
        NC = T // C
        TAU = 16.0
        w_alpha = sb("w_alpha", [16, H * P])
        seg, clip = sb("chunk_starts", [P, H * T]), sb("chunk_clip", [P, 2, P])
        gain = sb("g_gla_row", [P, H * DV])
        z, u, w, ls = (sb(f"ls_gla_{n}", [P, H, T]) for n in "zuwl")
        grow, shrink, rest = u, w, z
        b = sb("gla_sums", [P, H, T])
        qt, kt, kd = sb("gla_q", [P, H, T]), sb("gla_k", [P, H, T]), sb("gla_k_rest", [P, H, T])
        aT = sb("gla_att", [P, 2, P])
        qpad = [p2[:, h // 2, A_VAL:A_GATE].rearrange("p (h c n) -> p h c n", c=NC, n=P)[:, h % 2] for h in range(H)]
        at = SQ + H * (NC - 1) * DV
        state = p2[:, 0, SQ:at].rearrange("p (h c e) -> p h c e", c=NC - 1, e=DV)
        kd_tok = p2[:, 0, at:at + TB * H * P].rearrange("p (b h n) -> p b h n", b=TB, n=P)
        o, sq = (p2[:, 1, SQ + i * TB * H * DV:SQ + (i + 1) * TB * H * DV].rearrange("p (n e) -> p n e", e=DV) for i in range(2))
        stat = sb("gla_stat", [P, TB * H])
        tables, z_done, b_ready, exps, pad_ready = sem("gla_tables"), sem("z_done"), sem("b_ready"), sem("gla_exps"), sem("pad_zero")
        rest_ready, qk_turned, qk_ready, pad_done = sem("rest_ready"), sem("gla_turned"), sem("gla_qk_ready"), sem("pad_done")
        kd_turned, kd_out, kv_done, state_ready = sem("kd_turned"), sem("kd_out"), sem("kv_done"), sem("state_ready")
        a_done, a_ready, o_done, o_out = sem("a_done"), sem("a_ready"), sem("gla_o_done"), sem("gla_o_out")
        sq_ready, var_ready, root_ready, gate_ready = sem("gla_sq"), sem("gla_var"), sem("gla_root"), sem("gla_gate")
        use = e.ls_uses + 1
        gate = p2[:, :, C_GATE:C_GATE + H * DV]
        chunks = lambda t: t[:].rearrange("p h (c n) -> p (h c) n", n=C)
        flat = lambda t: t[:].rearrange("p h t -> p (h t)")
        block = ctx.enter_context(nc.Block())

        @block.scalar
        def _(act):
            act.dma_start(w_alpha[:], io["w_alpha_2"][0]).then_inc(tables, 16)
            act.dma_start(seg[:], io["k_seg"]).then_inc(tables, 16)
            act.dma_start(clip[:], io["k_chunk"]).then_inc(tables, 16)
            act.dma_start(gain[:], io["g_gla_2"][0].partition_broadcast(P)).then_inc(tables, 16)
            log_sigmoid_on_scalar(act, e, use, u[:], w[:], ls[:])
            act.wait_ge(b_ready, 1)
            act.activation(shrink[:], b[:], ACT.Exp, scale=1.0 / TAU).then_inc(exps, 1)
            act.activation(grow[:], b[:], ACT.Exp, scale=-1.0 / TAU).then_inc(exps, 1)
            act.wait_ge(rest_ready, 1)
            act.activation(rest[:], rest[:], ACT.Exp, scale=1.0 / TAU).then_inc(exps, 1)
            for f in range(2):
                act.wait_ge(kd_turned, f + 1)
                act.activation(kd_tok[:, f].rearrange("p h d -> p (h d)"), ps[:, 4 + f], ACT.Copy).then_inc(kd_out, 1)
            for n in range(TB * H):
                act.wait_ge(o_done, n + 1)
                act.activation(o[:, n], ps[:, 6 + n % 2, 0:DV], ACT.Copy).then_inc(o_out, 1)
            act.wait_ge(o_out, TB * H)
            act.activation(sq, o, ACT.Square).then_inc(sq_ready, 1)
            act.wait_ge(var_ready, 1)
            act.activation(stat[:], stat[:], ACT.Sqrt).then_inc(root_ready, 1)
            act.activation(gate, gate, ACT.Silu).then_inc(gate_ready, 1)

        @block.gpsimd
        def _(pool):
            pool.memset(p2[:, :, A_VAL:A_GATE], 0.0).then_inc(pad_ready, 1)
            pool.wait_ge(pad_ready, 1)
            for h in range(H):
                pool.wait_ge(qk_ready, 3 * h + 1)
                for r in range(2):
                    pool.tensor_copy(qpad[h][:, r::2, r * C:(r + 1) * C], qt[:, h].rearrange("p (b r n) -> p r b n", r=2, n=C)[:, r]).then_inc(pad_done, 1)

        @block.vector
        def _(dve):
            step = e.dve_step
            dve.wait_ge(z_done, 1)
            for h in range(H):
                step(dve.tensor_scalar(z[:, h], ps[:, h // 2, (h % 2) * T:(h % 2 + 1) * T], e.cols_b[:, 88 + h:89 + h], None, ALU.add))
            log_sigmoid_on_vector(dve, step, e, z[:], u[:], w[:], ls[:])
            dve.wait_ge(tables, 64)
            dve.tensor_tensor_scan(flat(b), seg[:], flat(ls), 0.0, ALU.mult, ALU.add).then_inc(b_ready, 1)
            dve.wait_ge(b_ready, 1)
            last = chunks(b)[:, :, C - 1:C].to_broadcast([P, H * NC, C])
            dve.tensor_tensor(chunks(rest), last, chunks(b), ALU.subtract).then_inc(rest_ready, 1)
            dve.wait_ge(exps, 3)
            for h in range(H):
                dve.wait_ge(qk_turned, h + 1)
                q, k = ps[:, h, 0:T], ps[:, h, T:2 * T]
                dve.scalar_tensor_tensor(qt[:, h], q, float(P) ** -0.5, shrink[:, h], ALU.mult, ALU.mult).then_inc(qk_ready, 1)
                dve.tensor_tensor(kt[:, h], k, grow[:, h], ALU.mult).then_inc(qk_ready, 1)
                dve.tensor_tensor(kd[:, h], k, rest[:, h], ALU.mult).then_inc(qk_ready, 1)
            for h in range(H):
                for c in range(NC - 1):
                    n = h * (NC - 1) + c
                    dve.wait_ge(kv_done, n + 1)
                    kv, s = ps[:, 2 + n % 2, 0:DV], state[:, h, c]
                    if c == 0:
                        x = dve.tensor_copy(s, kv)
                    else:
                        at = c * C + C - 1
                        x = dve.scalar_tensor_tensor(s, state[:, h, c - 1], shrink[:, h, at:at + 1], kv, ALU.mult, ALU.add)
                    x.then_inc(state_ready, 1)
                    dve.wait_ge(state_ready, n + 1)
            for n in range(TB * H):
                dve.wait_ge(a_done, n + 1)
                if n >= 2:
                    dve.wait_ge(o_done, n - 1)
                step(dve.tensor_tensor(aT[:, n % 2], ps[:, 4 + n % 2, 0:P], clip[:, 0], ALU.min))
                dve.tensor_tensor(aT[:, n % 2], aT[:, n % 2], clip[:, 1], ALU.max).then_inc(a_ready, 1)
            dve.wait_ge(sq_ready, 1)
            step(dve.tensor_reduce(stat[:], sq, AX, ALU.add))
            dve.tensor_scalar(stat[:], stat[:], 1.0 / DV, EPS, ALU.mult, ALU.add).then_inc(var_ready, 1)
            dve.wait_ge(root_ready, 1)
            step(dve.reciprocal(stat[:], stat[:]))
            step(dve.tensor_tensor(o, o, stat[:].unsqueeze(2).to_broadcast([P, TB * H, DV]), ALU.mult))
            dve.wait_ge(gate_ready, 1)
            for tb in range(TB):
                flat_o = o[:, tb * H:(tb + 1) * H].rearrange("p h e -> p (h e)")
                step(dve.tensor_tensor(flat_o, flat_o, gain[:], ALU.mult))
                step(dve.tensor_tensor(gate[:, tb], gate[:, tb], flat_o, ALU.mult))

        @block.tensor
        def _(pe):
            pe.wait_ge(tables, 64)
            for h in range(H):
                mm = pe.matmul(ps[:, h // 2, (h % 2) * T:(h % 2 + 1) * T], w_alpha[:, h * P:(h + 1) * P], e.lrT[:], start=True, stop=True)
            mm.then_inc(z_done, 1)
            pe.wait_ge(b_ready, 1)
            for h in range(H):
                for a, first in enumerate((CQ, CK)):
                    for tb in range(TB):
                        at = first + h * P
                        tr = pe.transpose(ps[:, h, a * T + tb * P:a * T + (tb + 1) * P], p2[:, tb, at:at + P], e.ident[:])
                tr.then_inc(qk_turned, 1)
            pe.wait_ge(qk_ready, 3 * H)
            for tb in range(TB):
                for h in range(H):
                    tr = pe.transpose(ps[:, 4 + tb, h * P:(h + 1) * P], kd[:, h, tb * P:(tb + 1) * P], e.ident[:])
                tr.then_inc(kd_turned, 1)
            pe.wait_ge(kd_out, 2)
            for h in range(H):
                for c in range(NC - 1):
                    n = h * (NC - 1) + c
                    if n >= 2:
                        pe.wait_ge(state_ready, n - 1)
                    lo = (c % 2) * C
                    pe.matmul(ps[:, 2 + n % 2, 0:DV], kd_tok[lo:lo + C, c // 2, h], p2[lo:lo + C, c // 2, CV + h * DV:CV + (h + 1) * DV],
                              start=True, stop=True).then_inc(kv_done, 1)
            pe.wait_ge(state_ready, H * (NC - 1))
            pe.wait_ge(pad_done, 2 * H)

            def scores(n):
                h, tb = n % H, n // H
                if n >= 2:
                    pe.wait_ge(a_ready, n - 1)
                pe.matmul(ps[:, 4 + n % 2, 0:P], kt[:, h, tb * P:(tb + 1) * P], qt[:, h, tb * P:(tb + 1) * P], start=True, stop=True).then_inc(a_done, 1)

            scores(0)
            for n in range(TB * H):
                h, tb = n % H, n // H
                if n + 1 < TB * H:
                    scores(n + 1)
                pe.wait_ge(a_ready, n + 1)
                if n >= 2:
                    pe.wait_ge(o_out, n - 1)
                out = ps[:, 6 + n % 2, 0:DV]
                mm = pe.matmul(out, aT[:, n % 2], p2[:, tb, CV + h * DV:CV + (h + 1) * DV], start=True, stop=False)
                for c in (2 * tb, 2 * tb + 1):
                    if c:
                        mm = pe.matmul(out, qpad[h][:, c], state[:, h, c - 1], start=False, stop=(c % 2 == 1))
                mm.then_inc(o_done, 1)


def phase_second_merge(nc, e):
    ring, ps, io, p2 = e.ring, e.ps, e.io, e.p2
    with ExitStack() as ctx:
        sem = phase_semaphores(nc, ctx)
        sb = lambda name, shape: ctx.enter_context(nc.sbuf_tensor(name, shape, F32))
        split = WeightSplit(nc, ctx, sem, "merge2_weights")
        sig = sb("gate2", [P, 2, TB, CG])
        ss, rstd = sb("ss5", [P, TB]), sb("rstd5", [P, TB])
        turned, hi_out, lo_out, tb_done = sem("m2_turned"), sem("m2_hi_out"), sem("m2_lo_out"), sem("m2_tb_done")
        b_in = [sem(f"b_merge_in{j}") for j in range(2)]
        logit_ready, sig_ready, merged_out = sem("logit_ready"), sem("gate2_ready"), sem("merged2_out")
        post_in, o_ready, squares, var_ready, root_ready = sem("g_post_in"), sem("product_out"), sem("squares5"), sem("var5_ready"), sem("root5_ready")
        x_back, out_ready, stored = sem("x_back"), sem("out_ready"), sem("stored")
        base, N = ring.turn, D // CG
        w_in = io["w_in_2"][0]
        branches = ((io["w_br_pool_2"][0], 0, 8), (io["w_br_swa_2"][0], 8, 4), (io["w_br_gla_2"][0], 12, 8), (io["w_br_mem_2"][0], 20, 4))
        first_tile, tiles = [], 0
        for _, _, blocks in branches:
            first_tile.append(tiles)
            tiles += KB // TILE_K + blocks // TILE_K
        ROUND = 2 * tiles // SLOTS
        assert ROUND * SLOTS == 2 * tiles
        y_at = [A_GATE + k * P for k in range(8)] + [S_GATE + k * P for k in range(4)] + [C_GATE + k * P for k in range(8)] + [MEM_GATE + k * P for k in range(4)]
        YB = len(y_at)
        FILLS_Y, FILLS = YB // 2, (YB + KB) // 2
        merged, x_again = p2[:, :, 0:D], p2[:, :, 0:D]
        Y_HI, Y_LO, M_HI, M_LO = SQ, SQ + YB * P, SQ + YB * P, SQ + (YB + KB) * P
        BIAS, POST = Y_LO + YB * P, Y_LO + YB * P + N_BRANCH * CG
        o = p2[:, :, Y_HI:Y_HI + D]
        b_row = [p2[:, j, BIAS:POST].rearrange("p (b n) -> p b n", b=N_BRANCH) for j in range(2)]
        g_post = p2[:, :, POST:POST + D // 2]
        block_of = lambda at, k, tb: e.p2_split[:, tb, at + k * P:at + (k + 1) * P]
        y_split = lambda k, tb: (block_of(Y_HI, k, tb), block_of(Y_LO, k, tb))
        m_split = lambda k, tb: (block_of(M_HI, k, tb), block_of(M_LO, k, tb))
        two_blocks = lambda at, f: e.p2_split[:, :, at + 2 * f * P:at + (2 * f + 2) * P].rearrange("p b (a t) -> p a b t", a=2)
        fills = [(f, Y_HI, Y_LO) for f in range(FILLS_Y)] + [(f, M_HI, M_LO) for f in range(KB // 2)]
        AHEAD = N_BRANCH * TB + 1
        PER = 2 * N_BRANCH * TB

        def sources(n):
            out, cols = [], ds(n * CG, CG)
            for b, (w, _, blocks) in enumerate(branches):
                logits = w_in[:, G_LOGIT + b * D:G_LOGIT + (b + 1) * D]
                out += [k_tile(logits, s, cols) for s in range(KB // TILE_K)] + [k_tile(w, s, cols) for s in range(blocks // TILE_K)]
            return out

        block = ctx.enter_context(nc.Block())

        @block.sync
        def _(sp):
            load_tiles(sp, ring, sources(0) + sources(1), base, SLOTS)
            with sp.Fori(1, N // 2) as i:
                load_tiles(sp, ring, sources(i * 2) + sources(i * 2 + 1), i * ROUND + base)
            with sp.Fori(0, N) as n:
                load_tiles(sp, ring, turn_of(io["w_out_2"][0], ds(n * CG, CG)), n + (base + N // 2 * ROUND))
            sp.wait_ge(turned, FILLS)
            sp.dma_start(x_again, e.x_rows).then_inc(x_back, 16)
            for tb in range(TB):
                sp.wait_ge(out_ready, tb + 1)
                sp.dma_start(tokens_of(e.out[0])[:, tb], o[:, tb]).then_inc(stored, 16)
            sp.wait_ge(stored, 16 * TB)

        @block.gpsimd
        def _(pool):
            with pool.Fori(0, N // 2) as i:
                for m, piece in enumerate(pieces_of(0, 2 * tiles, i * ROUND + base)):
                    split.write_lo(pool, ring, piece, i * (2 * tiles) + m)
            with pool.Fori(0, N) as n:
                for s, piece in enumerate(pieces_of(0, SLOTS, n + (base + N // 2 * ROUND))):
                    split.write_lo(pool, ring, piece, n * SLOTS + (N * tiles + s))

        @block.tensor
        def _(pe):
            pe.sem_inc(split.free, split.free_after(0))

            def turn(fill, f, source):
                if fill >= 2:
                    pe.wait_ge(lo_out, fill - 1)
                for a in range(2):
                    for tb in range(TB):
                        at = (a * TB + tb) * P
                        tr = pe.transpose(ps[:, 6 + fill % 2, at:at + P], source(2 * f + a, tb), e.ident[:])
                tr.then_inc(turned, 1)

            for f in range(FILLS_Y):
                turn(f, f, lambda k, tb: p2[:, tb, y_at[k]:y_at[k] + P])
            pe.wait_ge(lo_out, FILLS_Y)
            with pe.Fori(0, N // 2) as i:
                t = i * ROUND + base
                for j in range(2):
                    for b, (_, first, blocks) in enumerate(branches):
                        at, half = j * tiles + first_tile[b], 4 * (b % 2)
                        n = j * N_BRANCH + b
                        free = i * PER + (2 * max(n - 1, 0) + 1)
                        gemm_split(pe, ring, split, pieces_of(at, KB // TILE_K, t), i * (2 * tiles) + at, e.h_split, [ps[:, half], ps[:, half + 1]],
                                   lambda tb: pe.wait_ge(merged_out, free) if tb == 0 else None, tb_done)
                        gemm_split(pe, ring, split, pieces_of(at + KB // TILE_K, blocks // TILE_K, t), i * (2 * tiles) + (at + KB // TILE_K), lambda k, tb: y_split(first + k, tb),
                                   [ps[:, half + 2], ps[:, half + 3]], lambda tb: None, tb_done)
            pe.wait_ge(merged_out, 2 * N * N_BRANCH + 1)
            for f in range(KB // 2):
                turn(FILLS_Y + f, f, lambda k, tb: merged[:, tb, k * P:(k + 1) * P])
            pe.wait_ge(lo_out, FILLS)
            with pe.Fori(0, N) as n:
                gemm_split(pe, ring, split, pieces_of(0, SLOTS, n + (base + N // 2 * ROUND)), n * SLOTS + N * tiles, m_split, [ps[:, 0], ps[:, 1]],
                           lambda tb: pe.wait_ge(o_ready, n * TB + (tb + 1)), tb_done)

        @block.scalar
        def _(act):
            def copy_hi(fill):
                f, hi, _ = fills[fill]
                act.wait_ge(turned, fill + 1)
                act.activation(two_blocks(hi, f), bank_blocks(e, 6 + fill % 2), ACT.Copy).then_inc(hi_out, 1)

            def sigmoid(i, n):
                for tb in range(TB):
                    act.wait_ge(logit_ready, i * PER + (n * TB + tb + 1 + AHEAD))
                    act.activation(sig[:, n % 2, tb], sig[:, n % 2, tb], ACT.Sigmoid).then_inc(sig_ready, 1)

            for fill in range(FILLS_Y):
                copy_hi(fill)
            act.dma_start(g_post, io["g_post_2"][0].rearrange("(a n) -> a n", a=2).partition_broadcast(P)).then_inc(post_in, 16)
            after = {}
            for n in range(2 * N_BRANCH):
                last = n // N_BRANCH * tiles + first_tile[n % N_BRANCH] + KB // TILE_K - 1
                after.setdefault(min(last + 2, 2 * tiles - 1), []).append(n)
            with act.Fori(0, N // 2) as i:
                pieces = pieces_of(0, 2 * tiles, i * ROUND + base)
                for m in range(2 * tiles):
                    for j in range(2):
                        if m == 6 * j:
                            act.wait_ge(logit_ready, i * PER + (AHEAD - (1 - j) * N_BRANCH * TB))
                            act.dma_start(b_row[j], io["b_merge_2"][0][:, ds((i * 2 + j) * CG, CG)].partition_broadcast(P)).then_inc(b_in[j], 16)
                    split.write_hi(act, ring, pieces[m], i * (2 * tiles) + m)
                    for n in after.get(m, []):
                        sigmoid(i, n)
            first = N // 2 * ROUND + base
            for s in range(2):
                split.write_hi(act, ring, (s, first), N * tiles + s)
            for f in range(KB // 2):
                copy_hi(FILLS_Y + f)
            for s in range(2, SLOTS):
                split.write_hi(act, ring, (s, first), N * tiles + s)
            with act.Fori(1, N) as n:
                for s, piece in enumerate(pieces_of(0, SLOTS, n + first)):
                    split.write_hi(act, ring, piece, n * SLOTS + (N * tiles + s))
            act.wait_ge(o_ready, TB * N + TB)
            rms_stats_on_scalar(act, ps[:, 2:6].rearrange("p b n -> p (b n)"), [o[:, 0], o[:, 1]], ss, rstd[:], squares, var_ready, root_ready)

        @block.vector
        def _(dve):
            step = e.dve_step

            def copy_lo(fill):
                f, hi, lo = fills[fill]
                dve.wait_ge(hi_out, fill + 1)
                dve.tensor_tensor(two_blocks(lo, f), bank_blocks(e, 6 + fill % 2), two_blocks(hi, f), ALU.subtract).then_inc(lo_out, 1)

            dve.sem_inc(logit_ready, AHEAD)
            dve.sem_inc(merged_out, 1)
            dve.sem_inc(o_ready, TB)
            for fill in range(FILLS_Y):
                copy_lo(fill)
            with dve.Fori(0, N // 2) as i:
                step.enter(i, 2 * (N_BRANCH - 1) * TB)
                for j in range(2):
                    dve.wait_ge(b_in[j], (i + 1) * 16)
                    for b, (_, _, blocks) in enumerate(branches):
                        n, half = j * N_BRANCH + b, 4 * (b % 2)
                        done = j * tiles + first_tile[b] + KB // TILE_K
                        for tb in range(TB):
                            if tb == 0:
                                dve.wait_ge(tb_done, i * (4 * N_BRANCH) + (2 * n + 1))
                            else:
                                dve.wait_ge(split.free, i * (4 * tiles) + split.free_after(done))
                            dve.tensor_tensor(sig[:, n % 2, tb], ps[:, half + tb], b_row[j][:, b], ALU.add).then_inc(logit_ready, 1)
                        for tb in range(TB):
                            dve.wait_ge(sig_ready, i * PER + (n * TB + tb + 1))
                            if tb == 0:
                                dve.wait_ge(tb_done, i * (4 * N_BRANCH) + (2 * n + 2))
                            else:
                                dve.wait_ge(split.free, i * (4 * tiles) + split.free_after(done + blocks // TILE_K))
                            out, y = merged[:, tb, ds((i * 2 + j) * CG, CG)], ps[:, half + 2 + tb]
                            if b == 0:
                                dve.tensor_tensor(out, sig[:, n % 2, tb], y, ALU.mult).then_inc(merged_out, 1)
                            else:
                                step(dve.tensor_tensor(sig[:, n % 2, tb], sig[:, n % 2, tb], y, ALU.mult))
                                dve.tensor_tensor(out, out, sig[:, n % 2, tb], ALU.add).then_inc(merged_out, 1)
                        dve.wait_ge(merged_out, i * PER + ((n + 1) * TB + 1))
            step.leave(N // 2)
            for f in range(KB // 2):
                copy_lo(FILLS_Y + f)
            with dve.Fori(0, N) as n:
                for tb in range(TB):
                    if tb == 0:
                        dve.wait_ge(tb_done, n + (4 * N_BRANCH * (N // 2) + 1))
                    else:
                        dve.wait_ge(split.free, n * (2 * SLOTS) + split.free_after(N * tiles + SLOTS))
                    dve.tensor_scalar(o[:, tb, ds(n * CG, CG)], ps[:, tb], 1.0, None, ALU.mult).then_inc(o_ready, 1)
            rms_stats_on_vector(dve, step, TB, ss[:], rstd[:], squares, var_ready, root_ready)
            dve.wait_ge(post_in, 16)
            dve.wait_ge(x_back, 16)
            for tb in range(TB):
                halves = o[:, tb].rearrange("p (a n) -> p a n", a=2)
                step(dve.scalar_tensor_tensor(halves, halves, rstd[:, tb:tb + 1], g_post, ALU.mult, ALU.mult))
                dve.tensor_tensor(o[:, tb], o[:, tb], x_again[:, tb], ALU.add).then_inc(out_ready, 1)
    ring.turn += N // 2 * ROUND + N


class Shared:
    pass


def next_place(nc):
    return -(-nc.sbuf_base // 32) * 32


def build(nc, io, out):
    with ExitStack() as ctx:
        sb = lambda name, shape, dt=F32: ctx.enter_context(nc.sbuf_tensor(name, shape, dt))
        rounded = lambda name, shape, at: nc.alloc_sbuf_tensor_at(name, shape, F32R, offset=at)
        sem = lambda name: ctx.enter_context(nc.semaphore(name))
        e = Shared()
        e.io, e.out = io, out
        e.ps = ctx.enter_context(nc.psum_tensor("banks", [P, 8, CG], F32))
        e.ring = WeightRing(nc, ctx)
        e.ident = sb("identity", [P, P])
        e.cols_a, e.cols_b = sb("cols_a", [P, P]), sb("cols_b", [P, 92])
        e.cT, e.ada = sb("cond_T", [P, KB, 2]), sb("modulation_cols", [P, 2 * KB, 2])
        x_at = next_place(nc)
        e.x = sb("x_tokens", [P, TB, D])
        hT_at = next_place(nc)
        e.hT = sb("h_T", [P, KB, T])
        e.gates, e.gate_bias = sb("gates", [P, 2 * TB, N_GATES]), sb("gate_bias", [P, N_GATES])
        e.hT_hi, e.hT_lo = rounded("h_T_hi", [P, KB, T], hT_at), rounded("h_T_lo", [P, KB, T], x_at)
        e.h_split = lambda k, tb: tuple(h[:, k, tb * P:(tb + 1) * P] for h in (e.hT_hi, e.hT_lo))
        e.dve_step = Steps(nc.vector, sem("dve_steps"))
        e.pool_step = Steps(nc.gpsimd, sem("pool_steps"))
        e.mod_rows = nc.dram_tensor("mod_rows", (1, 4 * D), F32, kind="Internal").ap()
        e.x_rows = nc.dram_tensor("x_rows", (P, TB, D), F32, kind="Internal").ap()
        e.gate_bias_in, e.gates_ready = sem("gate_bias_in"), sem("gates_ready")
        e.ls_uses = e.hn_uses = 0
        e.ls_neg_abs, e.ls_exp, e.ls_one_plus, e.ls_ln = sem("ls_neg_abs"), sem("ls_exp"), sem("ls_one_plus"), sem("ls_ln")
        e.hn_centred, e.hn_squared, e.hn_var, e.hn_root = sem("hn_centred"), sem("hn_squared"), sem("hn_var"), sem("hn_root")
        with ExitStack() as block1:
            sb1 = lambda name, shape: block1.enter_context(nc.sbuf_tensor(name, shape, F32))
            lat_at = next_place(nc)
            e.lat = sb1("lat_cols", [P, TB, MG])
            cxt_at = next_place(nc)
            e.cxt = sb1("ctx_cols", [P, TB, 3072])
            e.lat_split, e.cxt_split = rounded("lat_split", [P, TB, MG], lat_at), rounded("cxt_split", [P, 24, T], cxt_at)
            with ExitStack() as proj:
                e.chT_hi = proj.enter_context(nc.sbuf_tensor("ctx_h_T_hi", [P, KB, T], F32R))
                late = [(tb, at + j * T) for at, width in ((4 * CG, 3 * CG), (10 * CG, CG)) for tb in range(TB) for j in range(width // T)]
                e.chT_lo = [e.lat_split[:, tb, at:at + T] for tb, at in late]
                phase_modulation(nc, e)
                phase_projection(nc, e)
            phase_retention(nc, e)
            phase_mlstm(nc, e)
            phase_merge(nc, e)
        e.kv = sb("mem_kv", [P, TB, 2 * MEM_W])
        with ExitStack() as peer:
            sbp = lambda name, shape, dt=F32: peer.enter_context(nc.sbuf_tensor(name, shape, dt))
            e.h2 = sbp("h2_tokens", [P, TB, D])
            e.expert = sbp("picked_experts", [P, 2 * TB * PICKS + 8], U32)
            e.weight = sbp("picked_weights", [P, TB * PICKS])
            phase_routing(nc, e)
            phase_experts(nc, e)
        with ExitStack() as block2:
            sb2 = lambda name, shape: block2.enter_context(nc.sbuf_tensor(name, shape, F32))
            p2_at = next_place(nc)
            e.p2, e.lrT = sb2("p2_cols", [P, TB, P2_COLS]), sb2("lr_T", [16, T])
            e.p2_split = rounded("p2_split", [P, TB, P2_COLS], p2_at)
            phase_second_projection(nc, e)
            phase_pool(nc, e)
            phase_attention(nc, e)
            phase_gla(nc, e)
            phase_second_merge(nc, e)


INPUTS = ["x", "c", "ctx", "c_ctx", "w_ada", "b_ada", "norm1_g", "w_in", "ret_decay", "m_conv", "m_gate_bias", "w_ret_out",
          "w_mlstm_out", "w_out", "norm2_g", "peer_query", "peer_keys", "peer_down", "peer_up", "final_g", "mem_2",
          "g_pre_2", "g_post_2", "g_mem_2", "w_in_2", "b_merge_2", "w_pool_2", "pool_scale_2", "w_alpha_2", "b_alpha_2",
          "g_gla_2", "w_mem_kv_2", "w_br_pool_2", "w_br_swa_2", "w_br_gla_2", "w_br_mem_2", "w_out_2"]


def kernel(**inputs):
    import concourse.bacc as bacc
    from concourse.bass_utils import run_bass_kernel_spmd

    nc = bacc.Bacc("TRN2", target_bir_lowering=False, num_devices=1)
    arrays = {name: np.ascontiguousarray(inputs[name]) for name in INPUTS}
    arrays.update(shape_constants())
    io = {
        name: nc.dram_tensor(name, a.shape, mybir.dt.from_np(a.dtype), kind="ExternalInput").ap() for name, a in arrays.items()}
    out = nc.dram_tensor("y_out", (1, T, D), F32, kind="ExternalOutput").ap()
    build(nc, io, out)
    r = run_bass_kernel_spmd(nc, [arrays], core_ids=[0])
    return r.results[0]["y_out"]
```
